# Optimizing a Trainium2 kernel written in Bass

```python
import jax, jax.numpy as jnp
from jax import lax
import numpy as np

D_MODEL = 2048
BATCH = 1
SEQ = 256
DEPTH = 1

N_HEADS_MLA = 8
Q_LORA = 512
KV_LORA = 256
MLA_NOPE = 128
MLA_ROPE = 64
MLA_V = 128
MLA_QK = MLA_NOPE + MLA_ROPE
DIL_GROUPS = ((128, 1), (512, 4), (2048, 16))
N_DIL_GROUPS = len(DIL_GROUPS)
N_HEADS_DIL = 8
DIL_HEAD = 128
DIL_ROT = DIL_HEAD // 4
ROPE_THETA = 500000.0
D_FF = 5632
PLE_DIM = 256
EPS = 1e-6
Q_BLOCK = 128
NEG = -1e30

OFF_CQ = 0
OFF_CKV = OFF_CQ + Q_LORA
OFF_KR = OFF_CKV + KV_LORA
OFF_DIL = OFF_KR + MLA_ROPE
DIL_QKV = N_DIL_GROUPS * 3 * N_HEADS_DIL * DIL_HEAD
OFF_GATE = OFF_DIL + DIL_QKV
N_BRANCH = 2
D_IN = OFF_GATE + N_BRANCH * D_MODEL

kernel_name = "hybrid_mla_dilated_gated_macaron"

def rmsnorm(x, g):
    xf = x.astype(jnp.float32)
    y = xf * lax.rsqrt(jnp.mean(xf * xf, axis=-1, keepdims=True) + EPS)
    return (y * g.astype(jnp.float32)).astype(x.dtype)

def rope(x, pos):
    rd = x.shape[-1]
    half = rd // 2
    inv = ROPE_THETA ** (-jnp.arange(half, dtype=jnp.float32) * 2.0 / rd)
    ang = pos.astype(jnp.float32)[..., None] * inv
    cos = jnp.cos(ang)[:, :, None, :]
    sin = jnp.sin(ang)[:, :, None, :]
    xf = x.astype(jnp.float32)
    x1, x2 = xf[..., :half], xf[..., half:]
    return jnp.concatenate([x1 * cos - x2 * sin, x2 * cos + x1 * sin], axis=-1).astype(x.dtype)

def swiglu(h, wg, wu, wd):
    return (jax.nn.silu(h @ wg) * (h @ wu)) @ wd

def causal_block_attention(q, k, v):
    B, S, H, Dq = q.shape
    nq = S // Q_BLOCK
    qb = q.reshape(B, nq, Q_BLOCK, H, Dq).transpose(1, 0, 2, 3, 4)
    starts = jnp.arange(nq, dtype=jnp.int32) * Q_BLOCK
    kpos = jnp.arange(S, dtype=jnp.int32)

    def one_block(args):
        qi, s0 = args
        sc = jnp.einsum('bqhd,bkhd->bhqk', qi, k).astype(jnp.float32)
        qpos = s0 + jnp.arange(Q_BLOCK, dtype=jnp.int32)
        mask = kpos[None, :] <= qpos[:, None]
        pr = jax.nn.softmax(jnp.where(mask[None, None], sc, NEG), axis=-1)
        return jnp.einsum('bhqk,bkhd->bqhd', pr.astype(v.dtype), v)

    out = lax.map(one_block, (qb, starts))
    return out.transpose(1, 0, 2, 3, 4).reshape(B, S, H, v.shape[-1])

def dilated_window_attention(q, k, v, dil, n):
    B, S, H, Dh = q.shape
    L = S // dil
    Lp = -(-L // n) * n
    nb = Lp // n

    def phase_major(t):
        t = t.reshape(B, L, dil, H, Dh).transpose(0, 2, 1, 3, 4)
        return jnp.pad(t, ((0, 0), (0, 0), (0, Lp - L), (0, 0), (0, 0)))

    def windows(t):
        t = jnp.pad(phase_major(t), ((0, 0), (0, 0), (n, 0), (0, 0), (0, 0)))
        t = t.reshape(B, dil, nb + 1, n, H, Dh)
        return jnp.concatenate([t[:, :, :-1], t[:, :, 1:]], axis=3)

    qb = phase_major(q).reshape(B, dil, nb, n, H, Dh)
    kw = windows(k)
    vw = windows(v)
    sc = jnp.einsum('brnqhc,brnkhc->brnhqk', qb, kw).astype(jnp.float32)
    i = jnp.arange(n)[:, None]
    j = jnp.arange(2 * n)[None, :]
    dist = i + n - j
    band = (dist >= 0) & (dist <= n)
    keyok = ((jnp.arange(nb)[:, None] - 1) * n + jnp.arange(2 * n)[None, :]) >= 0
    valid = (band[None] & keyok[:, None, :])[None, None, :, None]
    m = jnp.max(jnp.where(valid, sc, NEG), axis=-1)
    e = jnp.where(valid, jnp.exp(sc - m[..., None]), 0.0)
    l = jnp.sum(e, axis=-1)
    o = jnp.einsum('brnhqk,brnkhc->brnqhc', (e / l[..., None]).astype(v.dtype), vw)
    o = o.reshape(B, dil, Lp, H, Dh)[:, :, :L].transpose(0, 2, 1, 3, 4).reshape(B, S, H, Dh)

    def back(s):
        s = s.transpose(0, 1, 2, 4, 3).reshape(B, dil, Lp, H)[:, :, :L]
        return s.transpose(0, 2, 1, 3).reshape(B, S, H)

    return o, back(m), back(l)

def setup_inputs(seed: int = 0) -> dict:
    key = jax.random.key(seed)
    ks = jax.random.split(key, 32)
    f32 = jnp.float32

    def nrm(k, shape, fan):
        return jax.random.normal(k, shape, f32) * fan ** -0.5

    def gain(k, shape):
        return 1.0 + 0.1 * jax.random.normal(k, shape, f32)

    Dp = DEPTH
    return {
        "x": jax.random.normal(ks[0], (BATCH, SEQ, D_MODEL), f32),
        "p": jax.random.normal(ks[1], (DEPTH, BATCH, SEQ, PLE_DIM), f32),
        "positions": jnp.arange(SEQ, dtype=jnp.int32)[None, :]
        + jax.random.randint(ks[2], (BATCH, 1), 0, 4096, dtype=jnp.int32),
        "g_ffn1": gain(ks[3], (Dp, D_MODEL)),
        "w1_gate": nrm(ks[4], (Dp, D_MODEL, D_FF), D_MODEL),
        "w1_up": nrm(ks[5], (Dp, D_MODEL, D_FF), D_MODEL),
        "w1_down": nrm(ks[6], (Dp, D_FF, D_MODEL), D_FF),
        "g_mix": gain(ks[7], (Dp, D_MODEL)),
        "w_in": nrm(ks[8], (Dp, D_MODEL, D_IN), D_MODEL),
        "g_cq": gain(ks[9], (Dp, Q_LORA)),
        "w_uq": nrm(ks[10], (Dp, Q_LORA, N_HEADS_MLA * MLA_QK), Q_LORA),
        "g_ckv": gain(ks[11], (Dp, KV_LORA)),
        "w_ukv": nrm(ks[12], (Dp, KV_LORA, N_HEADS_MLA * (MLA_NOPE + MLA_V)), KV_LORA),
        "g_q_mla": gain(ks[13], (Dp, MLA_QK)),
        "g_k_mla": gain(ks[14], (Dp, MLA_QK)),
        "g_q_dil": gain(ks[15], (Dp, N_DIL_GROUPS, DIL_HEAD)),
        "g_k_dil": gain(ks[16], (Dp, N_DIL_GROUPS, DIL_HEAD)),
        "w_br_mla": nrm(ks[17], (Dp, N_HEADS_MLA * MLA_V, D_MODEL), N_HEADS_MLA * MLA_V),
        "w_br_dil": nrm(ks[18], (Dp, N_HEADS_DIL * DIL_HEAD, D_MODEL), N_HEADS_DIL * DIL_HEAD),
        "w_o": nrm(ks[19], (Dp, D_MODEL, D_MODEL), D_MODEL),
        "g_ffn2": gain(ks[20], (Dp, D_MODEL)),
        "w2_gate": nrm(ks[21], (Dp, D_MODEL, D_FF), D_MODEL),
        "w2_up": nrm(ks[22], (Dp, D_MODEL, D_FF), D_MODEL),
        "w2_down": nrm(ks[23], (Dp, D_FF, D_MODEL), D_FF),
        "g_ple": gain(ks[24], (Dp, D_MODEL)),
        "w_ple_gate": nrm(ks[25], (Dp, D_MODEL, D_MODEL), D_MODEL),
        "w_ple_proj": nrm(ks[26], (Dp, PLE_DIM, D_MODEL), PLE_DIM),
    }

def reference(x, p, positions, g_ffn1, w1_gate, w1_up, w1_down, g_mix, w_in, g_cq, w_uq,
              g_ckv, w_ukv, g_q_mla, g_k_mla, g_q_dil, g_k_dil, w_br_mla, w_br_dil, w_o,
              g_ffn2, w2_gate, w2_up, w2_down, g_ple, w_ple_gate, w_ple_proj):
    B, S, _ = x.shape
    scale_mla = MLA_QK ** -0.5
    scale_dil = DIL_HEAD ** -0.5
    for i in range(DEPTH):
        x = x + 0.5 * swiglu(rmsnorm(x, g_ffn1[i]), w1_gate[i], w1_up[i], w1_down[i])

        h = rmsnorm(x, g_mix[i])
        proj = h @ w_in[i]

        cq = rmsnorm(proj[..., OFF_CQ:OFF_CKV], g_cq[i])
        q = (cq @ w_uq[i]).reshape(B, S, N_HEADS_MLA, MLA_QK)
        ckv = rmsnorm(proj[..., OFF_CKV:OFF_KR], g_ckv[i])
        kv = (ckv @ w_ukv[i]).reshape(B, S, N_HEADS_MLA, MLA_NOPE + MLA_V)
        k_nope, v = kv[..., :MLA_NOPE], kv[..., MLA_NOPE:]
        k_rope = jnp.broadcast_to(proj[:, :, None, OFF_KR:OFF_DIL], (B, S, N_HEADS_MLA, MLA_ROPE))
        k = jnp.concatenate([k_nope, k_rope], axis=-1)
        q = rmsnorm(q, g_q_mla[i])
        k = rmsnorm(k, g_k_mla[i])
        q = jnp.concatenate([q[..., :MLA_NOPE], rope(q[..., MLA_NOPE:], positions)], axis=-1) * scale_mla
        k = jnp.concatenate([k[..., :MLA_NOPE], rope(k[..., MLA_NOPE:], positions)], axis=-1)
        o_mla = causal_block_attention(q, k, v).reshape(B, S, N_HEADS_MLA * MLA_V)

        dqkv = proj[..., OFF_DIL:OFF_GATE].reshape(B, S, N_DIL_GROUPS, 3, N_HEADS_DIL, DIL_HEAD)
        outs, ms, ls = [], [], []
        for g, (win, dil) in enumerate(DIL_GROUPS):
            qg = rmsnorm(dqkv[:, :, g, 0], g_q_dil[i, g])
            kg = rmsnorm(dqkv[:, :, g, 1], g_k_dil[i, g])
            vg = dqkv[:, :, g, 2]
            qg = jnp.concatenate([rope(qg[..., :DIL_ROT], positions), qg[..., DIL_ROT:]], axis=-1) * scale_dil
            kg = jnp.concatenate([rope(kg[..., :DIL_ROT], positions), kg[..., DIL_ROT:]], axis=-1)
            o, m, l = dilated_window_attention(qg, kg, vg, dil, win // dil)
            outs.append(o)
            ms.append(m)
            ls.append(l)
        m_all = jnp.stack(ms, axis=0)
        l_all = jnp.stack(ls, axis=0)
        wgt = l_all * jnp.exp(m_all - jnp.max(m_all, axis=0, keepdims=True))
        wgt = wgt / jnp.sum(wgt, axis=0, keepdims=True)
        o_dil = jnp.einsum('gbsh,gbshc->bshc', wgt.astype(x.dtype), jnp.stack(outs, axis=0))
        o_dil = o_dil.reshape(B, S, N_HEADS_DIL * DIL_HEAD)

        gates = jax.nn.sigmoid(proj[..., OFF_GATE:].reshape(B, S, N_BRANCH, D_MODEL))
        merged = gates[:, :, 0] * (o_mla @ w_br_mla[i]) + gates[:, :, 1] * (o_dil @ w_br_dil[i])
        x = x + merged @ w_o[i]

        x = x + 0.5 * swiglu(rmsnorm(x, g_ffn2[i]), w2_gate[i], w2_up[i], w2_down[i])

        ple_gate = jax.nn.sigmoid(rmsnorm(x, g_ple[i]) @ w_ple_gate[i])
        x = x + ple_gate * (p[i] @ w_ple_proj[i])
    return x


_drawn_inputs = setup_inputs


def setup_inputs(seed=0):
    import zlib

    import numpy as np

    out = dict(_drawn_inputs(seed))
    spreads = {}
    factors = {'g_cq': 6.361,
     'g_ckv': 4.235,
     'g_q_mla': 6.081,
     'g_k_mla': 6.695,
     'g_q_dil': 6.84,
     'g_k_dil': 7.211,
     'g_ple': 37.093,
     'g_ffn2': 3.411}
    for name, (base, spread) in spreads.items():
        noise = np.random.default_rng([zlib.crc32(name.encode()), seed]).standard_normal(out[name].shape)
        drawn = base * np.exp(spread * noise) if base else spread * noise
        out[name] = __import__('jax').numpy.asarray(drawn.astype(out[name].dtype))
    for name, factor in factors.items():
        out[name] = (out[name] * factor).astype(out[name].dtype)
    return out
```

```python
from contextlib import ExitStack

import concourse.bass as bass
from concourse import mybir

ALU = mybir.AluOpType
ACT = mybir.ActivationFunctionType
AX_X = mybir.AxisListType.X
F32 = mybir.dt.float32
F32R = mybir.dt.float32r
BF16 = mybir.dt.bfloat16
I32 = mybir.dt.int32
ds = bass.ds

P = 128
BANK = 512
SLOTS = 4
UNIT = 1024
EPS = 1e-6
PRIMED = 1
ROUND = 1.5 * 2.0 ** 23
TWO_PI_1 = 6.28125
TWO_PI_2 = 0.0019340515136718750
TWO_PI_3 = 6.283185307179586 - TWO_PI_1 - TWO_PI_2
PI_DOWN = 3.1415925


class Chain:

    def __init__(self, eng, sem):
        self.eng, self.sem, self.n, self.past = eng, sem, 0, 0

    def __call__(self, ins):
        ins.then_inc(self.sem, 1)
        self.n += 1
        self.eng.wait_ge(self.sem, self.past + self.n)

    def enter(self, i, steps):
        self.past, self.first, self.steps = i * steps, self.n, steps

    def leave(self, turns):
        assert self.n - self.first == self.steps, (self.n - self.first, self.steps)
        self.past, self.n = 0, self.n + self.steps * (turns - 1)


def hybrid_layer(nc, out, x, p, positions, g_ffn1, w1_gate, w1_up, w1_down, g_mix, w_in, g_cq, w_uq,
                 g_ckv, w_ukv, g_q_mla, g_k_mla, g_q_dil, g_k_dil, w_br_mla, w_br_dil, w_o, g_ffn2,
                 w2_gate, w2_up, w2_down, g_ple, w_ple_gate, w_ple_proj, identity, mla_masks,
                 dil_masks, inverse_frequencies):
    _, S, D = x.shape
    FF = w1_gate.shape[2]
    PLE = p.shape[3]
    LQ, LKV = g_cq.shape[1], g_ckv.shape[1]
    QK = g_q_mla.shape[1]
    GROUPS, HD = g_q_dil.shape[1:]
    NOPE = HD
    ROPE = QK - NOPE
    H = w_br_dil.shape[1] // HD
    ROT = HD // 4
    LAT = LQ + LKV + ROPE
    OFF_GATE = LAT + GROUPS * 3 * H * HD
    NF = inverse_frequencies.shape[1]
    T, KD, KF = S // P, D // P, FF // P
    HQ, HK = H * QK // 2, H * (NOPE + HD) // 2
    assert T == 2 and D == 2 * UNIT and H * HD == UNIT and NF == ROPE // 2 + ROT // 2
    SCALE_MLA, SCALE_DIL = QK ** -0.5, HD ** -0.5
    NG = LQ // P + LKV // P

    FFN_TURNS, FFN_BODY = FF // BANK, 2 * KD // 2
    MERGE_TURNS, MERGE_BODY = D // BANK, 2 * (KD // 2 + H // 2)
    counts = [FFN_TURNS * FFN_BODY, 2 * KF, KD, KD, 2 * (LQ // P), 2 * (LKV // P),
              KD, 2 * GROUPS * KD, KD, MERGE_TURNS * MERGE_BODY, 2 * KD,
              FFN_TURNS * FFN_BODY, 2 * KF, 2 * (KD + PLE // P)]
    starts = [sum(counts[:n]) for n in range(len(counts))]
    (U_GU1, U_DOWN1, U_LAT, U_V0, U_UQ, U_UKV, U_V1, U_QK, U_V2, U_MERGE, U_WO, U_GU2, U_DOWN2, U_PLE) = starts
    UNITS = sum(counts)
    assert all(n % SLOTS == 0 for n in counts)

    with ExitStack() as ctx:
        def sem(name):
            return ctx.enter_context(nc.semaphore(name))

        def sb(name, shape, dt=F32):
            return ctx.enter_context(nc.sbuf_tensor(name, shape, dt))

        ps = ctx.enter_context(nc.psum_tensor("ps", [P, 8, BANK], F32))
        flat = ps[:, :, :].rearrange("p b c -> p (b c)")

        def banks(b, width):
            return flat[:, b * BANK:b * BANK + width]

        res = sb("res", [P, T, D])
        hTh = sb("hTh", [P, KD, S], F32R)
        hTl = sb("hTl", [P, KD, S], F32R)
        raw = sb("raw", [P, SLOTS, UNIT])
        wh = sb("wh", [P, SLOTS, UNIT], F32R)
        wl = sb("wl", [P, SLOTS, UNIT], F32R)
        ident = sb("ident", [P, P])
        ones, diag = sb("ones", [P, P]), sb("diag", [P, P])
        inv_row = sb("inv_row", [P, S])
        gcol = sb("gcol", [P, 4 * KD + NG])
        gq_mla, gk_mla = sb("gq_mla", [P, QK]), sb("gk_mla", [P, QK])
        gq_dil, gk_dil = sb("gq_dil", [P, GROUPS, HD]), sb("gk_dil", [P, GROUPS, HD])
        m_mla = sb("m_mla", [P, 2 * P], BF16)
        m_dil = sb("m_dil", [P, GROUPS, 2 * P], BF16)
        sin, cos = sb("sin", [P, T, NF]), sb("cos", [P, T, NF])
        small = sb("small", [P, 256])

        base = nc.sbuf_base
        room = nc.sbuf_top - base

        def at(name, where, shape, dt=F32):
            size = 4
            for n in shape[1:]:
                size *= n
            assert where + size <= room, (name, where, size, room)
            return nc.alloc_sbuf_tensor_at(name, shape, dt, offset=base + where)

        KB = 1024
        aTh, aTl = at("aTh", 0, [P, KF, S], F32R), at("aTl", 44 * KB, [P, KF, S], F32R)
        sg, gs = at("sg", 88 * KB, [P, 4, S]), at("gs", 92 * KB, [P, 4, S])
        junk = at("junk", 88 * KB, [P, UNIT])
        grow = at("grow", 16 * KB, [4 * KD + NG, P])
        angle, turns, freq = (at(n, 96 * KB + 256 * j, [P, NF]) for j, n in enumerate(("angle", "turns", "freq")))
        pos_i, pos_f = at("pos_i", 96 * KB + 768, [P, T], I32), at("pos_f", 96 * KB + 800, [P, T])
        q_tok, kv_tok = at("q_tok", 0, [P, T, H * QK]), at("kv_tok", 16 * KB, [P, T, H * (NOPE + HD)])
        cTh, cTl = at("cTh", 32 * KB, [P, NG, S], F32R), at("cTl", 38 * KB, [P, NG, S], F32R)
        nT = at("nT", 32 * KB, [P, H, 2, S])
        rh = at("rh", 48 * KB, [P, T, 2, H, ROPE])
        rT = at("rT", 56 * KB, [P, 2, H // 2, S])
        sq = at("sq", 56 * KB, [P, H * QK])
        tmpA, tmpB = at("tmpA", 56 * KB, [P, 2 * H, ROPE // 2]), at("tmpB", 58 * KB, [P, 2 * H, ROPE // 2])
        c_tok = at("c_tok", 88 * KB, [P, T, LAT])
        prob_m, pT_m = at("prob_m", 88 * KB, [P, 3, 2 * P]), at("pT_m", 91 * KB, [P, 2 * P])
        omh, oml = at("omh", 0, [P, H, S], F32R), at("oml", 8 * KB, [P, H, S], F32R)
        qT, kT = at("qT", 16 * KB, [P, GROUPS, H * S]), at("kT", 40 * KB, [P, GROUPS, H * S])
        vd = at("vd", 64 * KB, [P, GROUPS, T * UNIT])
        tok = at("tok", 88 * KB, [P, T, UNIT])
        ropeA, ropeB = (at(n, 96 * KB + 512 * j, [P, H, ROT // 2]) for j, n in enumerate(("ropeA", "ropeB")))
        prob_d, pT_d = at("prob_d", 88 * KB, [P, 3, 6 * P]), at("pT_d", 97 * KB, [P, 6 * P])
        odh, odl = at("odh", 16 * KB, [P, H, S], F32R), at("odl", 40 * KB, [P, H, S], F32R)
        mTh, mTl = at("mTh", 48 * KB, [P, KD, S], F32R), at("mTl", 64 * KB, [P, KD, S], F32R)
        am = at("am", 80 * KB, [P, 4, S])
        sgp = at("sgp", 0, [P, T, UNIT])
        p_tok = at("p_tok", 16 * KB, [P, T, PLE])
        pTh, pTl = at("pTh", 18 * KB, [P, PLE // P, S], F32R), at("pTl", 20 * KB, [P, PLE // P, S], F32R)

        raw_in = [sem(f"raw_in{j}") for j in range(SLOTS)]
        hi_ready, lo_ready = sem("hi_ready"), sem("lo_ready")
        unit_done = sem("unit_done")
        x_in = [sem("x_in0"), sem("x_in1")]
        ident_in, rows_in, consts_in, gains_in, p_in = (
            sem(n) for n in ("ident_in", "rows_in", "consts_in", "gains_in", "p_in"))
        ones_ready, gains_turned, gcol_ready, angles_ready, tables_ready = (
            sem(n) for n in ("ones_ready", "gains_turned", "gcol_ready", "angles_ready", "tables_ready"))
        ss_ready, var_ready, dev_ready, inv_ready = (sem(n) for n in ("ss_ready", "var_ready", "dev_ready", "inv_ready"))
        diag_ready, row_turned, row_ready = (sem(n) for n in ("diag_ready", "row_turned", "row_ready"))
        turned, tr_hi, tr_lo = sem("turned"), sem("tr_hi"), sem("tr_lo")
        gi_ready, sig_ready, gs_ready, am_ready, ah_ready, a_ready = (
            sem(n) for n in ("gi_ready", "sig_ready", "gs_ready", "am_ready", "ah_ready", "a_ready"))
        res_ready = sem("res_ready")
        lat_tok, lat_ss, lat_var, lat_dev, lat_ready = (
            sem(n) for n in ("lat_tok", "lat_ss", "lat_var", "lat_dev", "lat_ready"))
        uq_tok, ukv_tok = sem("uq_tok"), sem("ukv_tok")
        mla_sq, mla_ss, mla_var, mla_dev, mla_inv, mla_scaled, mla_ready, mla_turned, rT_ready, nT_even, nT_odd = (
            sem(n) for n in ("mla_sq", "mla_ss", "mla_var", "mla_dev", "mla_inv", "mla_scaled", "mla_ready",
                             "mla_turned", "rT_ready", "nT_even", "nT_odd"))
        dil_tok, dil_sq, dil_ss, dil_var, dil_dev, dil_ready, dil_turned, dil_T, dil_v = (
            sem(n) for n in ("dil_tok", "dil_sq", "dil_ss", "dil_var", "dil_dev", "dil_ready", "dil_turned",
                             "dil_T", "dil_v"))
        score_done, masked, exp_done, prob_ready, prob_turned, pT_ready, pv_done, o_hi, o_lo = (
            sem(n) for n in ("score_done", "masked", "exp_done", "prob_ready", "prob_turned", "pT_ready",
                             "pv_done", "o_hi", "o_lo"))
        mgi_ready, msig_ready, mprod_ready, m_sum, mh_ready, m_ready = (
            sem(n) for n in ("mgi_ready", "msig_ready", "mprod_ready", "m_sum", "mh_ready", "m_ready"))
        p_turned, p_hi, p_lo, psig_ready, psig_used, out_done = (
            sem(n) for n in ("p_turned", "p_hi", "p_lo", "psig_ready", "psig_used", "out_done"))
        dve_step = sem("dve_step")

        ssq = small[:, 0:4]
        var, dev, inv, nwt = (small[:, 4 + 2 * j:6 + 2 * j] for j in range(4))
        css, cvar, cdev, cinv, cnwt = (small[:, 12 + 4 * j:16 + 4 * j] for j in range(5))
        mss, mvar, mdev, minv, mnwt = (small[:, 32 + 32 * j:64 + 32 * j] for j in range(5))
        dss, dvar, ddev, dinv, dnwt = (small[:, 32 + 32 * j:48 + 32 * j] for j in range(5))
        s_max, s_bias, s_sum, s_inv = (small[:, 192 + 16 * j:208 + 16 * j] for j in range(4))
        kss_m = small[:, 10:12]

        items = [(h, t) for h in range(H) for t in range(T)]

        PAIRS = [r * KD // 2 + (NG // 2 if r >= 2 else 0) for r in range(4)]
        C_PAIRS = PAIRS[1] + KD // 2

        block = ctx.enter_context(nc.Block())

        @block.sync
        def _(sp):
            def wide(n, j, w, k, c0, width=UNIT):
                sp.wait_ge(lo_ready, n - (SLOTS - 1))
                sp.dma_start(raw[:, j % SLOTS, 0:width], w[0, k * P:(k + 1) * P, ds(c0, width)])\
                  .then_inc(raw_in[j % SLOTS], 16)

            def square(n, j, w, k, c0, waits=1):
                if waits and not (isinstance(n, int) and n < SLOTS):
                    sp.wait_ge(lo_ready, n + waits - SLOTS)
                sp.dma_start(raw[:, j % SLOTS, :].rearrange("p (k c) -> p k c", k=2),
                             w[0, k * P:(k + 2) * P, ds(c0, BANK)].rearrange("(k p) c -> p k c", p=P))\
                  .then_inc(raw_in[j % SLOTS], 16)

            def load_x(half):
                sp.dma_start(res[:, :, half * UNIT:(half + 1) * UNIT],
                             x[0, :, half * UNIT:(half + 1) * UNIT].rearrange("(t p) c -> p t c", p=P))\
                  .then_inc(x_in[half], 16)

            def gate_up(u0, w_gate, w_up, i):
                for j in range(KD // 2):
                    if i is None:
                        if j == 1:
                            load_x(1)
                    square(u0 + (i or 0) * FFN_BODY + j if i is None else u0 + i * FFN_BODY + j, j, w_gate, 2 * j,
                           0 if i is None else i * BANK)
                for j in range(KD // 2):
                    n = KD // 2 + j
                    square(u0 + n if i is None else u0 + i * FFN_BODY + n, n, w_up, 2 * j, 0 if i is None else i * BANK)

            def projection(u0, c0):
                for k in range(KD):
                    wide(u0 + k, k, w_in, k, c0)

            Q_COLS, K_COLS, V_COLS = (LAT + a * UNIT for a in range(3))
            load_x(0)
            gate_up(U_GU1, w1_gate, w1_up, None)
            with sp.Fori(1, FFN_TURNS) as i:
                gate_up(U_GU1, w1_gate, w1_up, i)
            with sp.Fori(0, 2) as i:
                for k in range(KF):
                    wide(U_DOWN1 + i * KF + k, k, w1_down, k, i * UNIT)
            for k in range(KD):
                wide(U_LAT + k, k, w_in, k, 0, LAT)
            projection(U_V0, V_COLS)
            for h in range(2):
                for k in range(LQ // P):
                    wide(U_UQ + h * (LQ // P) + k, k, w_uq, k, h * HQ, HQ)
            for h in range(2):
                for k in range(LKV // P):
                    wide(U_UKV + h * (LKV // P) + k, h * (LKV // P) + k, w_ukv, k, h * HK, HK)
            projection(U_V1, V_COLS + 3 * UNIT)
            projection(U_QK, Q_COLS)
            with sp.Fori(0, GROUPS - 1) as g:
                projection(U_QK + KD + g * (2 * KD), K_COLS + g * (3 * UNIT))
                projection(U_QK + 2 * KD + g * (2 * KD), Q_COLS + 3 * UNIT + g * (3 * UNIT))
            projection(U_QK + (2 * GROUPS - 1) * KD, K_COLS + (GROUPS - 1) * 3 * UNIT)
            projection(U_V2, V_COLS + (GROUPS - 1) * 3 * UNIT)
            with sp.Fori(0, MERGE_TURNS) as i:
                j = 0
                for w, c0, K in ((w_in, OFF_GATE, KD), (w_br_mla, 0, H), (w_in, OFF_GATE + D, KD), (w_br_dil, 0, H)):
                    for k in range(0, K, 2):
                        waits = 2 if j == KD // 2 - 1 else 0 if j == KD // 2 else 1
                        square(U_MERGE + i * MERGE_BODY + j, j, w, k, c0 + i * BANK, waits)
                        j += 1
            with sp.Fori(0, 2) as i:
                for k in range(KD):
                    wide(U_WO + i * KD + k, k, w_o, k, i * UNIT)
            with sp.Fori(0, FFN_TURNS) as i:
                gate_up(U_GU2, w2_gate, w2_up, i)
            with sp.Fori(0, 2) as i:
                for k in range(KF):
                    wide(U_DOWN2 + i * KF + k, k, w2_down, k, i * UNIT)
            j = 0
            for h in range(2):
                for k in range(KD):
                    wide(U_PLE + j, j, w_ple_gate, k, h * UNIT)
                    j += 1
                for k in range(PLE // P):
                    wide(U_PLE + j, j, w_ple_proj, k, h * UNIT)
                    j += 1
            for h in range(2):
                for t in range(T):
                    sp.wait_ge(res_ready, PRIMED + 12 + 2 * h + t + 1)
                    sp.dma_start(out[0, t * P:(t + 1) * P, h * UNIT:(h + 1) * UNIT],
                                 res[:, t, h * UNIT:(h + 1) * UNIT]).then_inc(out_done, 16)
            sp.wait_ge(out_done, 4 * 16)

        @block.gpsimd
        def _(pool):
            for s in (gs_ready, am_ready, a_ready, res_ready, dil_turned, dil_T, dil_ready, gi_ready,
                      mgi_ready, mprod_ready, m_ready):
                pool.sem_inc(s, PRIMED)
            pool.memset(ones[:, :], 1.0).then_inc(ones_ready, 1)

        @block.tensor
        def _(pe):
            def wide_unit(n, j, k, hi, lo, b0, width, K):
                pe.wait_ge(lo_ready, n + 1)
                s = j % SLOTS
                cols = [(c, min(width, c + BANK)) for c in range(0, width, BANK)]
                for t in range(T):
                    xh, xl = hi[:, k, t * P:(t + 1) * P], lo[:, k, t * P:(t + 1) * P]
                    for a, w, first, last in ((xh, wh, k == 0, False), (xh, wl, False, False), (xl, wh, False, k == K - 1)):
                        for m, (c, e) in enumerate(cols):
                            mm = pe.matmul(ps[:, b0 + 2 * t + m, 0:e - c], a, w[:, s, c:e], start=first, stop=last)
                mm.then_inc(unit_done, 1)

            def square_unit(n, j, k, hi, lo, b0, K):
                pe.wait_ge(lo_ready, n + 1)
                s = j % SLOTS
                for kk in range(2):
                    for c in range(4):
                        w0 = kk * BANK + c * P
                        o = ps[:, b0 + c, 0:S]
                        pe.matmul(o, wh[:, s, w0:w0 + P], hi[:, k + kk, :], start=(k + kk == 0), stop=False)
                        pe.matmul(o, wh[:, s, w0:w0 + P], lo[:, k + kk, :], start=False, stop=False)
                        mm = pe.matmul(o, wl[:, s, w0:w0 + P], hi[:, k + kk, :], start=False, stop=(k + kk == K - 1))
                mm.then_inc(unit_done, 1)

            def turn(src, pairs, b0):
                for n, p in enumerate(pairs):
                    for s in range(2):
                        for t in range(T):
                            mm = pe.transpose(ps[:, b0 + n, s * S + t * P:s * S + (t + 1) * P],
                                              src[:, t, (2 * p + s) * P:(2 * p + s + 1) * P], ident[:, :])
                    mm.then_inc(turned, 1)

            LEFT, RIGHT = range(KD // 4), range(KD // 4, KD // 2)

            def entry(r, j):
                if j == 0:
                    pe.wait_ge(tr_lo, 2 * PAIRS[r] + KD // 2)
                if j == 2:
                    if r == 0:
                        pe.wait_ge(x_in[1], 16)
                        pe.wait_ge(tr_lo, KD // 2)
                    else:
                        pe.wait_ge(res_ready, PRIMED + 4 * r)
                    turn(res, RIGHT, 4)
                if j == 6:
                    pe.wait_ge(diag_ready, 2 * r + 1)
                    pe.wait_ge(tr_lo, 2 * PAIRS[r] + KD // 2 + 2)
                    pe.wait_ge(ones_ready, 1)
                    pe.matmul(ps[:, 4, 0:P], ones[:, :], diag[:, :], start=True, stop=True).then_inc(row_turned, 1)
                if j == 7:
                    pe.wait_ge(diag_ready, 2 * r + 2)
                    pe.wait_ge(row_ready, 2 * r + 1)
                    pe.matmul(ps[:, 4, P:2 * P], ones[:, :], diag[:, :], start=True, stop=True).then_inc(row_turned, 1)

            def gate_up(u0, f):
                r = 2 * f
                for j in range(KD // 2):
                    entry(r, j)
                    pe.wait_ge(tr_lo, 2 * PAIRS[r] + 2 * j + 2)
                    square_unit(u0 + j, j, 2 * j, hTh, hTl, 0, KD)
                pe.wait_ge(tr_lo, 2 * PAIRS[r] + KD)
                pe.wait_ge(row_ready, 2 * r + 2)
                for j in range(KD // 2):
                    square_unit(u0 + KD // 2 + j, j, 2 * j, hTh, hTl, 4, KD)
                with pe.Fori(1, FFN_TURNS) as i:
                    pe.wait_ge(gi_ready, PRIMED + f * FFN_TURNS + i)
                    for j in range(KD // 2):
                        square_unit(u0 + i * FFN_BODY + j, j, 2 * j, hTh, hTl, 0, KD)
                    pe.wait_ge(am_ready, PRIMED + f * FFN_TURNS + i)
                    for j in range(KD // 2):
                        square_unit(u0 + i * FFN_BODY + KD // 2 + j, j, 2 * j, hTh, hTl, 4, KD)

            def down(u0, hi, lo, K, r, ready, before, after):
                pe.wait_ge(ready, PRIMED + before)
                for half in range(2):
                    for k in range(K):
                        if half == 0 and k == K - 4:
                            pe.wait_ge(ready, PRIMED + after)
                        if half == 1 and k == 6:
                            pe.wait_ge(res_ready, PRIMED + 4 * (r - 1) + 2)
                            turn(res, LEFT, 0)
                        wide_unit(u0 + half * K + k, k, k, hi, lo, 4 * half, UNIT, K)

            def attention(first, scores, values, n_keys, prob, pT):
                def score(u):
                    h, t = items[u]
                    if u >= 2:
                        pe.wait_ge(masked, first + u - 1)
                    b = 2 * (u % 2)
                    for c, keys, parts in scores(h, t):
                        for m, (q, k) in enumerate(parts):
                            mm = pe.matmul(flat[:, b * BANK + c:b * BANK + c + keys], q, k,
                                           start=(m == 0), stop=(m == len(parts) - 1))
                    mm.then_inc(score_done, 1)

                def output(u):
                    h, t = items[u]
                    n = n_keys * (t + 1)
                    pe.wait_ge(pT_ready, first + u + 1)
                    if u >= 2:
                        pe.wait_ge(o_lo, first + u - 1)
                    for m in range(n):
                        mm = pe.matmul(ps[:, 6 + u % 2, 0:P], values(h, t, m), pT[:, m * P:(m + 1) * P],
                                       start=(m == 0), stop=(m == n - 1))
                    mm.then_inc(pv_done, 1)

                score(0)
                score(1)
                for u, (h, t) in enumerate(items):
                    pe.wait_ge(prob_ready, first + u + 1)
                    if u:
                        pe.wait_ge(pT_ready, first + u)
                    for m in range(n_keys * (t + 1)):
                        mm = pe.transpose(flat[:, 4 * BANK + m * P:4 * BANK + (m + 1) * P],
                                          prob[:, u % 3, m * P:(m + 1) * P], ident[:, :])
                    mm.then_inc(prob_turned, 1)
                    if u:
                        output(u - 1)
                    if u + 2 < len(items):
                        score(u + 2)
                output(len(items) - 1)

            pe.wait_ge(ident_in, 16)
            pe.wait_ge(rows_in, 16 * 6)
            pe.transpose(ps[:, 0, 0:4 * KD + NG], grow[:, :], ident[0:4 * KD + NG, 0:4 * KD + NG])\
              .then_inc(gains_turned, 1)
            pe.wait_ge(x_in[0], 16)
            turn(res, LEFT, 4)
            pe.wait_ge(gcol_ready, 1)

            gate_up(U_GU1, 0)
            down(U_DOWN1, aTh, aTl, KF, 1, a_ready, FFN_TURNS - 1, FFN_TURNS)

            for k in range(KD):
                entry(1, k)
                if k % 2 == 0:
                    pe.wait_ge(tr_lo, 2 * PAIRS[1] + k + 2)
                wide_unit(U_LAT + k, k, k, hTh, hTl, 0, LAT, KD)
            for k in range(KD):
                if k == 0:
                    pe.wait_ge(tr_lo, 2 * PAIRS[1] + KD)
                    pe.wait_ge(row_ready, 4)
                if k == 4:
                    pe.wait_ge(lat_ready, 1)
                    turn(c_tok, range(NG // 2), 0)
                wide_unit(U_V0 + k, k, k, hTh, hTl, 4, UNIT, KD)
            pe.wait_ge(tr_lo, 2 * C_PAIRS + NG)
            for h in range(2):
                if h:
                    pe.wait_ge(dil_v, 2)
                for k in range(LQ // P):
                    wide_unit(U_UQ + h * (LQ // P) + k, k, k, cTh, cTl, 4 * h, HQ, LQ // P)
            ch, cl = cTh[:, LQ // P:NG, :], cTl[:, LQ // P:NG, :]
            for h in range(2):
                pe.wait_ge(uq_tok, 2 * h + 2)
                for k in range(LKV // P):
                    wide_unit(U_UKV + h * (LKV // P) + k, h * (LKV // P) + k, k, ch, cl, 4 * h, HK, LKV // P)
            pe.wait_ge(ukv_tok, 2)
            for k in range(KD):
                wide_unit(U_V1 + k, k, k, hTh, hTl, 0, UNIT, KD)

            pe.wait_ge(ukv_tok, 4)
            pe.wait_ge(mla_ready, 2)
            for a in range(2):
                for h2 in range(H // 2):
                    for t in range(T):
                        c0 = (h2 % 2) * S + t * P
                        mm = pe.transpose(ps[:, 4 + 2 * a + h2 // 2, c0:c0 + P],
                                          rh[:, t, a, 2 * h2:2 * h2 + 2, :].rearrange("p h c -> p (h c)"), ident[:, :])
                mm.then_inc(mla_turned, 1)
            pe.wait_ge(dil_v, 4)
            for h in range(H):
                b = h % 8
                if h >= 4:
                    pe.wait_ge(rT_ready, 2)
                for t in range(T):
                    pe.transpose(ps[:, b, t * P:(t + 1) * P], q_tok[:, t, h * QK:h * QK + NOPE], ident[:, :])
                for t in range(T):
                    c0 = h * (NOPE + HD)
                    mm = pe.transpose(ps[:, b, S + t * P:S + (t + 1) * P], kv_tok[:, t, c0:c0 + NOPE], ident[:, :])
                mm.then_inc(mla_turned, 1)
            pe.wait_ge(nT_even, H // 2)
            pe.wait_ge(nT_odd, H // 2)

            def mla_scores(h, t):
                q0, r0 = t * P, (h % 2) * ROPE
                keys = (t + 1) * P
                yield 0, keys, [(nT[:, h, 0, q0:q0 + P], nT[:, h, 1, 0:keys]),
                                (rT[r0:r0 + ROPE, 0, h // 2, q0:q0 + P], rT[r0:r0 + ROPE, 1, h // 2, 0:keys])]

            def mla_values(h, t, m):
                c0 = h * (NOPE + HD) + NOPE
                return kv_tok[:, m, c0:c0 + HD]

            attention(0, mla_scores, mla_values, 1, prob_m, pT_m)

            def qk_pass(s, a, u0, b0=None, after=None):
                for k in range(KD):
                    if k == 11 and after is not False:
                        pe.wait_ge(dil_ready, PRIMED + 2 * s)
                        for h in range(H):
                            for t in range(T):
                                c0 = (4 - 4 * a) * BANK + h * S + t * P
                                mm = pe.transpose(flat[:, c0:c0 + P], tok[:, t, h * HD:(h + 1) * HD], ident[:, :])
                        mm.then_inc(dil_turned, 1)
                    wide_unit(u0 + k, k, k, hTh, hTl, 4 * a, UNIT, KD)

            pe.wait_ge(masked, len(items))
            qk_pass(0, 0, U_QK, after=False)
            pe.wait_ge(o_lo, len(items))
            with pe.Fori(0, GROUPS - 1) as g:
                pe.wait_ge(dil_T, PRIMED + 4 * g)
                qk_pass(2 * g + 1, 1, U_QK + KD + g * (2 * KD))
                pe.wait_ge(dil_T, PRIMED + 4 * g + 2)
                qk_pass(2 * g + 2, 0, U_QK + 2 * KD + g * (2 * KD))
            last = 2 * GROUPS - 1
            pe.wait_ge(dil_T, PRIMED + 2 * last - 2)
            qk_pass(last, 1, U_QK + last * KD)
            pe.wait_ge(dil_T, PRIMED + 2 * last)
            qk_pass(last + 1, 0, U_V2)

            def dil_scores(h, t):
                keys = (t + 1) * P
                for g in range(GROUPS):
                    q0, k0 = h * S + t * P, h * S
                    yield g * keys, keys, [(qT[:, g, q0:q0 + P], kT[:, g, k0:k0 + keys])]

            def dil_values(h, t, m):
                g, tk = m // (t + 1), m % (t + 1)
                return vd[:, g, tk * UNIT + h * HD:tk * UNIT + (h + 1) * HD]

            pe.wait_ge(dil_T, PRIMED + 4 * GROUPS)
            pe.wait_ge(dil_v, 6)
            attention(len(items), dil_scores, dil_values, GROUPS, prob_d, pT_d)

            with pe.Fori(0, MERGE_TURNS) as i:
                j = 0
                for part, (hi, lo, K) in enumerate(((hTh, hTl, KD), (omh, oml, H), (hTh, hTl, KD), (odh, odl, H))):
                    if part % 2 == 0:
                        pe.wait_ge(mgi_ready, PRIMED + 2 * i + part // 2)
                    else:
                        pe.wait_ge(mprod_ready, PRIMED + 2 * i + part // 2)
                    if part == 1:
                        pe.wait_ge(o_lo, 2 * len(items))
                    for k in range(0, K, 2):
                        square_unit(U_MERGE + i * MERGE_BODY + j, j, k, hi, lo, 4 * (part % 2), K)
                        j += 1
            pe.wait_ge(mgi_ready, PRIMED + 2 * MERGE_TURNS)
            down(U_WO, mTh, mTl, KD, 2, m_ready, MERGE_TURNS - 1, MERGE_TURNS)

            gate_up(U_GU2, 1)
            down(U_DOWN2, aTh, aTl, KF, 3, a_ready, 2 * FFN_TURNS - 1, 2 * FFN_TURNS)

            j = 0
            for h in range(2):
                if h:
                    pe.wait_ge(psig_ready, 2)
                for k in range(KD):
                    if h == 0:
                        entry(3, k)
                        if k % 2 == 0:
                            pe.wait_ge(tr_lo, 2 * PAIRS[3] + k + 2)
                        if k == 10:
                            pe.wait_ge(p_in, 16)
                            pe.wait_ge(tr_lo, 2 * PAIRS[3] + KD)
                            for t in range(T):
                                for c in range(PLE // P):
                                    mm = pe.transpose(ps[:, 5, c * S + t * P:c * S + (t + 1) * P],
                                                      p_tok[:, t, c * P:(c + 1) * P], ident[:, :])
                            mm.then_inc(p_turned, 1)
                    wide_unit(U_PLE + j, j, k, hTh, hTl, 0, UNIT, KD)
                    j += 1
                if h == 0:
                    pe.wait_ge(p_lo, 1)
                    pe.wait_ge(row_ready, 8)
                else:
                    pe.wait_ge(psig_used, 2)
                for k in range(PLE // P):
                    wide_unit(U_PLE + j, j, k, pTh, pTl, 4, UNIT, PLE // P)
                    j += 1

        @block.scalar
        def _(act):
            act.dma_start(ident[:, :], identity).then_inc(ident_in, 16)
            for r, g in enumerate((g_ffn1, g_mix, g_ffn2, g_ple)):
                act.dma_start(grow[r * KD:(r + 1) * KD, :], g[0].rearrange("(k p) -> k p", p=P)).then_inc(rows_in, 16)
            act.dma_start(grow[4 * KD:4 * KD + LQ // P, :], g_cq[0].rearrange("(k p) -> k p", p=P)).then_inc(rows_in, 16)
            act.dma_start(grow[4 * KD + LQ // P:, :], g_ckv[0].rearrange("(k p) -> k p", p=P)).then_inc(rows_in, 16)

            def later_loads():
                act.dma_start(freq[:, :], inverse_frequencies[0].partition_broadcast(P)).then_inc(consts_in, 16)
                with nc.allow_non_contiguous_dma(reason="256 positions"):
                    act.dma_start(pos_i[:, :], positions[0].rearrange("(t p) -> p t", p=P)).then_inc(consts_in, 16)
                for dst, src in ((gq_mla, g_q_mla[0]), (gk_mla, g_k_mla[0])):
                    act.dma_start(dst[:, :], src.partition_broadcast(P)).then_inc(gains_in, 16)
                for dst, src in ((gq_dil, g_q_dil[0]), (gk_dil, g_k_dil[0])):
                    act.dma_start(dst[:, :, :], src.partition_broadcast(P)).then_inc(gains_in, 16)
                act.dma_start(m_mla[:, :], mla_masks).then_inc(gains_in, 16)
                act.dma_start(m_dil[:, :, :], dil_masks.rearrange("p (g c) -> p g c", g=GROUPS)).then_inc(gains_in, 16)

            def split(n, j):
                first = isinstance(n, int) and n < SLOTS
                act.wait_ge(raw_in[j % SLOTS], ((n - j % SLOTS) * (16 // SLOTS) + 16) if not isinstance(n, int)
                            else 16 * (n // SLOTS + 1))
                if not first:
                    act.wait_ge(unit_done, n - (SLOTS - 1))
                act.activation(wh[:, j % SLOTS, :], raw[:, j % SLOTS, :], ACT.Copy).then_inc(hi_ready, 1)

            def ahead(n, j):
                split(n + SLOTS, j)

            def root(src, dst, ready, count, done):
                act.wait_ge(ready, count)
                act.activation(dst, src, ACT.Sqrt).then_inc(done, 1)

            def high(dst, g0, before, pairs, b0):
                for n, p in enumerate(pairs):
                    act.wait_ge(turned, before + p + 1)
                    for s in range(2):
                        k = 2 * p + s
                        act.activation(dst[:, k, :], ps[:, b0 + n, s * S:(s + 1) * S], ACT.Copy,
                                       scale=gcol[:, g0 + k:g0 + k + 1]).then_inc(tr_hi, 1)

            LEFT, RIGHT = range(KD // 4), range(KD // 4, KD // 2)

            def squares(r, half):
                for t in range(T):
                    if r == 0:
                        act.wait_ge(x_in[half], 16)
                    else:
                        act.wait_ge(res_ready, PRIMED + 4 * (r - 1) + 2 * half + t + 1)
                    if 4 * r + 2 * half + t:
                        act.wait_ge(ss_ready, 4 * r + 2 * half + t)
                    c = 2 * half + t
                    act.activation(junk[:, :], res[:, t, half * UNIT:(half + 1) * UNIT], ACT.Square,
                                   accum_out=ssq[:, c:c + 1]).then_inc(ss_ready, 1)

            def entry(r, j):
                if j == 0:
                    squares(r, 1)
                if j == 1:
                    high(hTh, r * KD, PAIRS[r], RIGHT, 4)
                if j == 2:
                    root(var, dev, var_ready, r + 1, dev_ready)

            def gate_up(u0, f):
                def turn(i, j):
                    if j == KD // 2 - 1:
                        act.wait_ge(gi_ready, PRIMED + f * FFN_TURNS + i + 1)
                        act.activation(sg[:, :, :], gs[:, :, :], ACT.Sigmoid).then_inc(sig_ready, 1)
                    if j == FFN_BODY - 1:
                        act.wait_ge(am_ready, PRIMED + f * FFN_TURNS + i + 1)
                        act.activation(aTh[:, ds(i * 4, 4), :], gs[:, :, :], ACT.Copy).then_inc(ah_ready, 1)

                for j in range(FFN_BODY):
                    ahead(u0 + j, j)
                    entry(2 * f, j)
                    turn(0, j)
                with act.Fori(1, FFN_TURNS) as i:
                    for j in range(FFN_BODY):
                        ahead(u0 + i * FFN_BODY + j, j)
                        turn(i, j)

            def down(u0, K, r):
                for half in range(2):
                    for k in range(K):
                        ahead(u0 + half * K + k, k)
                        if half == 1 and k == 5:
                            squares(r, 0)
                        if half == 1 and k in (6, 8, 10, 12):
                            high(hTh, r * KD, PAIRS[r], LEFT[k // 2 - 3:k // 2 - 2], k // 2 - 3)

            def v_tile(g, b0):
                act.activation(vd[:, g, 0:UNIT], banks(b0, UNIT), ACT.Copy, scale=inv[:, 0:1]).then_inc(dil_v, 1)

            def attention(first, prob, pT, oh, n_keys, scale):
                def exp(u):
                    h, t = items[u]
                    n = n_keys * (t + 1) * P
                    act.wait_ge(masked, first + u + 1)
                    act.activation(prob[:, u % 3, 0:n], prob[:, u % 3, 0:n], ACT.Exp, bias=s_bias[:, u:u + 1],
                                   scale=scale, accum_out=s_sum[:, u:u + 1]).then_inc(exp_done, 1)

                def out_high(u):
                    h, t = items[u]
                    act.wait_ge(pv_done, first + u + 1)
                    act.activation(oh[:, h, t * P:(t + 1) * P], ps[:, 6 + u % 2, 0:P], ACT.Copy).then_inc(o_hi, 1)

                exp(0)
                for u, (h, t) in enumerate(items):
                    if u + 1 < len(items):
                        exp(u + 1)
                    n = n_keys * (t + 1) * P
                    act.wait_ge(prob_turned, first + u + 1)
                    if u:
                        act.wait_ge(pv_done, first + u)
                    act.activation(pT[:, 0:n], banks(4, n), ACT.Copy).then_inc(pT_ready, 1)
                    if u:
                        out_high(u - 1)
                out_high(len(items) - 1)

            act.wait_ge(gains_turned, 1)
            act.activation(gcol[:, :], ps[:, 0, 0:4 * KD + NG], ACT.Copy).then_inc(gcol_ready, 1)
            act.wait_ge(gcol_ready, 1)
            high(hTh, 0, PAIRS[0], LEFT, 4)
            for n in range(SLOTS):
                split(n, n)
                if n == 1:
                    squares(0, 0)
            later_loads()
            gate_up(U_GU1, 0)
            for n, (dst, t) in enumerate((d, t) for t in range(T) for d in (sin, cos)):
                act.wait_ge(angles_ready, n + 1)
                act.activation(dst[:, t, :], turns[:, :], ACT.Sin).then_inc(tables_ready, 1)
            down(U_DOWN1, KF, 1)

            for k in range(KD):
                ahead(U_LAT + k, k)
                entry(1, k)
            act.wait_ge(inv_ready, 2)
            for t in range(T):
                act.activation(c_tok[:, t, :], banks(2 * t, LAT), ACT.Copy, scale=inv[:, t:t + 1]).then_inc(lat_tok, 1)
            act.wait_ge(lat_tok, T)
            for t in range(T):
                for a, (c0, c1) in enumerate(((0, LQ), (LQ, LQ + LKV), (LQ + LKV, LAT))):
                    total = css[:, 2 * t + a:2 * t + a + 1] if a < 2 else kss_m[:, t:t + 1]
                    src = flat[:, 2 * t * BANK + c0:2 * t * BANK + c1]
                    act.activation(src, c_tok[:, t, c0:c1], ACT.Square, accum_out=total).then_inc(lat_ss, 1)
            for k in range(KD):
                ahead(U_V0 + k, k)
                if k == 1:
                    root(cvar, cdev, lat_var, 2, lat_dev)
                if k == 4:
                    high(cTh, 4 * KD, C_PAIRS, range(NG // 2), 0)
            v_tile(0, 4)
            for h in range(2):
                for k in range(LQ // P):
                    ahead(U_UQ + h * (LQ // P) + k, k)
                for t in range(T):
                    act.activation(q_tok[:, t, h * HQ:(h + 1) * HQ], banks(4 * h + 2 * t, HQ), ACT.Copy).then_inc(uq_tok, 1)
            for h in range(2):
                for k in range(LKV // P):
                    ahead(U_UKV + h * (LKV // P) + k, h * (LKV // P) + k)
                for t in range(T):
                    act.activation(kv_tok[:, t, h * HK:(h + 1) * HK], banks(4 * h + 2 * t, HK), ACT.Copy)\
                       .then_inc(ukv_tok, 1)
            act.wait_ge(uq_tok, 4)
            act.wait_ge(ukv_tok, 4)
            for k in range(KD):
                ahead(U_V1 + k, k)
                if k in (0, 1):
                    if k:
                        act.wait_ge(mla_ss, k)
                    act.activation(sq[:, :], q_tok[:, k, :], ACT.Square).then_inc(mla_sq, 1)
                if k in (2, 3):
                    act.wait_ge(mla_ss, k)
                    act.activation(sq[:, 0:H * NOPE].rearrange("p (h c) -> p h c", h=H),
                                   kv_tok[:, k - 2, :].rearrange("p (h c) -> p h c", h=H)[:, :, 0:NOPE],
                                   ACT.Square).then_inc(mla_sq, 1)
                if k == 4:
                    root(mvar, mdev, mla_var, 1, mla_dev)
                if k in (5, 6, 7, 8):
                    if k == 5:
                        act.wait_ge(mla_inv, 1)
                    t, a = (k - 5) // 2, (k - 5) % 2
                    for h in range(H):
                        c = (a * T + t) * H + h
                        v = kv_tok[:, t, h * (NOPE + HD):h * (NOPE + HD) + NOPE] if a else q_tok[:, t, h * QK:(h + 1) * QK]
                        last = act.activation(v, v, ACT.Copy, scale=minv[:, c:c + 1])
                    last.then_inc(mla_scaled, 1)
            v_tile(1, 0)
            for h in range(2, 2 + H, 2):
                act.wait_ge(mla_turned, h + 1)
                act.activation(nT[:, h - 2, :, :], ps[:, h - 2, :].rearrange("p (a s) -> p a s", a=2), ACT.Copy)\
                   .then_inc(nT_even, 1)
            attention(0, prob_m, pT_m, omh, 1, SCALE_MLA)

            def evict(s, a):
                act.wait_ge(dil_turned, PRIMED + s)
                for t in range(T):
                    act.activation(tok[:, t, :], banks(4 * a + 2 * t, UNIT), ACT.Copy, scale=inv[:, t:t + 1])\
                       .then_inc(dil_tok, 1)
                act.wait_ge(dil_tok, 2 * s + 2)
                for t in range(T):
                    act.activation(banks(4 * a + 2 * t, UNIT), tok[:, t, :], ACT.Square).then_inc(dil_sq, 1)

            def follow(s, a, g, k):
                if k == 2:
                    root(dvar, ddev, dil_var, s + 1, dil_dev)
                if k == 11:
                    act.wait_ge(dil_turned, PRIMED + s + 1)
                    for e in range(2):
                        act.activation((qT, kT)[a][:, ds(g, 1), e * UNIT:(e + 1) * UNIT].rearrange("p a c -> p (a c)"),
                                       banks(4 * a + 2 * e, UNIT), ACT.Copy).then_inc(dil_T, 1)

            for k in range(KD):
                ahead(U_QK + k, k)
            evict(0, 0)
            with act.Fori(0, GROUPS - 1) as g:
                for k in range(KD):
                    ahead(U_QK + KD + g * (2 * KD) + k, k)
                    follow(2 * g, 0, g, k)
                evict(2 * g + 1, 1)
                for k in range(KD):
                    ahead(U_QK + 2 * KD + g * (2 * KD) + k, k)
                    follow(2 * g + 1, 1, g, k)
                evict(2 * g + 2, 0)
            last = 2 * GROUPS - 1
            for k in range(KD):
                ahead(U_QK + last * KD + k, k)
                follow(last - 1, 0, GROUPS - 1, k)
            evict(last, 1)
            for k in range(KD):
                ahead(U_V2 + k, k)
                follow(last, 1, GROUPS - 1, k)
            v_tile(GROUPS - 1, 0)
            attention(len(items), prob_d, pT_d, odh, GROUPS, SCALE_DIL)

            with act.Fori(0, MERGE_TURNS) as i:
                for j in range(MERGE_BODY):
                    ahead(U_MERGE + i * MERGE_BODY + j, j)
                    for a in range(2):
                        if j == a * (MERGE_BODY // 2) + KD // 2 - 1:
                            act.wait_ge(mgi_ready, PRIMED + 2 * i + a + 1)
                            act.activation(sg[:, :, :], sg[:, :, :], ACT.Sigmoid).then_inc(msig_ready, 1)
                    if j == MERGE_BODY - 1:
                        act.wait_ge(m_sum, i + 1)
                        act.activation(mTh[:, ds(i * 4, 4), :], gs[:, :, :], ACT.Copy).then_inc(mh_ready, 1)
            down(U_WO, KD, 2)
            gate_up(U_GU2, 1)
            down(U_DOWN2, KF, 3)

            act.wait_ge(unit_done, U_PLE)
            act.dma_start(p_tok[:, :, :], p[0, 0].rearrange("(t p) c -> p t c", p=P)).then_inc(p_in, 16)
            j = 0
            for h in range(2):
                for k in range(KD + PLE // P):
                    if U_PLE + j + SLOTS < UNITS:
                        ahead(U_PLE + j, j)
                    if h == 0:
                        entry(3, k)
                    if h == 0 and k == 10:
                        act.wait_ge(p_turned, 1)
                        act.activation(pTh[:, :, :], ps[:, 5, :].rearrange("p (k s) -> p k s", s=S), ACT.Copy).then_inc(p_hi, 1)
                    if k == KD - 1:
                        act.wait_ge(unit_done, U_PLE + j + 1)
                        if h == 0:
                            act.wait_ge(inv_ready, 4)
                        for t in range(T):
                            if h:
                                act.wait_ge(res_ready, PRIMED + 12 + t + 1)
                            act.activation(sgp[:, t, :], banks(2 * t, UNIT), ACT.Sigmoid, scale=inv[:, t:t + 1])\
                               .then_inc(psig_ready, 1)
                    j += 1

        @block.vector
        def _(dve):
            chain = Chain(dve, dve_step)

            def split(n, j):
                dve.wait_ge(hi_ready, n + 1)
                dve.tensor_tensor(wl[:, j % SLOTS, :], raw[:, j % SLOTS, :], wh[:, j % SLOTS, :].bitcast(F32),
                                  ALU.subtract).then_inc(lo_ready, 1)

            def ahead(n, j):
                split(n + SLOTS, j)

            def rsqrt(v, s, y, tmp, ready, count):
                dve.wait_ge(ready, count)
                chain(dve.reciprocal(y, s))
                chain(dve.scalar_tensor_tensor(out=tmp, in0=y, scalar=-0.5, in1=y, op0=ALU.mult, op1=ALU.mult))
                chain(dve.tensor_tensor(tmp, tmp, v, ALU.mult))
                return dve.scalar_tensor_tensor(out=y, in0=tmp, scalar=1.5, in1=y, op0=ALU.add, op1=ALU.mult)

            def rest(dst, hi, g0, before, pairs, b0):
                for n, p in enumerate(pairs):
                    dve.wait_ge(tr_hi, 2 * (before + p) + 2)
                    for s in range(2):
                        k = 2 * p + s
                        dve.scalar_tensor_tensor(out=dst[:, k, :], in0=ps[:, b0 + n, s * S:(s + 1) * S],
                                                 scalar=gcol[:, g0 + k:g0 + k + 1], in1=hi[:, k, :].bitcast(F32),
                                                 op0=ALU.mult, op1=ALU.subtract).then_inc(tr_lo, 1)

            LEFT, RIGHT = range(KD // 4), range(KD // 4, KD // 2)

            def entry(r, j):
                if j == 1:
                    rest(hTl, hTh, r * KD, PAIRS[r], RIGHT, 4)
                if j == 2:
                    dve.wait_ge(ss_ready, 4 * r + 4)
                    chain(dve.tensor_tensor(var, ssq[:, 0:2], ssq[:, 2:4], ALU.add))
                    dve.tensor_scalar(var, var, 1.0 / D, EPS, ALU.mult, ALU.add).then_inc(var_ready, 1)
                    rsqrt(var, dev, inv, nwt, dev_ready, r + 1).then_inc(inv_ready, 1)
                    dve.wait_ge(inv_ready, r + 1)
                    if r:
                        dve.wait_ge(row_turned, 2 * r)
                    dve.tensor_scalar(diag[:, :], ident[:, :], inv[:, 0:1], None, ALU.mult).then_inc(diag_ready, 1)
                if j == 6:
                    dve.wait_ge(row_turned, 2 * r + 1)
                    dve.tensor_scalar(diag[:, :], ident[:, :], inv[:, 1:2], None, ALU.mult).then_inc(diag_ready, 1)
                    dve.tensor_copy(inv_row[:, 0:P], ps[:, 4, 0:P]).then_inc(row_ready, 1)
                if j == 7:
                    dve.wait_ge(row_turned, 2 * r + 2)
                    dve.tensor_copy(inv_row[:, P:2 * P], ps[:, 4, P:2 * P]).then_inc(row_ready, 1)
                    dve.wait_ge(row_ready, 2 * r + 2)

            rms4 = inv_row[:, :].unsqueeze(1).to_broadcast([P, 4, S])

            def gate_up(u0, f):
                def turn(i, j, n):
                    if j == KD // 2 - 1:
                        dve.wait_ge(unit_done, n + 1)
                        dve.wait_ge(a_ready, PRIMED + f * FFN_TURNS + i)
                        dve.tensor_tensor(gs[:, :, :], ps[:, 0:4, 0:S], rms4, ALU.mult).then_inc(gi_ready, 1)
                    if j == KD // 2:
                        dve.wait_ge(sig_ready, f * FFN_TURNS + i + 1)
                        chain(dve.tensor_tensor(gs[:, :, :], gs[:, :, :], sg[:, :, :], ALU.mult))
                        dve.tensor_tensor(gs[:, :, :], gs[:, :, :], rms4, ALU.mult).then_inc(gs_ready, 1)
                    if j == FFN_BODY - 1:
                        dve.wait_ge(unit_done, n + 1)
                        dve.wait_ge(gs_ready, PRIMED + f * FFN_TURNS + i + 1)
                        dve.tensor_tensor(gs[:, :, :], ps[:, 4:8, 0:S], gs[:, :, :], ALU.mult).then_inc(am_ready, 1)
                        dve.wait_ge(ah_ready, f * FFN_TURNS + i + 1)
                        dve.tensor_tensor(aTl[:, ds(i * 4, 4), :], gs[:, :, :],
                                          aTh[:, ds(i * 4, 4), :].bitcast(F32), ALU.subtract).then_inc(a_ready, 1)

                for j in range(FFN_BODY):
                    ahead(u0 + j, j)
                    entry(2 * f, j)
                    turn(0, j, u0 + j)
                with dve.Fori(1, FFN_TURNS) as i:
                    chain.enter(i - 1, 1)
                    for j in range(FFN_BODY):
                        ahead(u0 + i * FFN_BODY + j, j)
                        turn(i, j, u0 + i * FFN_BODY + j)
                    chain.leave(FFN_TURNS - 1)

            def down(u0, K, r, factor):
                for half in range(2):
                    for k in range(K):
                        if k == K - 1:
                            dve.wait_ge(unit_done, u0 + half * K + K)
                            for t in range(T):
                                part = res[:, t, half * UNIT:(half + 1) * UNIT]
                                dve.scalar_tensor_tensor(out=part, in0=banks(4 * half + 2 * t, UNIT), scalar=factor,
                                                         in1=part, op0=ALU.mult, op1=ALU.add).then_inc(res_ready, 1)
                        ahead(u0 + half * K + k, k)
                        if half == 1 and k in (6, 8, 10, 12):
                            rest(hTl, hTh, r * KD, PAIRS[r], LEFT[k // 2 - 3:k // 2 - 2], k // 2 - 3)

            def rotate(x1, x2, c, s, a, b):
                dve.tensor_tensor(a, x2, s, ALU.mult)
                chain(dve.tensor_tensor(b, x1, s, ALU.mult))
                dve.tensor_tensor(x1, x1, c, ALU.mult)
                chain(dve.tensor_tensor(x2, x2, c, ALU.mult))
                dve.tensor_tensor(x1, x1, a, ALU.subtract)
                return dve.tensor_tensor(x2, x2, b, ALU.add)

            def v_tile(g, b0):
                dve.tensor_scalar(vd[:, g, UNIT:2 * UNIT], banks(b0 + 2, UNIT), inv[:, 1:2], None, ALU.mult)\
                   .then_inc(dil_v, 1)

            def attention(first, prob, masks, ol, oh, n_keys, scale):
                def mask(u):
                    h, t = items[u]
                    n = n_keys * (t + 1) * P
                    dve.wait_ge(score_done, first + u + 1)
                    if u >= 3:
                        dve.wait_ge(prob_turned, first + u - 2)
                    a = prob[:, u % 3, 0:n].rearrange("p (g c) -> p g c", g=n_keys)
                    s = banks(2 * (u % 2), n).rearrange("p (g c) -> p g c", g=n_keys)
                    chain(dve.tensor_tensor_reduce(a, s, masks(t), 1.0, -3.0e38, ALU.add, ALU.max, s_max[:, u:u + 1]))
                    dve.tensor_scalar(s_bias[:, u:u + 1], s_max[:, u:u + 1], -scale, None, ALU.mult).then_inc(masked, 1)

                def out_rest(u):
                    h, t = items[u]
                    dve.wait_ge(o_hi, first + u + 1)
                    dve.tensor_tensor(ol[:, h, t * P:(t + 1) * P], ps[:, 6 + u % 2, 0:P],
                                      oh[:, h, t * P:(t + 1) * P].bitcast(F32), ALU.subtract).then_inc(o_lo, 1)

                mask(0)
                for u, (h, t) in enumerate(items):
                    if u + 1 < len(items):
                        mask(u + 1)
                    n = n_keys * (t + 1) * P
                    dve.wait_ge(exp_done, first + u + 1)
                    chain(dve.reciprocal(s_inv[:, u:u + 1], s_sum[:, u:u + 1]))
                    dve.tensor_scalar(prob[:, u % 3, 0:n], prob[:, u % 3, 0:n], s_inv[:, u:u + 1], None, ALU.mult)\
                       .then_inc(prob_ready, 1)
                    if u >= 2:
                        out_rest(u - 2)
                out_rest(len(items) - 2)
                out_rest(len(items) - 1)

            rest(hTl, hTh, 0, PAIRS[0], LEFT, 4)
            for n in range(SLOTS):
                split(n, n)
            gate_up(U_GU1, 0)

            dve.wait_ge(consts_in, 16 * 2)
            chain(dve.tensor_copy(pos_f[:, :], pos_i[:, :]))
            for n, (t, quarter) in enumerate((t, q) for t in range(T) for q in (0.0, 0.25)):
                if n:
                    dve.wait_ge(angles_ready, n)
                chain(dve.tensor_scalar(angle[:, :], freq[:, :], pos_f[:, t:t + 1], None, ALU.mult))
                if n:
                    dve.wait_ge(tables_ready, n)
                chain(dve.tensor_scalar(turns[:, :], angle[:, :], 0.15915494309189535, quarter, ALU.mult, ALU.add))
                chain(dve.tensor_scalar(turns[:, :], turns[:, :], ROUND, -ROUND, ALU.add, ALU.add))
                for part in (TWO_PI_1, TWO_PI_2, TWO_PI_3):
                    chain(dve.scalar_tensor_tensor(out=angle[:, :], in0=turns[:, :], scalar=-part, in1=angle[:, :],
                                                   op0=ALU.mult, op1=ALU.add))
                chain(dve.tensor_scalar(angle[:, :], angle[:, :], quarter * 6.283185307179586, PI_DOWN, ALU.add, ALU.min))
                dve.tensor_scalar(turns[:, :], angle[:, :], -PI_DOWN, None, ALU.max).then_inc(angles_ready, 1)
            down(U_DOWN1, KF, 1, 0.5)

            for k in range(KD):
                ahead(U_LAT + k, k)
                entry(1, k)
            for k in range(KD):
                ahead(U_V0 + k, k)
                if k == 1:
                    dve.wait_ge(lat_ss, 6)
                    cs, cv = (a.rearrange("p (t a) -> p t a", a=2) for a in (css, cvar))
                    dve.tensor_scalar(cv[:, :, 0], cs[:, :, 0], 1.0 / LQ, EPS, ALU.mult, ALU.add).then_inc(lat_var, 1)
                    dve.tensor_scalar(cv[:, :, 1], cs[:, :, 1], 1.0 / LKV, EPS, ALU.mult, ALU.add).then_inc(lat_var, 1)
                    dve.wait_ge(lat_var, 2)
                    chain(rsqrt(cvar, cdev, cinv, cnwt, lat_dev, 1))
                if k == 2:
                    for t in range(T):
                        for a, (c0, c1) in enumerate(((0, LQ), (LQ, LQ + LKV))):
                            ins = dve.tensor_scalar(c_tok[:, t, c0:c1], c_tok[:, t, c0:c1],
                                                    cinv[:, 2 * t + a:2 * t + a + 1], None, ALU.mult)
                    ins.then_inc(lat_ready, 1)
                if k == 4:
                    rest(cTl, cTh, 4 * KD, C_PAIRS, range(NG // 2), 0)
            dve.wait_ge(unit_done, U_V0 + KD)
            v_tile(0, 4)
            for n in range(2 * (LQ // P)):
                ahead(U_UQ + n, n)
            for n in range(2 * (LKV // P)):
                ahead(U_UKV + n, n)

            ms = mss.rearrange("p (a t h) -> p a t h", a=2, t=T)
            mi = minv.rearrange("p (a t h) -> p a t h", a=2, t=T)

            def gain(g, a, e):
                return g[:, a:e].unsqueeze(1).to_broadcast([P, H, e - a])

            half = ROPE // 2
            for k in range(KD):
                ahead(U_V1 + k, k)
                if k < 4:
                    a, t = k // 2, k % 2
                    width = (QK, NOPE)[a]
                    dve.wait_ge(mla_sq, k + 1)
                    dve.tensor_reduce(ms[:, a, t, :], sq[:, 0:H * width].rearrange("p (h c) -> p h c", h=H),
                                      AX_X, ALU.add).then_inc(mla_ss, 1)
                if k == 4:
                    dve.wait_ge(mla_ss, 4)
                    dve.wait_ge(gains_in, 16 * 6)
                    for t in range(T):
                        chain(dve.tensor_scalar(ms[:, 1, t, :], ms[:, 1, t, :], kss_m[:, t:t + 1], None, ALU.add))
                    dve.tensor_scalar(mvar, mss, 1.0 / QK, EPS, ALU.mult, ALU.add).then_inc(mla_var, 1)
                    dve.wait_ge(mla_var, 1)
                    rsqrt(mvar, mdev, minv, mnwt, mla_dev, 1).then_inc(mla_inv, 1)
                    dve.wait_ge(mla_inv, 1)
                if k in (6, 7, 8, 9, 10, 11):
                    t = (k - 6) // 3
                    qv = q_tok[:, t, :].rearrange("p (h c) -> p h c", h=H)
                    kv = kv_tok[:, t, :].rearrange("p (h c) -> p h c", h=H)[:, :, 0:NOPE]
                    qr, kr = rh[:, t, 0, :, :], rh[:, t, 1, :, :]
                    if (k - 6) % 3 == 0:
                        ik = mi[:, 1, t, :].unsqueeze(2)
                        chain(dve.tensor_tensor(kr, c_tok[:, t, LQ + LKV:LAT].unsqueeze(1).to_broadcast([P, H, ROPE]),
                                                ik.to_broadcast([P, H, ROPE]), ALU.mult))
                        dve.tensor_tensor(kr, kr, gain(gk_mla, NOPE, QK), ALU.mult)
                        dve.wait_ge(mla_scaled, 2 * t + 1)
                        chain(dve.tensor_tensor(qr, qv[:, :, NOPE:QK], gain(gq_mla, NOPE, QK), ALU.mult))
                    if (k - 6) % 3 == 1:
                        if t:
                            dve.wait_ge(mla_ready, t)
                        both = rh[:, t, :, :, :].rearrange("p a h c -> p (a h) c")
                        c, s = (b[:, t, 0:half].unsqueeze(1).to_broadcast([P, 2 * H, half]) for b in (cos, sin))
                        chain(rotate(both[:, :, 0:half], both[:, :, half:ROPE], c, s, tmpA[:, :, :], tmpB[:, :, :]))
                    if (k - 6) % 3 == 2:
                        dve.wait_ge(mla_scaled, 2 * t + 2)
                        dve.tensor_tensor(qv[:, :, 0:NOPE], qv[:, :, 0:NOPE], gain(gq_mla, 0, NOPE), ALU.mult)
                        dve.tensor_tensor(kv, kv, gain(gk_mla, 0, NOPE), ALU.mult).then_inc(mla_ready, 1)
            dve.wait_ge(unit_done, U_V1 + KD)
            v_tile(1, 0)
            for a in range(2):
                dve.wait_ge(mla_turned, a + 1)
                dve.tensor_copy(rT[:, a, :, :].rearrange("p h s -> p (h s)"), banks(4 + 2 * a, UNIT)).then_inc(rT_ready, 1)
            for h in range(3, 2 + H, 2):
                dve.wait_ge(mla_turned, h + 1)
                dve.tensor_copy(nT[:, h - 2, :, :], ps[:, h - 2, :].rearrange("p (a s) -> p a s", a=2)).then_inc(nT_odd, 1)

            def mla_mask(t):
                return m_mla[:, (1 - t) * P:2 * P].unsqueeze(1)

            attention(0, prob_m, mla_mask, oml, omh, 1, SCALE_MLA)

            di = dinv.rearrange("p (t h) -> p t h", t=T)

            def follow(s, a, g, k):
                if k == 0:
                    for t in range(T):
                        dve.wait_ge(dil_sq, 2 * s + t + 1)
                        dve.tensor_reduce(dss[:, t * H:(t + 1) * H], banks(4 * a + 2 * t, UNIT)
                                          .rearrange("p (h c) -> p h c", h=H), AX_X, ALU.add).then_inc(dil_ss, 1)
                if k == 2:
                    dve.wait_ge(dil_ss, 2 * s + 2)
                    dve.tensor_scalar(dvar, dss, 1.0 / HD, EPS, ALU.mult, ALU.add).then_inc(dil_var, 1)
                    dve.wait_ge(dil_var, s + 1)
                    chain(rsqrt(dvar, ddev, dinv, dnwt, dil_dev, s + 1))
                for t in range(T):
                    if k == 3 + 2 * t:
                        gains = (gq_dil, gk_dil)[a][:, ds(g, 1), :].rearrange("p a c -> p (a c)")
                        for h in range(H):
                            v = tok[:, t, h * HD:(h + 1) * HD]
                            ins = dve.scalar_tensor_tensor(out=v, in0=v, scalar=di[:, t, h:h + 1], in1=gains,
                                                           op0=ALU.mult, op1=ALU.mult)
                        chain(ins)
                    if k == 4 + 2 * t:
                        v = tok[:, t, :].rearrange("p (h c) -> p h c", h=H)
                        hf = ROT // 2
                        c, sn = (b[:, t, NF - hf:NF].unsqueeze(1).to_broadcast([P, H, hf]) for b in (cos, sin))
                        dve.wait_ge(dil_ready, PRIMED + 2 * s + t)
                        rotate(v[:, :, 0:hf], v[:, :, hf:ROT], c, sn, ropeA[:, :, :], ropeB[:, :, :])\
                            .then_inc(dil_ready, 1)

            FOLLOW_STEPS = 4 + T * 3
            for k in range(KD):
                ahead(U_QK + k, k)
            with dve.Fori(0, GROUPS - 1) as g:
                chain.enter(g, 2 * FOLLOW_STEPS)
                for k in range(KD):
                    ahead(U_QK + KD + g * (2 * KD) + k, k)
                    follow(2 * g, 0, g, k)
                for k in range(KD):
                    ahead(U_QK + 2 * KD + g * (2 * KD) + k, k)
                    follow(2 * g + 1, 1, g, k)
                chain.leave(GROUPS - 1)
            last = 2 * GROUPS - 1
            for k in range(KD):
                ahead(U_QK + last * KD + k, k)
                follow(last - 1, 0, GROUPS - 1, k)
            for k in range(KD):
                ahead(U_V2 + k, k)
                follow(last, 1, GROUPS - 1, k)
            dve.wait_ge(unit_done, U_V2 + KD)
            v_tile(GROUPS - 1, 0)

            def dil_mask(t):
                return m_dil[:, :, (1 - t) * P:2 * P]

            attention(len(items), prob_d, dil_mask, odl, odh, GROUPS, SCALE_DIL)

            with dve.Fori(0, MERGE_TURNS) as i:
                for j in range(MERGE_BODY):
                    ahead(U_MERGE + i * MERGE_BODY + j, j)
                    for a in range(2):
                        if j == a * (MERGE_BODY // 2) + KD // 2 - 1:
                            dve.wait_ge(unit_done, U_MERGE + i * MERGE_BODY + j + 1)
                            dve.wait_ge(mprod_ready, PRIMED + 2 * i + a)
                            dve.tensor_tensor(sg[:, :, :], ps[:, 0:4, 0:S], rms4, ALU.mult).then_inc(mgi_ready, 1)
                        if j == (a + 1) * (MERGE_BODY // 2) - 1:
                            dve.wait_ge(msig_ready, 2 * i + a + 1)
                            dve.wait_ge(unit_done, U_MERGE + i * MERGE_BODY + j + 1)
                            dve.wait_ge(m_ready, PRIMED + i)
                            dst = (gs, am)[a]
                            dve.tensor_tensor(dst[:, :, :], ps[:, 4:8, 0:S], sg[:, :, :], ALU.mult).then_inc(mprod_ready, 1)
                    if j == MERGE_BODY - 1:
                        dve.wait_ge(mprod_ready, PRIMED + 2 * i + 2)
                        dve.tensor_tensor(gs[:, :, :], gs[:, :, :], am[:, :, :], ALU.add).then_inc(m_sum, 1)
                        dve.wait_ge(mh_ready, i + 1)
                        dve.tensor_tensor(mTl[:, ds(i * 4, 4), :], gs[:, :, :],
                                          mTh[:, ds(i * 4, 4), :].bitcast(F32), ALU.subtract).then_inc(m_ready, 1)
            down(U_WO, KD, 2, 1.0)
            gate_up(U_GU2, 1)
            down(U_DOWN2, KF, 3, 0.5)

            j = 0
            for h in range(2):
                for k in range(KD + PLE // P):
                    if U_PLE + j + SLOTS < UNITS:
                        ahead(U_PLE + j, j)
                    if h == 0:
                        entry(3, k)
                    if h == 0 and k == 10:
                        dve.wait_ge(p_hi, 1)
                        dve.tensor_tensor(pTl[:, :, :], ps[:, 5, :].rearrange("p (k s) -> p k s", s=S),
                                          pTh[:, :, :].bitcast(F32), ALU.subtract).then_inc(p_lo, 1)
                    j += 1
                dve.wait_ge(unit_done, U_PLE + j)
                for t in range(T):
                    dve.wait_ge(psig_ready, 2 * h + t + 1)
                    part = sgp[:, t, :]
                    dve.tensor_tensor(part, part, banks(4 + 2 * t, UNIT), ALU.mult).then_inc(psig_used, 1)
                    dve.wait_ge(psig_used, 2 * h + t + 1)
                    dst = res[:, t, h * UNIT:(h + 1) * UNIT]
                    dve.tensor_tensor(dst, dst, part, ALU.add).then_inc(res_ready, 1)


_INS = ['x', 'p', 'positions', 'g_ffn1', 'w1_gate', 'w1_up', 'w1_down', 'g_mix', 'w_in', 'g_cq', 'w_uq',
        'g_ckv', 'w_ukv', 'g_q_mla', 'g_k_mla', 'g_q_dil', 'g_k_dil', 'w_br_mla', 'w_br_dil', 'w_o', 'g_ffn2',
        'w2_gate', 'w2_up', 'w2_down', 'g_ple', 'w_ple_gate', 'w_ple_proj']


def constants(np, bf16):
    P, NEG, THETA = 128, -1e30, 500000.0
    q, k = np.arange(P)[:, None], np.arange(P)[None, :]
    causal = k <= q
    mla = np.concatenate([np.ones((P, P), bool), causal], axis=1)
    groups = ((128, 1), (512, 4), (2048, 16))

    def seen(qi, ki, win, dil):
        gap = qi - ki
        return (gap >= 0) & (gap % dil == 0) & (gap <= win)

    dil = np.concatenate([seen(q + P, np.arange(2 * P)[None, :], w, d) for w, d in groups], axis=1)
    freq = [THETA ** (-np.arange(rd // 2, dtype=np.float64) * 2.0 / rd) for rd in (64, 32)]
    return {
        "identity": np.eye(P, dtype=np.float32),
        "mla_masks": np.where(mla, 0.0, NEG).astype(bf16),
        "dil_masks": np.where(dil, 0.0, NEG).astype(bf16),
        "inverse_frequencies": np.concatenate(freq).astype(np.float32)[None, :],
    }


def kernel(**inputs):
    import ml_dtypes
    import numpy as np
    import concourse.bacc as bacc
    from concourse.bass_utils import run_bass_kernel_spmd

    nc = bacc.Bacc("TRN2", target_bir_lowering=False, num_devices=1)
    arrays = {name: np.ascontiguousarray(inputs[name]) for name in _INS}
    arrays.update(constants(np, ml_dtypes.bfloat16))
    aps = {name: nc.dram_tensor(f"in_{name}", a.shape, mybir.dt.from_np(a.dtype), kind="ExternalInput").ap()
           for name, a in arrays.items()}
    out = nc.dram_tensor("out_x", arrays["x"].shape, F32, kind="ExternalOutput").ap()
    hybrid_layer(nc, out, **aps)
    r = run_bass_kernel_spmd(nc, [{f"in_{name}": a for name, a in arrays.items()}], core_ids=[0])
    return r.results[0]["out_x"]
```

```python
from contextlib import ExitStack

import concourse.bass as bass
from concourse import mybir

ALU = mybir.AluOpType
ACT = mybir.ActivationFunctionType
AX_X = mybir.AxisListType.X
F32 = mybir.dt.float32
F32R = mybir.dt.float32r
BF16 = mybir.dt.bfloat16
I32 = mybir.dt.int32
ds = bass.ds

P = 128
BANK = 512
SLOTS = 4
UNIT = 1024
EPS = 1e-6
PRIMED = 1
ROUND = 1.5 * 2.0 ** 23
TWO_PI_1 = 6.28125
TWO_PI_2 = 0.0019340515136718750
TWO_PI_3 = 6.283185307179586 - TWO_PI_1 - TWO_PI_2
PI_DOWN = 3.1415925


class Chain:

    def __init__(self, eng, sem):
        self.eng, self.sem, self.n, self.past = eng, sem, 0, 0

    def __call__(self, ins):
        ins.then_inc(self.sem, 1)
        self.n += 1
        self.eng.wait_ge(self.sem, self.past + self.n)

    def enter(self, i, steps):
        self.past, self.first, self.steps = i * steps, self.n, steps

    def leave(self, turns):
        assert self.n - self.first == self.steps, (self.n - self.first, self.steps)
        self.past, self.n = 0, self.n + self.steps * (turns - 1)


def hybrid_layer(nc, out, x, p, positions, g_ffn1, w1_gate, w1_up, w1_down, g_mix, w_in, g_cq, w_uq,
                 g_ckv, w_ukv, g_q_mla, g_k_mla, g_q_dil, g_k_dil, w_br_mla, w_br_dil, w_o, g_ffn2,
                 w2_gate, w2_up, w2_down, g_ple, w_ple_gate, w_ple_proj, identity, mla_masks,
                 dil_masks, inverse_frequencies):
    _, S, D = x.shape
    FF = w1_gate.shape[2]
    PLE = p.shape[3]
    LQ, LKV = g_cq.shape[1], g_ckv.shape[1]
    QK = g_q_mla.shape[1]
    GROUPS, HD = g_q_dil.shape[1:]
    NOPE = HD
    ROPE = QK - NOPE
    H = w_br_dil.shape[1] // HD
    ROT = HD // 4
    LAT = LQ + LKV + ROPE
    OFF_GATE = LAT + GROUPS * 3 * H * HD
    NF = inverse_frequencies.shape[1]
    T, KD, KF = S // P, D // P, FF // P
    HQ, HK = H * QK // 2, H * (NOPE + HD) // 2
    assert T == 2 and D == 2 * UNIT and H * HD == UNIT and NF == ROPE // 2 + ROT // 2
    SCALE_MLA, SCALE_DIL = QK ** -0.5, HD ** -0.5
    NG = LQ // P + LKV // P

    FFN_TURNS, FFN_BODY = FF // BANK, 2 * KD // 2
    MERGE_TURNS, MERGE_BODY = D // BANK, 2 * (KD // 2 + H // 2)
    counts = [FFN_TURNS * FFN_BODY, 2 * KF, KD, KD, 2 * (LQ // P), 2 * (LKV // P),
              KD, 2 * GROUPS * KD, KD, MERGE_TURNS * MERGE_BODY, 2 * KD,
              FFN_TURNS * FFN_BODY, 2 * KF, 2 * (KD + PLE // P)]
    starts = [sum(counts[:n]) for n in range(len(counts))]
    (U_GU1, U_DOWN1, U_LAT, U_V0, U_UQ, U_UKV, U_V1, U_QK, U_V2, U_MERGE, U_WO, U_GU2, U_DOWN2, U_PLE) = starts
    UNITS = sum(counts)
    assert all(n % SLOTS == 0 for n in counts)

    with ExitStack() as ctx:
        def sem(name):
            return ctx.enter_context(nc.semaphore(name))

        def sb(name, shape, dt=F32):
            return ctx.enter_context(nc.sbuf_tensor(name, shape, dt))

        ps = ctx.enter_context(nc.psum_tensor("ps", [P, 8, BANK], F32))
        flat = ps[:, :, :].rearrange("p b c -> p (b c)")

        def banks(b, width):
            return flat[:, b * BANK:b * BANK + width]

        def quad(b):
            return banks(b, 4 * S).rearrange("p (c s) -> p c s", s=S)

        res = sb("res", [P, T, D])
        hTh = sb("hTh", [P, KD, S], F32R)
        hTl = sb("hTl", [P, KD, S], F32R)
        raw = sb("raw", [P, SLOTS, UNIT])
        wh = sb("wh", [P, SLOTS, UNIT], F32R)
        wl = sb("wl", [P, SLOTS, UNIT], F32R)
        ident = sb("ident", [P, P])
        ones = sb("ones", [P, P])
        inv_row = sb("inv_row", [P, S])
        gcol = sb("gcol", [P, 4 * KD + NG])
        gq_mla, gk_mla = sb("gq_mla", [P, QK]), sb("gk_mla", [P, QK])
        gq_dil, gk_dil = sb("gq_dil", [P, GROUPS, HD]), sb("gk_dil", [P, GROUPS, HD])
        m_mla = sb("m_mla", [P, 2 * P], BF16)
        m_dil = sb("m_dil", [P, GROUPS, 2 * P], BF16)
        sin, cos = sb("sin", [P, T, NF]), sb("cos", [P, T, NF])
        small = sb("small", [P, 256])

        base = nc.sbuf_base
        room = nc.sbuf_top - base

        def at(name, where, shape, dt=F32):
            size = 4
            for n in shape[1:]:
                size *= n
            assert where + size <= room, (name, where, size, room)
            return nc.alloc_sbuf_tensor_at(name, shape, dt, offset=base + where)

        KB = 1024
        aTh, aTl = at("aTh", 0, [P, KF, S], F32R), at("aTl", 44 * KB, [P, KF, S], F32R)
        sg, gs = at("sg", 88 * KB, [P, 4, S]), at("gs", 92 * KB, [P, 4, S])
        junk = at("junk", 88 * KB, [P, UNIT])
        diag = at("diag", 98 * KB, [P, T, P])
        grow_1, grow_rest = at("grow_1", 16 * KB, [KD, P]), at("grow_rest", 17 * KB, [3 * KD + NG, P])
        angle, turns, freq = (at(n, 96 * KB + 256 * j, [P, NF]) for j, n in enumerate(("angle", "turns", "freq")))
        pos_i, pos_f = at("pos_i", 96 * KB + 768, [P, T], I32), at("pos_f", 96 * KB + 800, [P, T])
        q_tok, kv_tok = at("q_tok", 0, [P, T, H * QK]), at("kv_tok", 16 * KB, [P, T, H * (NOPE + HD)])
        cTh, cTl = at("cTh", 32 * KB, [P, NG, S], F32R), at("cTl", 38 * KB, [P, NG, S], F32R)
        nT = at("nT", 32 * KB, [P, H, 2, S])
        rh = at("rh", 48 * KB, [P, T, 2, H, ROPE])
        rT = at("rT", 56 * KB, [P, 2, H // 2, S])
        sq = at("sq", 56 * KB, [P, H * QK])
        tmpA, tmpB = at("tmpA", 56 * KB, [P, 2 * H, ROPE // 2]), at("tmpB", 58 * KB, [P, 2 * H, ROPE // 2])
        c_tok = at("c_tok", 88 * KB, [P, T, LAT])
        prob_m, pT_m = at("prob_m", 88 * KB, [P, 2, 2 * P]), at("pT_m", 90 * KB, [P, 2 * P])
        omh, oml = at("omh", 0, [P, H, S], F32R), at("oml", 8 * KB, [P, H, S], F32R)
        qT, kT = at("qT", 16 * KB, [P, GROUPS, H * S]), at("kT", 40 * KB, [P, GROUPS, H * S])
        vd = at("vd", 64 * KB, [P, GROUPS, T * UNIT])
        tok = at("tok", 88 * KB, [P, T, UNIT])
        ropeA, ropeB = (at(n, 96 * KB + 512 * j, [P, H, ROT // 2]) for j, n in enumerate(("ropeA", "ropeB")))
        prob_d, pT_d = at("prob_d", 88 * KB, [P, 2, 6 * P]), at("pT_d", 94 * KB, [P, 6 * P])
        sg_first = at("sg_first", 97 * KB, [P, 4, S])
        odh, odl = at("odh", 16 * KB, [P, H, S], F32R), at("odl", 40 * KB, [P, H, S], F32R)
        mTh, mTl = at("mTh", 48 * KB, [P, KD, S], F32R), at("mTl", 64 * KB, [P, KD, S], F32R)
        am = at("am", 80 * KB, [P, 4, S])
        sgp = at("sgp", 0, [P, T, UNIT])
        p_tok = at("p_tok", 16 * KB, [P, T, PLE])
        pTh, pTl = at("pTh", 18 * KB, [P, PLE // P, S], F32R), at("pTl", 20 * KB, [P, PLE // P, S], F32R)

        raw_in = [sem(f"raw_in{j}") for j in range(SLOTS)]
        hi_ready, lo_ready = sem("hi_ready"), sem("lo_ready")
        unit_done = sem("unit_done")
        x_in = [sem(f"x_in{j}") for j in range(4)]
        ident_in, row1_in, rows_in, consts_in, gains_in, p_in = (
            sem(n) for n in ("ident_in", "row1_in", "rows_in", "consts_in", "gains_in", "p_in"))
        ones_ready, gains_turned, gcol_ready, angles_ready, tables_ready = (
            sem(n) for n in ("ones_ready", "gains_turned", "gcol_ready", "angles_ready", "tables_ready"))
        ss_ready, var_ready, dev_ready, inv_ready = (sem(n) for n in ("ss_ready", "var_ready", "dev_ready", "inv_ready"))
        diag_ready, row_turned, row_ready = (sem(n) for n in ("diag_ready", "row_turned", "row_ready"))
        turned, tr_hi, tr_lo = sem("turned"), sem("tr_hi"), sem("tr_lo")
        gi_ready, sig_ready, gs_ready, am_ready, ah_ready, a_ready = (
            sem(n) for n in ("gi_ready", "sig_ready", "gs_ready", "am_ready", "ah_ready", "a_ready"))
        res_ready = sem("res_ready")
        lat_tok, lat_ss, lat_var, lat_dev, lat_ready = (
            sem(n) for n in ("lat_tok", "lat_ss", "lat_var", "lat_dev", "lat_ready"))
        uq_tok, ukv_tok = sem("uq_tok"), sem("ukv_tok")
        mla_sq, mla_ss, mla_var, mla_dev, mla_inv, mla_scaled, mla_ready, mla_turned, rT_ready, nT_even, nT_odd = (
            sem(n) for n in ("mla_sq", "mla_ss", "mla_var", "mla_dev", "mla_inv", "mla_scaled", "mla_ready",
                             "mla_turned", "rT_ready", "nT_even", "nT_odd"))
        dil_tok, dil_sq, dil_ss, dil_var, dil_dev, dil_ready, dil_turned, dil_T, dil_v = (
            sem(n) for n in ("dil_tok", "dil_sq", "dil_ss", "dil_var", "dil_dev", "dil_ready", "dil_turned",
                             "dil_T", "dil_v"))
        score_done, masked, exp_done, prob_ready, prob_turned, pT_ready, pv_done, o_hi, o_lo = (
            sem(n) for n in ("score_done", "masked", "exp_done", "prob_ready", "prob_turned", "pT_ready",
                             "pv_done", "o_hi", "o_lo"))
        mgi_ready, msig_ready, mprod_ready, m_sum, mh_ready, m_ready = (
            sem(n) for n in ("mgi_ready", "msig_ready", "mprod_ready", "m_sum", "mh_ready", "m_ready"))
        p_turned, p_hi, p_lo, psig_ready, psig_used, out_done = (
            sem(n) for n in ("p_turned", "p_hi", "p_lo", "psig_ready", "psig_used", "out_done"))
        dve_step = sem("dve_step")

        ssq = small[:, 0:4]
        var, dev, inv, nwt = (small[:, 4 + 2 * j:6 + 2 * j] for j in range(4))
        css, cvar, cdev, cinv, cnwt = (small[:, 12 + 4 * j:16 + 4 * j] for j in range(5))
        mss, mvar, mdev, minv, mnwt = (small[:, 32 + 32 * j:64 + 32 * j] for j in range(5))
        dss, dvar, ddev, dinv, dnwt = (small[:, 32 + 32 * j:48 + 32 * j] for j in range(5))
        s_max, s_bias, s_sum, s_inv = (small[:, 192 + 16 * j:208 + 16 * j] for j in range(4))
        kss_m = small[:, 10:12]

        items = [(h, t) for h in range(H) for t in range(T)]

        PAIRS = [r * KD // 2 + (NG // 2 if r >= 2 else 0) for r in range(4)]
        C_PAIRS = PAIRS[1] + KD // 2

        block = ctx.enter_context(nc.Block())

        @block.sync
        def _(sp):
            def wide(n, j, w, k, c0, width=UNIT):
                sp.wait_ge(lo_ready, n - (SLOTS - 1))
                sp.dma_start(raw[:, j % SLOTS, 0:width], w[0, k * P:(k + 1) * P, ds(c0, width)])\
                  .then_inc(raw_in[j % SLOTS], 16)

            def square(n, j, w, k, c0, waits=1):
                if waits and not (isinstance(n, int) and n < SLOTS):
                    sp.wait_ge(lo_ready, n + waits - SLOTS)
                sp.dma_start(raw[:, j % SLOTS, :].rearrange("p (k c) -> p k c", k=2),
                             w[0, k * P:(k + 2) * P, ds(c0, BANK)].rearrange("(k p) c -> p k c", p=P))\
                  .then_inc(raw_in[j % SLOTS], 16)

            def load_x(quarter):
                c0, c1 = quarter * BANK, (quarter + 1) * BANK
                sp.dma_start(res[:, :, c0:c1], x[0, :, c0:c1].rearrange("(t p) c -> p t c", p=P))\
                  .then_inc(x_in[quarter], 16)

            def gate_up(u0, w_gate, w_up, i):
                for j in range(KD // 2):
                    if i is None and j in (2, 3):
                        load_x(j)
                    square(u0 + (i or 0) * FFN_BODY + j if i is None else u0 + i * FFN_BODY + j, j, w_gate, 2 * j,
                           0 if i is None else i * BANK)
                for j in range(KD // 2):
                    n = KD // 2 + j
                    square(u0 + n if i is None else u0 + i * FFN_BODY + n, n, w_up, 2 * j, 0 if i is None else i * BANK)

            def projection(u0, c0):
                for k in range(KD):
                    wide(u0 + k, k, w_in, k, c0)

            Q_COLS, K_COLS, V_COLS = (LAT + a * UNIT for a in range(3))
            sp.dma_start(ident[:, :], identity).then_inc(ident_in, 16)
            sp.dma_start(grow_1[:, :], g_ffn1[0].rearrange("(k p) -> k p", p=P)).then_inc(row1_in, 16)
            load_x(0)
            load_x(1)
            gate_up(U_GU1, w1_gate, w1_up, None)
            with sp.Fori(1, FFN_TURNS) as i:
                gate_up(U_GU1, w1_gate, w1_up, i)
            with sp.Fori(0, 2) as i:
                for k in range(KF):
                    wide(U_DOWN1 + i * KF + k, k, w1_down, k, i * UNIT)
            for k in range(KD):
                wide(U_LAT + k, k, w_in, k, 0, LAT)
            projection(U_V0, V_COLS)
            for h in range(2):
                for k in range(LQ // P):
                    wide(U_UQ + h * (LQ // P) + k, k, w_uq, k, h * HQ, HQ)
            for h in range(2):
                for k in range(LKV // P):
                    wide(U_UKV + h * (LKV // P) + k, h * (LKV // P) + k, w_ukv, k, h * HK, HK)
            projection(U_V1, V_COLS + 3 * UNIT)
            projection(U_QK, Q_COLS)
            with sp.Fori(0, GROUPS - 1) as g:
                projection(U_QK + KD + g * (2 * KD), K_COLS + g * (3 * UNIT))
                projection(U_QK + 2 * KD + g * (2 * KD), Q_COLS + 3 * UNIT + g * (3 * UNIT))
            projection(U_QK + (2 * GROUPS - 1) * KD, K_COLS + (GROUPS - 1) * 3 * UNIT)
            projection(U_V2, V_COLS + (GROUPS - 1) * 3 * UNIT)
            j = 0
            for w, c0, K in ((w_in, OFF_GATE, KD), (w_in, OFF_GATE + D, KD), (w_br_mla, 0, H), (w_br_dil, 0, H)):
                for k in range(0, K, 2):
                    square(U_MERGE + j, j, w, k, c0)
                    j += 1
            with sp.Fori(1, MERGE_TURNS) as i:
                j = 0
                for w, c0, K in ((w_in, OFF_GATE, KD), (w_br_mla, 0, H), (w_in, OFF_GATE + D, KD), (w_br_dil, 0, H)):
                    for k in range(0, K, 2):
                        waits = 2 if j == KD // 2 - 1 else 0 if j == KD // 2 else 1
                        square(U_MERGE + i * MERGE_BODY + j, j, w, k, c0 + i * BANK, waits)
                        j += 1
            with sp.Fori(0, 2) as i:
                for k in range(KD):
                    wide(U_WO + i * KD + k, k, w_o, k, i * UNIT)
            with sp.Fori(0, FFN_TURNS) as i:
                gate_up(U_GU2, w2_gate, w2_up, i)
            with sp.Fori(0, 2) as i:
                for k in range(KF):
                    wide(U_DOWN2 + i * KF + k, k, w2_down, k, i * UNIT)
            j = 0
            for h in range(2):
                for k in range(KD):
                    wide(U_PLE + j, j, w_ple_gate, k, h * UNIT)
                    j += 1
                for k in range(PLE // P):
                    wide(U_PLE + j, j, w_ple_proj, k, h * UNIT)
                    j += 1
            for h in range(2):
                for t in range(T):
                    sp.wait_ge(res_ready, PRIMED + 12 + 2 * h + t + 1)
                    sp.dma_start(out[0, t * P:(t + 1) * P, h * UNIT:(h + 1) * UNIT],
                                 res[:, t, h * UNIT:(h + 1) * UNIT]).then_inc(out_done, 16)
            sp.wait_ge(out_done, 4 * 16)

        @block.gpsimd
        def _(pool):
            for s in (gs_ready, am_ready, a_ready, res_ready, dil_turned, dil_T, dil_ready, gi_ready):
                pool.sem_inc(s, PRIMED)
            pool.memset(ones[:, :], 1.0).then_inc(ones_ready, 1)

        @block.tensor
        def _(pe):
            def wide_unit(n, j, k, hi, lo, b0, width, K):
                pe.wait_ge(lo_ready, n + 1)
                s = j % SLOTS
                cols = [(c, min(width, c + BANK)) for c in range(0, width, BANK)]
                for t in range(T):
                    xh, xl = hi[:, k, t * P:(t + 1) * P], lo[:, k, t * P:(t + 1) * P]
                    for a, w, first, last in ((xh, wh, k == 0, False), (xh, wl, False, False), (xl, wh, False, k == K - 1)):
                        for m, (c, e) in enumerate(cols):
                            mm = pe.matmul(ps[:, b0 + 2 * t + m, 0:e - c], a, w[:, s, c:e], start=first, stop=last)
                mm.then_inc(unit_done, 1)

            def square_unit(n, j, k, hi, lo, b0, K):
                pe.wait_ge(lo_ready, n + 1)
                s = j % SLOTS
                for kk in range(2):
                    for c in range(4):
                        w0 = kk * BANK + c * P
                        o, end = ps[:, b0 + c // 2, (c % 2) * S:(c % 2 + 1) * S], k + kk == K - 1
                        pe.matmul(o, wh[:, s, w0:w0 + P], hi[:, k + kk, :], start=(k + kk == 0 and c % 2 == 0),
                                  stop=False, skip_group_check=True)
                        pe.matmul(o, wh[:, s, w0:w0 + P], lo[:, k + kk, :], start=False, stop=False,
                                  skip_group_check=True)
                        mm = pe.matmul(o, wl[:, s, w0:w0 + P], hi[:, k + kk, :], start=False, stop=end,
                                       skip_group_check=True)
                mm.then_inc(unit_done, 1)

            def turn(src, pairs, b0):
                for n, p in enumerate(pairs):
                    for s in range(2):
                        for t in range(T):
                            mm = pe.transpose(ps[:, b0 + n, s * S + t * P:s * S + (t + 1) * P],
                                              src[:, t, (2 * p + s) * P:(2 * p + s + 1) * P], ident[:, :])
                    mm.then_inc(turned, 1)

            LEFT, RIGHT = range(KD // 4), range(KD // 4, KD // 2)

            def entry(r, j):
                if j == 0:
                    pe.wait_ge(tr_lo, 2 * PAIRS[r] + KD // 2)
                if j == 2:
                    if r == 0:
                        pe.wait_ge(x_in[2], 16)
                        pe.wait_ge(x_in[3], 16)
                        pe.wait_ge(tr_lo, KD // 2)
                    else:
                        pe.wait_ge(res_ready, PRIMED + 4 * r)
                    turn(res, RIGHT, 4)
                if j == 6:
                    pe.wait_ge(diag_ready, r + 1)
                    pe.wait_ge(tr_lo, 2 * PAIRS[r] + KD // 2 + 2)
                    pe.wait_ge(ones_ready, 1)
                    pe.matmul(ps[:, 4, 0:S], ones[:, :], diag[:, :, :].rearrange("p t c -> p (t c)"),
                              start=True, stop=True).then_inc(row_turned, 1)

            def gate_up(u0, f):
                r = 2 * f
                for j in range(KD // 2):
                    entry(r, j)
                    pe.wait_ge(tr_lo, 2 * PAIRS[r] + 2 * j + 2)
                    square_unit(u0 + j, j, 2 * j, hTh, hTl, 0, KD)
                pe.wait_ge(row_ready, r + 1)
                for j in range(KD // 2):
                    square_unit(u0 + KD // 2 + j, j, 2 * j, hTh, hTl, 4, KD)
                with pe.Fori(1, FFN_TURNS) as i:
                    pe.wait_ge(gi_ready, PRIMED + f * FFN_TURNS + i)
                    for j in range(KD // 2):
                        square_unit(u0 + i * FFN_BODY + j, j, 2 * j, hTh, hTl, 0, KD)
                    pe.wait_ge(am_ready, PRIMED + f * FFN_TURNS + i)
                    for j in range(KD // 2):
                        square_unit(u0 + i * FFN_BODY + KD // 2 + j, j, 2 * j, hTh, hTl, 4, KD)

            def down(u0, hi, lo, K, r, ready, before, after):
                pe.wait_ge(ready, PRIMED + before)
                for half in range(2):
                    for k in range(K):
                        if half == 0 and k == K - 4:
                            pe.wait_ge(ready, PRIMED + after)
                        if half == 1 and k == 6:
                            pe.wait_ge(res_ready, PRIMED + 4 * (r - 1) + 2)
                            turn(res, LEFT, 0)
                        wide_unit(u0 + half * K + k, k, k, hi, lo, 4 * half, UNIT, K)

            def attention(first, scores, values, n_keys, prob, pT, score_bank, turned_bank, out_bank, begun, between):
                def score(u):
                    h, t = items[u]
                    if u:
                        pe.wait_ge(masked, first + u)
                    for c, keys, parts in scores(h, t):
                        for m, (q, k) in enumerate(parts):
                            mm = pe.matmul(flat[:, score_bank * BANK + c:score_bank * BANK + c + keys], q, k,
                                           start=(m == 0), stop=(m == len(parts) - 1))
                    mm.then_inc(score_done, 1)

                def output(u):
                    h, t = items[u]
                    n = n_keys * (t + 1)
                    pe.wait_ge(pT_ready, first + u + 1)
                    if u >= 2:
                        pe.wait_ge(o_lo, first + u - 1)
                    for m in range(n):
                        mm = pe.matmul(ps[:, out_bank + u % 2, 0:P], values(h, t, m), pT[:, m * P:(m + 1) * P],
                                       start=(m == 0), stop=(m == n - 1))
                    mm.then_inc(pv_done, 1)

                score(0)
                begun()
                for u, (h, t) in enumerate(items):
                    if u + 1 < len(items):
                        score(u + 1)
                    pe.wait_ge(prob_ready, first + u + 1)
                    if u:
                        pe.wait_ge(pT_ready, first + u)
                    for m in range(n_keys * (t + 1)):
                        mm = pe.transpose(flat[:, turned_bank * BANK + m * P:turned_bank * BANK + (m + 1) * P],
                                          prob[:, u % 2, m * P:(m + 1) * P], ident[:, :])
                    mm.then_inc(prob_turned, 1)
                    if u:
                        output(u - 1)
                    between(u)
                output(len(items) - 1)

            pe.wait_ge(ident_in, 16)
            pe.wait_ge(row1_in, 16)
            pe.transpose(ps[:, 2, 0:KD], grow_1[:, :], ident[0:KD, 0:KD]).then_inc(gains_turned, 1)
            for quarter in range(2):
                pe.wait_ge(x_in[quarter], 16)
                turn(res, LEFT[2 * quarter:2 * quarter + 2], 4 + 2 * quarter)
            pe.wait_ge(rows_in, 16 * 5)
            pe.transpose(ps[:, 3, 0:3 * KD + NG], grow_rest[:, :], ident[0:3 * KD + NG, 0:3 * KD + NG])\
              .then_inc(gains_turned, 1)

            gate_up(U_GU1, 0)
            down(U_DOWN1, aTh, aTl, KF, 1, a_ready, FFN_TURNS - 1, FFN_TURNS)

            for k in range(KD):
                entry(1, k)
                if k % 2 == 0:
                    pe.wait_ge(tr_lo, 2 * PAIRS[1] + k + 2)
                wide_unit(U_LAT + k, k, k, hTh, hTl, 0, LAT, KD)
            for k in range(KD):
                if k == 0:
                    pe.wait_ge(tr_lo, 2 * PAIRS[1] + KD)
                    pe.wait_ge(row_ready, 2)
                if k == 4:
                    pe.wait_ge(lat_ready, 1)
                    turn(c_tok, range(NG // 2), 0)
                wide_unit(U_V0 + k, k, k, hTh, hTl, 4, UNIT, KD)
            pe.wait_ge(tr_lo, 2 * C_PAIRS + NG)
            for h in range(2):
                if h:
                    pe.wait_ge(dil_v, 2)
                for k in range(LQ // P):
                    wide_unit(U_UQ + h * (LQ // P) + k, k, k, cTh, cTl, 4 * h, HQ, LQ // P)
            ch, cl = cTh[:, LQ // P:NG, :], cTl[:, LQ // P:NG, :]
            for h in range(2):
                pe.wait_ge(uq_tok, 2 * h + 2)
                for k in range(LKV // P):
                    wide_unit(U_UKV + h * (LKV // P) + k, h * (LKV // P) + k, k, ch, cl, 4 * h, HK, LKV // P)
            def turn_heads(heads):
                for h in heads:
                    b, c0 = (h + 4) % 8, h * (NOPE + HD)
                    for t in range(T):
                        pe.transpose(ps[:, b, t * P:(t + 1) * P], q_tok[:, t, h * QK:h * QK + NOPE], ident[:, :])
                    for t in range(T):
                        mm = pe.transpose(ps[:, b, S + t * P:S + (t + 1) * P], kv_tok[:, t, c0:c0 + NOPE], ident[:, :])
                    mm.then_inc(mla_turned, 1)

            pe.wait_ge(ukv_tok, 2)
            for k in range(KD):
                if k == 13:
                    pe.wait_ge(ukv_tok, 4)
                    pe.wait_ge(mla_ready, 2)
                    for a in range(2):
                        for h2 in range(H // 2):
                            for t in range(T):
                                c0 = (h2 % 2) * S + t * P
                                mm = pe.transpose(ps[:, 4 + 2 * a + h2 // 2, c0:c0 + P],
                                                  rh[:, t, a, 2 * h2:2 * h2 + 2, :].rearrange("p h c -> p (h c)"),
                                                  ident[:, :])
                        mm.then_inc(mla_turned, 1)
                if k == 15:
                    pe.wait_ge(rT_ready, 2)
                    turn_heads(range(H // 2))
                wide_unit(U_V1 + k, k, k, hTh, hTl, 0, UNIT, KD)


            def mla_scores(h, t):
                q0, r0 = t * P, (h % 2) * ROPE
                keys = (t + 1) * P
                if t == 0:
                    pe.wait_ge((nT_even, nT_odd)[h % 2], h // 2 + 1)
                yield 0, keys, [(nT[:, h, 0, q0:q0 + P], nT[:, h, 1, 0:keys]),
                                (rT[r0:r0 + ROPE, 0, h // 2, q0:q0 + P], rT[r0:r0 + ROPE, 1, h // 2, 0:keys])]

            def mla_values(h, t, m):
                c0 = h * (NOPE + HD) + NOPE
                return kv_tok[:, m, c0:c0 + HD]

            def other_heads():
                pe.wait_ge(dil_v, 4)
                turn_heads(range(H // 2, H))

            def first_q(u):
                if u == 0:
                    pe.wait_ge(nT_even, H // 2)
                    pe.wait_ge(nT_odd, H // 2)
                wide_unit(U_QK + u, u, u, hTh, hTl, 0, UNIT, KD)

            assert len(items) == KD
            attention(0, mla_scores, mla_values, 1, prob_m, pT_m, 4, 5, 6, other_heads, first_q)

            def qk_pass(s, a, u0):
                for k in range(KD):
                    if k == 11:
                        pe.wait_ge(dil_ready, PRIMED + 2 * s)
                        for h in range(H):
                            for t in range(T):
                                c0 = (4 - 4 * a) * BANK + h * S + t * P
                                mm = pe.transpose(flat[:, c0:c0 + P], tok[:, t, h * HD:(h + 1) * HD], ident[:, :])
                        mm.then_inc(dil_turned, 1)
                    wide_unit(u0 + k, k, k, hTh, hTl, 4 * a, UNIT, KD)

            pe.wait_ge(o_lo, len(items))
            with pe.Fori(0, GROUPS - 1) as g:
                pe.wait_ge(dil_T, PRIMED + 4 * g)
                qk_pass(2 * g + 1, 1, U_QK + KD + g * (2 * KD))
                pe.wait_ge(dil_T, PRIMED + 4 * g + 2)
                qk_pass(2 * g + 2, 0, U_QK + 2 * KD + g * (2 * KD))
            last = 2 * GROUPS - 1
            pe.wait_ge(dil_T, PRIMED + 2 * last - 2)
            qk_pass(last, 1, U_QK + last * KD)
            pe.wait_ge(dil_T, PRIMED + 2 * last)
            qk_pass(last + 1, 0, U_V2)

            def dil_scores(h, t):
                keys = (t + 1) * P
                for g in range(GROUPS):
                    q0, k0 = h * S + t * P, h * S
                    yield g * keys, keys, [(qT[:, g, q0:q0 + P], kT[:, g, k0:k0 + keys])]

            def dil_values(h, t, m):
                g, tk = m // (t + 1), m % (t + 1)
                return vd[:, g, tk * UNIT + h * HD:tk * UNIT + (h + 1) * HD]

            pe.wait_ge(dil_T, PRIMED + 4 * GROUPS)

            def last_v():
                pe.wait_ge(dil_v, 6)

            def first_gates(u):
                if u == KD // 2:
                    pe.wait_ge(mgi_ready, 1)
                square_unit(U_MERGE + u, u, 2 * (u % (KD // 2)), hTh, hTl, 2, KD)

            attention(len(items), dil_scores, dil_values, GROUPS, prob_d, pT_d, 4, 6, 0, last_v, first_gates)

            j = KD
            pe.wait_ge(masked, 2 * len(items))
            pe.wait_ge(pT_ready, 2 * len(items))
            for part, (hi, lo) in enumerate(((omh, oml), (odh, odl))):
                if part:
                    pe.wait_ge(o_lo, 2 * len(items))
                for k in range(0, H, 2):
                    square_unit(U_MERGE + j, j, k, hi, lo, 4 + 2 * part, H)
                    j += 1
            with pe.Fori(1, MERGE_TURNS) as i:
                j = 0
                for part, (hi, lo, K, b0) in enumerate(((hTh, hTl, KD, 2), (omh, oml, H, 4),
                                                        (hTh, hTl, KD, 0), (odh, odl, H, 6))):
                    if part == 0:
                        pe.wait_ge(mgi_ready, 2 * i)
                    if part == 1:
                        pe.wait_ge(mprod_ready, 2 * i - 1)
                    if part == 3:
                        pe.wait_ge(mprod_ready, 2 * i)
                    for k in range(0, K, 2):
                        square_unit(U_MERGE + i * MERGE_BODY + j, j, k, hi, lo, b0, K)
                        j += 1
            pe.wait_ge(mgi_ready, 2 * MERGE_TURNS)
            down(U_WO, mTh, mTl, KD, 2, m_ready, MERGE_TURNS - 1 - PRIMED, MERGE_TURNS - PRIMED)

            gate_up(U_GU2, 1)
            down(U_DOWN2, aTh, aTl, KF, 3, a_ready, 2 * FFN_TURNS - 1, 2 * FFN_TURNS)

            j = 0
            for h in range(2):
                if h:
                    pe.wait_ge(psig_ready, 2)
                for k in range(KD):
                    if h == 0:
                        entry(3, k)
                        if k % 2 == 0:
                            pe.wait_ge(tr_lo, 2 * PAIRS[3] + k + 2)
                        if k == 10:
                            pe.wait_ge(p_in, 16)
                            pe.wait_ge(tr_lo, 2 * PAIRS[3] + KD)
                            for t in range(T):
                                for c in range(PLE // P):
                                    mm = pe.transpose(ps[:, 5, c * S + t * P:c * S + (t + 1) * P],
                                                      p_tok[:, t, c * P:(c + 1) * P], ident[:, :])
                            mm.then_inc(p_turned, 1)
                    wide_unit(U_PLE + j, j, k, hTh, hTl, 0, UNIT, KD)
                    j += 1
                if h == 0:
                    pe.wait_ge(p_lo, 1)
                    pe.wait_ge(row_ready, 4)
                else:
                    pe.wait_ge(psig_used, 2)
                for k in range(PLE // P):
                    wide_unit(U_PLE + j, j, k, pTh, pTl, 4, UNIT, PLE // P)
                    j += 1

        @block.scalar
        def _(act):
            r0 = 0
            for g in (g_mix, g_ffn2, g_ple, g_cq, g_ckv):
                n = g.shape[1] // P
                act.dma_start(grow_rest[r0:r0 + n, :], g[0].rearrange("(k p) -> k p", p=P)).then_inc(rows_in, 16)
                r0 += n

            def later_loads():
                act.dma_start(freq[:, :], inverse_frequencies[0].partition_broadcast(P)).then_inc(consts_in, 16)
                with nc.allow_non_contiguous_dma(reason="256 positions"):
                    act.dma_start(pos_i[:, :], positions[0].rearrange("(t p) -> p t", p=P)).then_inc(consts_in, 16)
                for dst, src in ((gq_mla, g_q_mla[0]), (gk_mla, g_k_mla[0])):
                    act.dma_start(dst[:, :], src.partition_broadcast(P)).then_inc(gains_in, 16)
                for dst, src in ((gq_dil, g_q_dil[0]), (gk_dil, g_k_dil[0])):
                    act.dma_start(dst[:, :, :], src.partition_broadcast(P)).then_inc(gains_in, 16)
                act.dma_start(m_mla[:, :], mla_masks).then_inc(gains_in, 16)
                act.dma_start(m_dil[:, :, :], dil_masks.rearrange("p (g c) -> p g c", g=GROUPS)).then_inc(gains_in, 16)

            def split(n, j):
                first = isinstance(n, int) and n < SLOTS
                act.wait_ge(raw_in[j % SLOTS], ((n - j % SLOTS) * (16 // SLOTS) + 16) if not isinstance(n, int)
                            else 16 * (n // SLOTS + 1))
                if not first:
                    act.wait_ge(unit_done, n - (SLOTS - 1))
                act.activation(wh[:, j % SLOTS, :], raw[:, j % SLOTS, :], ACT.Copy).then_inc(hi_ready, 1)

            def ahead(n, j):
                split(n + SLOTS, j)

            def root(src, dst, ready, count, done):
                act.wait_ge(ready, count)
                act.activation(dst, src, ACT.Sqrt).then_inc(done, 1)

            def high(dst, g0, before, pairs, b0):
                for n, p in enumerate(pairs):
                    act.wait_ge(turned, before + p + 1)
                    for s in range(2):
                        k = 2 * p + s
                        act.activation(dst[:, k, :], ps[:, b0 + n, s * S:(s + 1) * S], ACT.Copy,
                                       scale=gcol[:, g0 + k:g0 + k + 1]).then_inc(tr_hi, 1)

            LEFT, RIGHT = range(KD // 4), range(KD // 4, KD // 2)

            def squares(r, half):
                for t in range(T):
                    if r == 0:
                        act.wait_ge(x_in[2 * half + 1], 16)
                        act.wait_ge(x_in[2 * half], 16)
                    else:
                        act.wait_ge(res_ready, PRIMED + 4 * (r - 1) + 2 * half + t + 1)
                    if 4 * r + 2 * half + t:
                        act.wait_ge(ss_ready, 4 * r + 2 * half + t)
                    c = 2 * half + t
                    act.activation(junk[:, :], res[:, t, half * UNIT:(half + 1) * UNIT], ACT.Square,
                                   accum_out=ssq[:, c:c + 1]).then_inc(ss_ready, 1)

            def entry(r, j):
                if j == 0:
                    squares(r, 1)
                if j == 1:
                    high(hTh, r * KD, PAIRS[r], RIGHT, 4)
                if j == 2:
                    root(var, dev, var_ready, r + 1, dev_ready)

            def gate_up(u0, f):
                def turn(i, j):
                    if j == KD // 2 - 1:
                        act.wait_ge(gi_ready, PRIMED + f * FFN_TURNS + i + 1)
                        act.activation(sg[:, :, :], gs[:, :, :], ACT.Sigmoid).then_inc(sig_ready, 1)
                    if j == FFN_BODY - 1:
                        act.wait_ge(am_ready, PRIMED + f * FFN_TURNS + i + 1)
                        act.activation(aTh[:, ds(i * 4, 4), :], gs[:, :, :], ACT.Copy).then_inc(ah_ready, 1)

                for j in range(FFN_BODY):
                    ahead(u0 + j, j)
                    entry(2 * f, j)
                    turn(0, j)
                with act.Fori(1, FFN_TURNS) as i:
                    for j in range(FFN_BODY):
                        ahead(u0 + i * FFN_BODY + j, j)
                        turn(i, j)

            def down(u0, K, r, meanwhile=None):
                for half in range(2):
                    for k in range(K):
                        ahead(u0 + half * K + k, k)
                        if half == 0 and meanwhile:
                            meanwhile(k)
                        if half == 1 and k == 5:
                            squares(r, 0)
                        if half == 1 and k in (6, 8, 10, 12):
                            high(hTh, r * KD, PAIRS[r], LEFT[k // 2 - 3:k // 2 - 2], k // 2 - 3)

            def v_tile(g, b0):
                act.activation(vd[:, g, 0:UNIT], banks(b0, UNIT), ACT.Copy, scale=inv[:, 0:1]).then_inc(dil_v, 1)

            def attention(first, prob, pT, oh, n_keys, scale, turned_bank, out_bank, begun, between):
                def exp(u):
                    h, t = items[u]
                    n = n_keys * (t + 1) * P
                    act.wait_ge(masked, first + u + 1)
                    act.activation(prob[:, u % 2, 0:n], prob[:, u % 2, 0:n], ACT.Exp, bias=s_bias[:, u:u + 1],
                                   scale=scale, accum_out=s_sum[:, u:u + 1]).then_inc(exp_done, 1)

                def out_high(u):
                    h, t = items[u]
                    act.wait_ge(pv_done, first + u + 1)
                    act.activation(oh[:, h, t * P:(t + 1) * P], ps[:, out_bank + u % 2, 0:P], ACT.Copy)\
                       .then_inc(o_hi, 1)

                exp(0)
                begun()
                for u, (h, t) in enumerate(items):
                    if u:
                        between(u - 1)
                    n = n_keys * (t + 1) * P
                    act.wait_ge(prob_turned, first + u + 1)
                    if u:
                        act.wait_ge(pv_done, first + u)
                    act.activation(pT[:, 0:n], banks(turned_bank, n), ACT.Copy).then_inc(pT_ready, 1)
                    if u + 1 < len(items):
                        exp(u + 1)
                    if u:
                        out_high(u - 1)
                between(len(items) - 1)
                out_high(len(items) - 1)

            act.wait_ge(gains_turned, 1)
            act.activation(gcol[:, 0:KD], ps[:, 2, 0:KD], ACT.Copy).then_inc(gcol_ready, 1)
            act.wait_ge(gcol_ready, 1)
            for n in range(SLOTS):
                high(hTh, 0, PAIRS[0], LEFT[n:n + 1], 4 + n)
                split(n, n)
            act.wait_ge(gains_turned, 2)
            act.activation(gcol[:, KD:], ps[:, 3, 0:3 * KD + NG], ACT.Copy).then_inc(gcol_ready, 1)
            squares(0, 0)
            later_loads()
            gate_up(U_GU1, 0)
            def tables(k):
                if k in (2, 4, 6, 8):
                    n = k // 2 - 1
                    act.wait_ge(angles_ready, n + 1)
                    act.activation((sin, cos)[n % 2][:, n // 2, :], turns[:, :], ACT.Sin).then_inc(tables_ready, 1)

            down(U_DOWN1, KF, 1, tables)

            for k in range(KD):
                ahead(U_LAT + k, k)
                entry(1, k)
            act.wait_ge(inv_ready, 2)
            for t in range(T):
                act.activation(c_tok[:, t, :], banks(2 * t, LAT), ACT.Copy, scale=inv[:, t:t + 1]).then_inc(lat_tok, 1)
            act.wait_ge(lat_tok, T)
            for t in range(T):
                for a, (c0, c1) in enumerate(((0, LQ), (LQ, LQ + LKV), (LQ + LKV, LAT))):
                    total = css[:, 2 * t + a:2 * t + a + 1] if a < 2 else kss_m[:, t:t + 1]
                    src = flat[:, 2 * t * BANK + c0:2 * t * BANK + c1]
                    act.activation(src, c_tok[:, t, c0:c1], ACT.Square, accum_out=total).then_inc(lat_ss, 1)
            for k in range(KD):
                ahead(U_V0 + k, k)
                if k == 1:
                    root(cvar, cdev, lat_var, 2, lat_dev)
                if k == 4:
                    high(cTh, 4 * KD, C_PAIRS, range(NG // 2), 0)
            v_tile(0, 4)
            for h in range(2):
                for k in range(LQ // P):
                    ahead(U_UQ + h * (LQ // P) + k, k)
                for t in range(T):
                    act.activation(q_tok[:, t, h * HQ:(h + 1) * HQ], banks(4 * h + 2 * t, HQ), ACT.Copy).then_inc(uq_tok, 1)
            for h in range(2):
                for k in range(LKV // P):
                    ahead(U_UKV + h * (LKV // P) + k, h * (LKV // P) + k)
                for t in range(T):
                    act.activation(kv_tok[:, t, h * HK:(h + 1) * HK], banks(4 * h + 2 * t, HK), ACT.Copy)\
                       .then_inc(ukv_tok, 1)
            act.wait_ge(uq_tok, 4)
            act.wait_ge(ukv_tok, 4)
            for k in range(KD):
                ahead(U_V1 + k, k)
                if k in (0, 1):
                    if k:
                        act.wait_ge(mla_ss, k)
                    act.activation(sq[:, :], q_tok[:, k, :], ACT.Square).then_inc(mla_sq, 1)
                if k in (2, 3):
                    act.wait_ge(mla_ss, k)
                    act.activation(sq[:, 0:H * NOPE].rearrange("p (h c) -> p h c", h=H),
                                   kv_tok[:, k - 2, :].rearrange("p (h c) -> p h c", h=H)[:, :, 0:NOPE],
                                   ACT.Square).then_inc(mla_sq, 1)
                if k == 4:
                    root(mvar, mdev, mla_var, 1, mla_dev)
                if k in (5, 6, 7, 8):
                    if k == 5:
                        act.wait_ge(mla_inv, 1)
                    t, a = (k - 5) // 2, (k - 5) % 2
                    for h in range(H):
                        c = (a * T + t) * H + h
                        v = kv_tok[:, t, h * (NOPE + HD):h * (NOPE + HD) + NOPE] if a else q_tok[:, t, h * QK:(h + 1) * QK]
                        last = act.activation(v, v, ACT.Copy, scale=minv[:, c:c + 1])
                    last.then_inc(mla_scaled, 1)

            def even_heads(heads):
                for h in heads:
                    act.wait_ge(mla_turned, 2 + h + 1)
                    act.activation(nT[:, h, :, :], ps[:, (h + 4) % 8, :].rearrange("p (a s) -> p a s", a=2), ACT.Copy)\
                       .then_inc(nT_even, 1)

            even_heads(range(0, H // 2, 2))
            v_tile(1, 0)
            attention(0, prob_m, pT_m, omh, 1, SCALE_MLA, 5, 6, lambda: even_heads(range(H // 2, H, 2)),
                      lambda u: ahead(U_QK + u, u))

            def evict(s, a):
                act.wait_ge(dil_turned, PRIMED + s)
                for t in range(T):
                    act.activation(tok[:, t, :], banks(4 * a + 2 * t, UNIT), ACT.Copy, scale=inv[:, t:t + 1])\
                       .then_inc(dil_tok, 1)
                act.wait_ge(dil_tok, 2 * s + 2)
                for t in range(T):
                    act.activation(banks(4 * a + 2 * t, UNIT), tok[:, t, :], ACT.Square).then_inc(dil_sq, 1)

            def follow(s, a, g, k):
                if k == 2:
                    root(dvar, ddev, dil_var, s + 1, dil_dev)
                if k == 11:
                    act.wait_ge(dil_turned, PRIMED + s + 1)
                    for e in range(2):
                        act.activation((qT, kT)[a][:, ds(g, 1), e * UNIT:(e + 1) * UNIT].rearrange("p a c -> p (a c)"),
                                       banks(4 * a + 2 * e, UNIT), ACT.Copy).then_inc(dil_T, 1)

            evict(0, 0)
            with act.Fori(0, GROUPS - 1) as g:
                for k in range(KD):
                    ahead(U_QK + KD + g * (2 * KD) + k, k)
                    follow(2 * g, 0, g, k)
                evict(2 * g + 1, 1)
                for k in range(KD):
                    ahead(U_QK + 2 * KD + g * (2 * KD) + k, k)
                    follow(2 * g + 1, 1, g, k)
                evict(2 * g + 2, 0)
            last = 2 * GROUPS - 1
            for k in range(KD):
                ahead(U_QK + last * KD + k, k)
                follow(last - 1, 0, GROUPS - 1, k)
            evict(last, 1)
            for k in range(KD):
                ahead(U_V2 + k, k)
                follow(last, 1, GROUPS - 1, k)
            v_tile(GROUPS - 1, 0)
            attention(len(items), prob_d, pT_d, odh, GROUPS, SCALE_DIL, 6, 0, lambda: None,
                      lambda u: ahead(U_MERGE + u, u))

            def gate(n, dst):
                act.wait_ge(mgi_ready, n)
                act.activation(dst[:, :, :], dst[:, :, :], ACT.Sigmoid).then_inc(msig_ready, 1)

            def merged(i):
                act.wait_ge(m_sum, i + 1)
                act.activation(mTh[:, ds(i * 4, 4), :], gs[:, :, :], ACT.Copy).then_inc(mh_ready, 1)

            gate(1, sg_first)
            gate(2, sg)
            for j in range(KD, MERGE_BODY):
                ahead(U_MERGE + j, j)
            merged(0)
            with act.Fori(1, MERGE_TURNS) as i:
                for j in range(MERGE_BODY):
                    ahead(U_MERGE + i * MERGE_BODY + j, j)
                    for a in range(2):
                        if j == a * (MERGE_BODY // 2) + KD // 2 - 1:
                            gate(2 * i + a + 1, sg)
                    if j == MERGE_BODY - 1:
                        merged(i)
            down(U_WO, KD, 2)
            gate_up(U_GU2, 1)
            down(U_DOWN2, KF, 3)

            act.wait_ge(unit_done, U_PLE)
            act.dma_start(p_tok[:, :, :], p[0, 0].rearrange("(t p) c -> p t c", p=P)).then_inc(p_in, 16)
            j = 0
            for h in range(2):
                for k in range(KD + PLE // P):
                    if U_PLE + j + SLOTS < UNITS:
                        ahead(U_PLE + j, j)
                    if h == 0:
                        entry(3, k)
                    if h == 0 and k == 10:
                        act.wait_ge(p_turned, 1)
                        act.activation(pTh[:, :, :], ps[:, 5, :].rearrange("p (k s) -> p k s", s=S), ACT.Copy).then_inc(p_hi, 1)
                    if k == KD - 1:
                        act.wait_ge(unit_done, U_PLE + j + 1)
                        if h == 0:
                            act.wait_ge(inv_ready, 4)
                        for t in range(T):
                            if h:
                                act.wait_ge(res_ready, PRIMED + 12 + t + 1)
                            act.activation(sgp[:, t, :], banks(2 * t, UNIT), ACT.Sigmoid, scale=inv[:, t:t + 1])\
                               .then_inc(psig_ready, 1)
                    j += 1

        @block.vector
        def _(dve):
            chain = Chain(dve, dve_step)

            def split(n, j):
                dve.wait_ge(hi_ready, n + 1)
                dve.tensor_tensor(wl[:, j % SLOTS, :], raw[:, j % SLOTS, :], wh[:, j % SLOTS, :].bitcast(F32),
                                  ALU.subtract).then_inc(lo_ready, 1)

            def ahead(n, j):
                split(n + SLOTS, j)

            def rsqrt(v, s, y, tmp, ready, count):
                dve.wait_ge(ready, count)
                chain(dve.reciprocal(y, s))
                chain(dve.scalar_tensor_tensor(out=tmp, in0=y, scalar=-0.5, in1=y, op0=ALU.mult, op1=ALU.mult))
                chain(dve.tensor_tensor(tmp, tmp, v, ALU.mult))
                return dve.scalar_tensor_tensor(out=y, in0=tmp, scalar=1.5, in1=y, op0=ALU.add, op1=ALU.mult)

            def rest(dst, hi, g0, before, pairs, b0):
                for n, p in enumerate(pairs):
                    dve.wait_ge(tr_hi, 2 * (before + p) + 2)
                    for s in range(2):
                        k = 2 * p + s
                        dve.scalar_tensor_tensor(out=dst[:, k, :], in0=ps[:, b0 + n, s * S:(s + 1) * S],
                                                 scalar=gcol[:, g0 + k:g0 + k + 1], in1=hi[:, k, :].bitcast(F32),
                                                 op0=ALU.mult, op1=ALU.subtract).then_inc(tr_lo, 1)

            LEFT, RIGHT = range(KD // 4), range(KD // 4, KD // 2)

            def entry(r, j):
                if j == 1:
                    rest(hTl, hTh, r * KD, PAIRS[r], RIGHT, 4)
                if j == 2:
                    dve.wait_ge(ss_ready, 4 * r + 4)
                    chain(dve.tensor_tensor(var, ssq[:, 0:2], ssq[:, 2:4], ALU.add))
                    dve.tensor_scalar(var, var, 1.0 / D, EPS, ALU.mult, ALU.add).then_inc(var_ready, 1)
                    rsqrt(var, dev, inv, nwt, dev_ready, r + 1).then_inc(inv_ready, 1)
                    dve.wait_ge(inv_ready, r + 1)
                    for t in range(T):
                        ins = dve.tensor_scalar(diag[:, t, :], ident[:, :], inv[:, t:t + 1], None, ALU.mult)
                    ins.then_inc(diag_ready, 1)
                if j == 6:
                    dve.wait_ge(row_turned, r + 1)
                    dve.tensor_copy(inv_row[:, :], ps[:, 4, 0:S]).then_inc(row_ready, 1)
                    dve.wait_ge(row_ready, r + 1)

            rms4 = inv_row[:, :].unsqueeze(1).to_broadcast([P, 4, S])

            def gate_up(u0, f):
                def turn(i, j, n):
                    if j == KD // 2 - 1:
                        dve.wait_ge(unit_done, n + 1)
                        dve.wait_ge(a_ready, PRIMED + f * FFN_TURNS + i)
                        dve.tensor_tensor(gs[:, :, :], quad(0), rms4, ALU.mult).then_inc(gi_ready, 1)
                    if j == KD // 2:
                        dve.wait_ge(sig_ready, f * FFN_TURNS + i + 1)
                        chain(dve.tensor_tensor(gs[:, :, :], gs[:, :, :], sg[:, :, :], ALU.mult))
                        dve.tensor_tensor(gs[:, :, :], gs[:, :, :], rms4, ALU.mult).then_inc(gs_ready, 1)
                    if j == FFN_BODY - 1:
                        dve.wait_ge(unit_done, n + 1)
                        dve.wait_ge(gs_ready, PRIMED + f * FFN_TURNS + i + 1)
                        dve.tensor_tensor(gs[:, :, :], quad(4), gs[:, :, :], ALU.mult).then_inc(am_ready, 1)
                        dve.wait_ge(ah_ready, f * FFN_TURNS + i + 1)
                        dve.tensor_tensor(aTl[:, ds(i * 4, 4), :], gs[:, :, :],
                                          aTh[:, ds(i * 4, 4), :].bitcast(F32), ALU.subtract).then_inc(a_ready, 1)

                for j in range(FFN_BODY):
                    ahead(u0 + j, j)
                    entry(2 * f, j)
                    turn(0, j, u0 + j)
                with dve.Fori(1, FFN_TURNS) as i:
                    chain.enter(i - 1, 1)
                    for j in range(FFN_BODY):
                        ahead(u0 + i * FFN_BODY + j, j)
                        turn(i, j, u0 + i * FFN_BODY + j)
                    chain.leave(FFN_TURNS - 1)

            def down(u0, K, r, factor, meanwhile=None):
                for half in range(2):
                    for k in range(K):
                        if k == K - 1:
                            dve.wait_ge(unit_done, u0 + half * K + K)
                            for t in range(T):
                                part = res[:, t, half * UNIT:(half + 1) * UNIT]
                                dve.scalar_tensor_tensor(out=part, in0=banks(4 * half + 2 * t, UNIT), scalar=factor,
                                                         in1=part, op0=ALU.mult, op1=ALU.add).then_inc(res_ready, 1)
                        ahead(u0 + half * K + k, k)
                        if half == 0 and meanwhile:
                            meanwhile(k)
                        if half == 1 and k in (6, 8, 10, 12):
                            rest(hTl, hTh, r * KD, PAIRS[r], LEFT[k // 2 - 3:k // 2 - 2], k // 2 - 3)

            def rotate(x1, x2, c, s, a, b):
                dve.tensor_tensor(a, x2, s, ALU.mult)
                chain(dve.tensor_tensor(b, x1, s, ALU.mult))
                dve.tensor_tensor(x1, x1, c, ALU.mult)
                chain(dve.tensor_tensor(x2, x2, c, ALU.mult))
                dve.tensor_tensor(x1, x1, a, ALU.subtract)
                return dve.tensor_tensor(x2, x2, b, ALU.add)

            def v_tile(g, b0):
                dve.tensor_scalar(vd[:, g, UNIT:2 * UNIT], banks(b0 + 2, UNIT), inv[:, 1:2], None, ALU.mult)\
                   .then_inc(dil_v, 1)

            def attention(first, prob, masks, ol, oh, n_keys, scale, score_bank, out_bank, begun, between):
                def mask(u):
                    h, t = items[u]
                    n = n_keys * (t + 1) * P
                    dve.wait_ge(score_done, first + u + 1)
                    if u >= 2:
                        dve.wait_ge(prob_turned, first + u - 1)
                    a = prob[:, u % 2, 0:n].rearrange("p (g c) -> p g c", g=n_keys)
                    s = banks(score_bank, n).rearrange("p (g c) -> p g c", g=n_keys)
                    chain(dve.tensor_tensor_reduce(a, s, masks(t), 1.0, -3.0e38, ALU.add, ALU.max, s_max[:, u:u + 1]))
                    dve.tensor_scalar(s_bias[:, u:u + 1], s_max[:, u:u + 1], -scale, None, ALU.mult).then_inc(masked, 1)

                def norm(u):
                    h, t = items[u]
                    n = n_keys * (t + 1) * P
                    dve.wait_ge(exp_done, first + u + 1)
                    chain(dve.reciprocal(s_inv[:, u:u + 1], s_sum[:, u:u + 1]))
                    dve.tensor_scalar(prob[:, u % 2, 0:n], prob[:, u % 2, 0:n], s_inv[:, u:u + 1], None, ALU.mult)\
                       .then_inc(prob_ready, 1)

                def out_rest(u):
                    h, t = items[u]
                    dve.wait_ge(o_hi, first + u + 1)
                    dve.tensor_tensor(ol[:, h, t * P:(t + 1) * P], ps[:, out_bank + u % 2, 0:P],
                                      oh[:, h, t * P:(t + 1) * P].bitcast(F32), ALU.subtract).then_inc(o_lo, 1)

                mask(0)
                begun()
                norm(0)
                for u in range(len(items)):
                    if u + 1 < len(items):
                        mask(u + 1)
                    if u:
                        between(u - 1)
                    if u + 1 < len(items):
                        norm(u + 1)
                    if u >= 2:
                        out_rest(u - 2)
                between(len(items) - 1)
                out_rest(len(items) - 2)
                out_rest(len(items) - 1)

            for n in range(SLOTS):
                rest(hTl, hTh, 0, PAIRS[0], LEFT[n:n + 1], 4 + n)
                split(n, n)
            gate_up(U_GU1, 0)

            def angles(k):
                if k == 0:
                    dve.wait_ge(consts_in, 16 * 2)
                    chain(dve.tensor_copy(pos_f[:, :], pos_i[:, :]))
                if k in (1, 3, 5, 7):
                    n = k // 2
                    t, quarter = n // 2, (n % 2) * 0.25
                    if n:
                        dve.wait_ge(angles_ready, n)
                    chain(dve.tensor_scalar(angle[:, :], freq[:, :], pos_f[:, t:t + 1], None, ALU.mult))
                    if n:
                        dve.wait_ge(tables_ready, n)
                    chain(dve.tensor_scalar(turns[:, :], angle[:, :], 0.15915494309189535, quarter, ALU.mult, ALU.add))
                    chain(dve.tensor_scalar(turns[:, :], turns[:, :], ROUND, -ROUND, ALU.add, ALU.add))
                    for part in (TWO_PI_1, TWO_PI_2, TWO_PI_3):
                        chain(dve.scalar_tensor_tensor(out=angle[:, :], in0=turns[:, :], scalar=-part,
                                                       in1=angle[:, :], op0=ALU.mult, op1=ALU.add))
                    chain(dve.tensor_scalar(angle[:, :], angle[:, :], quarter * 6.283185307179586, PI_DOWN,
                                            ALU.add, ALU.min))
                    dve.tensor_scalar(turns[:, :], angle[:, :], -PI_DOWN, None, ALU.max).then_inc(angles_ready, 1)

            down(U_DOWN1, KF, 1, 0.5, angles)

            for k in range(KD):
                ahead(U_LAT + k, k)
                entry(1, k)
            for k in range(KD):
                ahead(U_V0 + k, k)
                if k == 1:
                    dve.wait_ge(lat_ss, 6)
                    cs, cv = (a.rearrange("p (t a) -> p t a", a=2) for a in (css, cvar))
                    dve.tensor_scalar(cv[:, :, 0], cs[:, :, 0], 1.0 / LQ, EPS, ALU.mult, ALU.add).then_inc(lat_var, 1)
                    dve.tensor_scalar(cv[:, :, 1], cs[:, :, 1], 1.0 / LKV, EPS, ALU.mult, ALU.add).then_inc(lat_var, 1)
                    dve.wait_ge(lat_var, 2)
                    chain(rsqrt(cvar, cdev, cinv, cnwt, lat_dev, 1))
                if k == 2:
                    for t in range(T):
                        for a, (c0, c1) in enumerate(((0, LQ), (LQ, LQ + LKV))):
                            ins = dve.tensor_scalar(c_tok[:, t, c0:c1], c_tok[:, t, c0:c1],
                                                    cinv[:, 2 * t + a:2 * t + a + 1], None, ALU.mult)
                    ins.then_inc(lat_ready, 1)
                if k == 4:
                    rest(cTl, cTh, 4 * KD, C_PAIRS, range(NG // 2), 0)
            dve.wait_ge(unit_done, U_V0 + KD)
            v_tile(0, 4)
            for n in range(2 * (LQ // P)):
                ahead(U_UQ + n, n)
            for n in range(2 * (LKV // P)):
                ahead(U_UKV + n, n)

            ms = mss.rearrange("p (a t h) -> p a t h", a=2, t=T)
            mi = minv.rearrange("p (a t h) -> p a t h", a=2, t=T)

            def gain(g, a, e):
                return g[:, a:e].unsqueeze(1).to_broadcast([P, H, e - a])

            half = ROPE // 2
            for k in range(KD):
                ahead(U_V1 + k, k)
                if k < 4:
                    a, t = k // 2, k % 2
                    width = (QK, NOPE)[a]
                    dve.wait_ge(mla_sq, k + 1)
                    dve.tensor_reduce(ms[:, a, t, :], sq[:, 0:H * width].rearrange("p (h c) -> p h c", h=H),
                                      AX_X, ALU.add).then_inc(mla_ss, 1)
                if k == 4:
                    dve.wait_ge(mla_ss, 4)
                    dve.wait_ge(gains_in, 16 * 6)
                    for t in range(T):
                        chain(dve.tensor_scalar(ms[:, 1, t, :], ms[:, 1, t, :], kss_m[:, t:t + 1], None, ALU.add))
                    dve.tensor_scalar(mvar, mss, 1.0 / QK, EPS, ALU.mult, ALU.add).then_inc(mla_var, 1)
                    dve.wait_ge(mla_var, 1)
                    rsqrt(mvar, mdev, minv, mnwt, mla_dev, 1).then_inc(mla_inv, 1)
                    dve.wait_ge(mla_inv, 1)
                if k in (6, 7, 8, 9, 10, 11):
                    t = (k - 6) // 3
                    qv = q_tok[:, t, :].rearrange("p (h c) -> p h c", h=H)
                    kv = kv_tok[:, t, :].rearrange("p (h c) -> p h c", h=H)[:, :, 0:NOPE]
                    qr, kr = rh[:, t, 0, :, :], rh[:, t, 1, :, :]
                    if (k - 6) % 3 == 0:
                        ik = mi[:, 1, t, :].unsqueeze(2)
                        chain(dve.tensor_tensor(kr, c_tok[:, t, LQ + LKV:LAT].unsqueeze(1).to_broadcast([P, H, ROPE]),
                                                ik.to_broadcast([P, H, ROPE]), ALU.mult))
                        dve.tensor_tensor(kr, kr, gain(gk_mla, NOPE, QK), ALU.mult)
                        dve.wait_ge(mla_scaled, 2 * t + 1)
                        chain(dve.tensor_tensor(qr, qv[:, :, NOPE:QK], gain(gq_mla, NOPE, QK), ALU.mult))
                    if (k - 6) % 3 == 1:
                        if t:
                            dve.wait_ge(mla_ready, t)
                        both = rh[:, t, :, :, :].rearrange("p a h c -> p (a h) c")
                        c, s = (b[:, t, 0:half].unsqueeze(1).to_broadcast([P, 2 * H, half]) for b in (cos, sin))
                        chain(rotate(both[:, :, 0:half], both[:, :, half:ROPE], c, s, tmpA[:, :, :], tmpB[:, :, :]))
                    if (k - 6) % 3 == 2:
                        dve.wait_ge(mla_scaled, 2 * t + 2)
                        dve.tensor_tensor(qv[:, :, 0:NOPE], qv[:, :, 0:NOPE], gain(gq_mla, 0, NOPE), ALU.mult)
                        dve.tensor_tensor(kv, kv, gain(gk_mla, 0, NOPE), ALU.mult).then_inc(mla_ready, 1)
                if k == 13:
                    for a in range(2):
                        dve.wait_ge(mla_turned, a + 1)
                        dve.tensor_copy(rT[:, a, :, :].rearrange("p h s -> p (h s)"), banks(4 + 2 * a, UNIT))\
                           .then_inc(rT_ready, 1)

            def odd_heads(heads):
                for h in heads:
                    dve.wait_ge(mla_turned, 2 + h + 1)
                    dve.tensor_copy(nT[:, h, :, :], ps[:, (h + 4) % 8, :].rearrange("p (a s) -> p a s", a=2))\
                       .then_inc(nT_odd, 1)

            odd_heads(range(1, H // 2, 2))
            dve.wait_ge(unit_done, U_V1 + KD)
            v_tile(1, 0)

            def mla_mask(t):
                return m_mla[:, (1 - t) * P:2 * P].unsqueeze(1)

            attention(0, prob_m, mla_mask, oml, omh, 1, SCALE_MLA, 4, 6, lambda: odd_heads(range(H // 2 + 1, H, 2)),
                      lambda u: ahead(U_QK + u, u))

            di = dinv.rearrange("p (t h) -> p t h", t=T)

            def follow(s, a, g, k):
                if k == 0:
                    for t in range(T):
                        dve.wait_ge(dil_sq, 2 * s + t + 1)
                        dve.tensor_reduce(dss[:, t * H:(t + 1) * H], banks(4 * a + 2 * t, UNIT)
                                          .rearrange("p (h c) -> p h c", h=H), AX_X, ALU.add).then_inc(dil_ss, 1)
                if k == 2:
                    dve.wait_ge(dil_ss, 2 * s + 2)
                    dve.tensor_scalar(dvar, dss, 1.0 / HD, EPS, ALU.mult, ALU.add).then_inc(dil_var, 1)
                    dve.wait_ge(dil_var, s + 1)
                    chain(rsqrt(dvar, ddev, dinv, dnwt, dil_dev, s + 1))
                for t in range(T):
                    if k == 3 + 2 * t:
                        gains = (gq_dil, gk_dil)[a][:, ds(g, 1), :].rearrange("p a c -> p (a c)")
                        for h in range(H):
                            v = tok[:, t, h * HD:(h + 1) * HD]
                            ins = dve.scalar_tensor_tensor(out=v, in0=v, scalar=di[:, t, h:h + 1], in1=gains,
                                                           op0=ALU.mult, op1=ALU.mult)
                        chain(ins)
                    if k == 4 + 2 * t:
                        v = tok[:, t, :].rearrange("p (h c) -> p h c", h=H)
                        hf = ROT // 2
                        c, sn = (b[:, t, NF - hf:NF].unsqueeze(1).to_broadcast([P, H, hf]) for b in (cos, sin))
                        dve.wait_ge(dil_ready, PRIMED + 2 * s + t)
                        rotate(v[:, :, 0:hf], v[:, :, hf:ROT], c, sn, ropeA[:, :, :], ropeB[:, :, :])\
                            .then_inc(dil_ready, 1)

            FOLLOW_STEPS = 4 + T * 3
            with dve.Fori(0, GROUPS - 1) as g:
                chain.enter(g, 2 * FOLLOW_STEPS)
                for k in range(KD):
                    ahead(U_QK + KD + g * (2 * KD) + k, k)
                    follow(2 * g, 0, g, k)
                for k in range(KD):
                    ahead(U_QK + 2 * KD + g * (2 * KD) + k, k)
                    follow(2 * g + 1, 1, g, k)
                chain.leave(GROUPS - 1)
            last = 2 * GROUPS - 1
            for k in range(KD):
                ahead(U_QK + last * KD + k, k)
                follow(last - 1, 0, GROUPS - 1, k)
            for k in range(KD):
                ahead(U_V2 + k, k)
                follow(last, 1, GROUPS - 1, k)
            dve.wait_ge(unit_done, U_V2 + KD)
            v_tile(GROUPS - 1, 0)

            def dil_mask(t):
                return m_dil[:, :, (1 - t) * P:2 * P]

            def gate(n, b0, dst, units):
                dve.wait_ge(unit_done, units)
                dve.tensor_tensor(dst[:, :, :], quad(b0), rms4, ALU.mult).then_inc(mgi_ready, 1)

            def first_gates(u):
                ahead(U_MERGE + u, u)
                if u == KD // 2 - 1:
                    gate(1, 2, sg_first, U_MERGE + KD // 2)

            attention(len(items), prob_d, dil_mask, odl, odh, GROUPS, SCALE_DIL, 4, 0, lambda: None, first_gates)
            dve.wait_ge(prob_turned, 2 * len(items))
            dve.wait_ge(prob_ready, 2 * len(items))
            gate(2, 2, sg, U_MERGE + KD)

            def product(n, b0, src, dst, units):
                dve.wait_ge(msig_ready, n)
                dve.wait_ge(unit_done, units)
                dve.tensor_tensor(dst[:, :, :], quad(b0), src[:, :, :], ALU.mult).then_inc(mprod_ready, 1)

            def merged(i):
                dve.wait_ge(mprod_ready, 2 * i + 2)
                dve.tensor_tensor(gs[:, :, :], gs[:, :, :], am[:, :, :], ALU.add).then_inc(m_sum, 1)
                dve.wait_ge(mh_ready, i + 1)
                dve.tensor_tensor(mTl[:, ds(i * 4, 4), :], gs[:, :, :],
                                  mTh[:, ds(i * 4, 4), :].bitcast(F32), ALU.subtract).then_inc(m_ready, 1)

            for j in range(KD, MERGE_BODY):
                ahead(U_MERGE + j, j)
                if j == KD + H // 2 - 1:
                    dve.wait_ge(pv_done, 2 * len(items))
                    product(1, 4, sg_first, gs, U_MERGE + j + 1)
                if j == MERGE_BODY - 1:
                    product(2, 6, sg, am, U_MERGE + j + 1)
            merged(0)
            with dve.Fori(1, MERGE_TURNS) as i:
                for j in range(MERGE_BODY):
                    ahead(U_MERGE + i * MERGE_BODY + j, j)
                    for a in range(2):
                        if j == a * (MERGE_BODY // 2) + KD // 2 - 1:
                            dve.wait_ge(mprod_ready, 2 * i + a)
                            gate(2 * i + a + 1, (2, 0)[a], sg, U_MERGE + i * MERGE_BODY + j + 1)
                        if j == (a + 1) * (MERGE_BODY // 2) - 1:
                            if a == 0:
                                dve.wait_ge(m_ready, i)
                            product(2 * i + a + 1, (4, 6)[a], sg, (gs, am)[a], U_MERGE + i * MERGE_BODY + j + 1)
                merged(i)
            down(U_WO, KD, 2, 1.0)
            gate_up(U_GU2, 1)
            down(U_DOWN2, KF, 3, 0.5)

            j = 0
            for h in range(2):
                for k in range(KD + PLE // P):
                    if U_PLE + j + SLOTS < UNITS:
                        ahead(U_PLE + j, j)
                    if h == 0:
                        entry(3, k)
                    if h == 0 and k == 10:
                        dve.wait_ge(p_hi, 1)
                        dve.tensor_tensor(pTl[:, :, :], ps[:, 5, :].rearrange("p (k s) -> p k s", s=S),
                                          pTh[:, :, :].bitcast(F32), ALU.subtract).then_inc(p_lo, 1)
                    j += 1
                dve.wait_ge(unit_done, U_PLE + j)
                for t in range(T):
                    dve.wait_ge(psig_ready, 2 * h + t + 1)
                    part = sgp[:, t, :]
                    dve.tensor_tensor(part, part, banks(4 + 2 * t, UNIT), ALU.mult).then_inc(psig_used, 1)
                    dve.wait_ge(psig_used, 2 * h + t + 1)
                    dst = res[:, t, h * UNIT:(h + 1) * UNIT]
                    dve.tensor_tensor(dst, dst, part, ALU.add).then_inc(res_ready, 1)


_INS = ['x', 'p', 'positions', 'g_ffn1', 'w1_gate', 'w1_up', 'w1_down', 'g_mix', 'w_in', 'g_cq', 'w_uq',
        'g_ckv', 'w_ukv', 'g_q_mla', 'g_k_mla', 'g_q_dil', 'g_k_dil', 'w_br_mla', 'w_br_dil', 'w_o', 'g_ffn2',
        'w2_gate', 'w2_up', 'w2_down', 'g_ple', 'w_ple_gate', 'w_ple_proj']


def constants(np, bf16):
    P, NEG, THETA = 128, -1e30, 500000.0
    q, k = np.arange(P)[:, None], np.arange(P)[None, :]
    causal = k <= q
    mla = np.concatenate([np.ones((P, P), bool), causal], axis=1)
    groups = ((128, 1), (512, 4), (2048, 16))

    def seen(qi, ki, win, dil):
        gap = qi - ki
        return (gap >= 0) & (gap % dil == 0) & (gap <= win)

    dil = np.concatenate([seen(q + P, np.arange(2 * P)[None, :], w, d) for w, d in groups], axis=1)
    freq = [THETA ** (-np.arange(rd // 2, dtype=np.float64) * 2.0 / rd) for rd in (64, 32)]
    return {
        "identity": np.eye(P, dtype=np.float32),
        "mla_masks": np.where(mla, 0.0, NEG).astype(bf16),
        "dil_masks": np.where(dil, 0.0, NEG).astype(bf16),
        "inverse_frequencies": np.concatenate(freq).astype(np.float32)[None, :],
    }


def kernel(**inputs):
    import ml_dtypes
    import numpy as np
    import concourse.bacc as bacc
    from concourse.bass_utils import run_bass_kernel_spmd

    nc = bacc.Bacc("TRN2", target_bir_lowering=False, num_devices=1)
    arrays = {name: np.ascontiguousarray(inputs[name]) for name in _INS}
    arrays.update(constants(np, ml_dtypes.bfloat16))
    aps = {name: nc.dram_tensor(f"in_{name}", a.shape, mybir.dt.from_np(a.dtype), kind="ExternalInput").ap()
           for name, a in arrays.items()}
    out = nc.dram_tensor("out_x", arrays["x"].shape, F32, kind="ExternalOutput").ap()
    hybrid_layer(nc, out, **aps)
    r = run_bass_kernel_spmd(nc, [{f"in_{name}": a for name, a in arrays.items()}], core_ids=[0])
    return r.results[0]["out_x"]
```

```python
from contextlib import ExitStack

import concourse.bass as bass
from concourse import mybir

ALU = mybir.AluOpType
ACT = mybir.ActivationFunctionType
AX_X = mybir.AxisListType.X
F32 = mybir.dt.float32
F32R = mybir.dt.float32r
BF16 = mybir.dt.bfloat16
I32 = mybir.dt.int32
ds = bass.ds

P = 128
BANK = 512
SLOTS = 4
UNIT = 1024
EPS = 1e-6
PRIMED = 1
ROUND = 1.5 * 2.0 ** 23
TWO_PI_1 = 6.28125
TWO_PI_2 = 0.0019340515136718750
TWO_PI_3 = 6.283185307179586 - TWO_PI_1 - TWO_PI_2
PI_DOWN = 3.1415925


class Chain:

    def __init__(self, eng, sem):
        self.eng, self.sem, self.n, self.past = eng, sem, 0, 0

    def __call__(self, ins):
        ins.then_inc(self.sem, 1)
        self.n += 1
        self.eng.wait_ge(self.sem, self.past + self.n)

    def enter(self, i, steps):
        self.past, self.first, self.steps = i * steps, self.n, steps

    def leave(self, turns):
        assert self.n - self.first == self.steps, (self.n - self.first, self.steps)
        self.past, self.n = 0, self.n + self.steps * (turns - 1)


def hybrid_layer(nc, out, x, p, positions, g_ffn1, w1_gate, w1_up, w1_down, g_mix, w_in, g_cq, w_uq,
                 g_ckv, w_ukv, g_q_mla, g_k_mla, g_q_dil, g_k_dil, w_br_mla, w_br_dil, w_o, g_ffn2,
                 w2_gate, w2_up, w2_down, g_ple, w_ple_gate, w_ple_proj, identity, mla_masks,
                 dil_masks, inverse_frequencies):
    _, S, D = x.shape
    FF = w1_gate.shape[2]
    PLE = p.shape[3]
    LQ, LKV = g_cq.shape[1], g_ckv.shape[1]
    QK = g_q_mla.shape[1]
    GROUPS, HD = g_q_dil.shape[1:]
    NOPE = HD
    ROPE = QK - NOPE
    H = w_br_dil.shape[1] // HD
    ROT = HD // 4
    LAT = LQ + LKV + ROPE
    OFF_GATE = LAT + GROUPS * 3 * H * HD
    NF = inverse_frequencies.shape[1]
    T, KD, KF = S // P, D // P, FF // P
    HQ, HK = H * QK // 2, H * (NOPE + HD) // 2
    assert T == 2 and D == 2 * UNIT and H * HD == UNIT and NF == ROPE // 2 + ROT // 2
    SCALE_MLA, SCALE_DIL = QK ** -0.5, HD ** -0.5
    NG = LQ // P + LKV // P

    FFN_TURNS, FFN_BODY = FF // BANK, 2 * KD // 2
    MERGE_TURNS, MERGE_BODY = D // BANK, 2 * (KD // 2 + H // 2)
    counts = [FFN_TURNS * FFN_BODY, 2 * KF, KD, KD, 2 * (LQ // P), 2 * (LKV // P),
              KD, 2 * GROUPS * KD, KD, MERGE_TURNS * MERGE_BODY, 2 * KD,
              FFN_TURNS * FFN_BODY, 2 * KF, 2 * (KD + PLE // P)]
    starts = [sum(counts[:n]) for n in range(len(counts))]
    (U_GU1, U_DOWN1, U_LAT, U_V0, U_UQ, U_UKV, U_V1, U_QK, U_V2, U_MERGE, U_WO, U_GU2, U_DOWN2, U_PLE) = starts
    UNITS = sum(counts)
    assert all(n % SLOTS == 0 for n in counts)

    with ExitStack() as ctx:
        def sem(name):
            return ctx.enter_context(nc.semaphore(name))

        def sb(name, shape, dt=F32):
            return ctx.enter_context(nc.sbuf_tensor(name, shape, dt))

        ps = ctx.enter_context(nc.psum_tensor("ps", [P, 8, BANK], F32))
        flat = ps[:, :, :].rearrange("p b c -> p (b c)")

        def banks(b, width):
            return flat[:, b * BANK:b * BANK + width]

        def quad(b):
            return banks(b, 4 * S).rearrange("p (c s) -> p c s", s=S)

        res = sb("res", [P, T, D])
        hTh = sb("hTh", [P, KD, S], F32R)
        hTl = sb("hTl", [P, KD, S], F32R)
        raw = sb("raw", [P, SLOTS, UNIT])
        wh = sb("wh", [P, SLOTS, UNIT], F32R)
        wl = sb("wl", [P, SLOTS, UNIT], F32R)
        ident = sb("ident", [P, P])
        ones = sb("ones", [P, P])
        inv_row = sb("inv_row", [P, S])
        gcol = sb("gcol", [P, 4 * KD + NG + 2])
        gq_mla, gk_mla = sb("gq_mla", [P, QK]), sb("gk_mla", [P, QK])
        gq_dil, gk_dil = sb("gq_dil", [P, GROUPS, HD]), sb("gk_dil", [P, GROUPS, HD])
        m_mla = sb("m_mla", [P, 2 * P], BF16)
        m_dil = sb("m_dil", [P, GROUPS, 2 * P], BF16)
        sin, cos = sb("sin", [P, T, NF]), sb("cos", [P, T, NF])
        small = sb("small", [P, 256])

        base = nc.sbuf_base
        room = nc.sbuf_top - base

        def at(name, where, shape, dt=F32):
            size = 4
            for n in shape[1:]:
                size *= n
            assert where + size <= room, (name, where, size, room)
            return nc.alloc_sbuf_tensor_at(name, shape, dt, offset=base + where)

        KB = 1024
        aTh, aTl = at("aTh", 0, [P, KF, S], F32R), at("aTl", 44 * KB, [P, KF, S], F32R)
        sg, gs = at("sg", 88 * KB, [P, 4, S]), at("gs", 92 * KB, [P, 4, S])
        junk = at("junk", 88 * KB, [P, UNIT])
        diag = at("diag", 98 * KB, [P, T, P])
        grow_1, grow_rest = at("grow_1", 16 * KB, [KD, P]), at("grow_rest", 17 * KB, [3 * KD + NG + 2, P])
        angle, turns, freq = (at(n, 96 * KB + 256 * j, [P, NF]) for j, n in enumerate(("angle", "turns", "freq")))
        pos_i, pos_f = at("pos_i", 96 * KB + 768, [P, T], I32), at("pos_f", 96 * KB + 800, [P, T])
        q_tok, kv_tok = at("q_tok", 0, [P, T, H * QK]), at("kv_tok", 16 * KB, [P, T, H * (NOPE + HD)])
        cTh, cTl = at("cTh", 32 * KB, [P, NG, S], F32R), at("cTl", 38 * KB, [P, NG, S], F32R)
        nT = at("nT", 32 * KB, [P, H, 2, S])
        rh = at("rh", 48 * KB, [P, T, 2, H, ROPE])
        rT = at("rT", 56 * KB, [P, 2, H // 2, S])
        sq = at("sq", 56 * KB, [P, H * QK])
        tmpA, tmpB = at("tmpA", 62 * KB, [P, H, ROPE // 2]), at("tmpB", 63 * KB, [P, H, ROPE // 2])
        k_rot = at("k_rot", 96 * KB, [P, T, ROPE])
        c_tok = at("c_tok", 88 * KB, [P, T, LAT])
        prob_m, pT_m = at("prob_m", 88 * KB, [P, 2, 2 * P]), at("pT_m", 90 * KB, [P, 2 * P])
        omh, oml = at("omh", 0, [P, H, S], F32R), at("oml", 8 * KB, [P, H, S], F32R)
        qT, kT = at("qT", 16 * KB, [P, GROUPS, H * S]), at("kT", 40 * KB, [P, GROUPS, H * S])
        vd = at("vd", 64 * KB, [P, GROUPS, T * UNIT])
        tok = at("tok", 88 * KB, [P, T, UNIT])
        ropeA, ropeB = (at(n, 96 * KB + 512 * j, [P, H, ROT // 2]) for j, n in enumerate(("ropeA", "ropeB")))
        prob_d, pT_d = at("prob_d", 88 * KB, [P, 2, 6 * P]), at("pT_d", 94 * KB, [P, 6 * P])
        sg_first = at("sg_first", 97 * KB, [P, 4, S])
        odh, odl = at("odh", 16 * KB, [P, H, S], F32R), at("odl", 40 * KB, [P, H, S], F32R)
        mTh, mTl = at("mTh", 48 * KB, [P, KD, S], F32R), at("mTl", 64 * KB, [P, KD, S], F32R)
        am = at("am", 80 * KB, [P, 4, S])
        sgp = at("sgp", 0, [P, T, UNIT])
        p_tok = at("p_tok", 16 * KB, [P, T, PLE])
        pTh, pTl = at("pTh", 18 * KB, [P, PLE // P, S], F32R), at("pTl", 20 * KB, [P, PLE // P, S], F32R)

        raw_in = [sem(f"raw_in{j}") for j in range(SLOTS)]
        hi_ready, lo_ready = sem("hi_ready"), sem("lo_ready")
        unit_done = sem("unit_done")
        x_in = [sem(f"x_in{j}") for j in range(4)]
        ident_in, row1_in, rows_in, consts_in, gains_in, p_in = (
            sem(n) for n in ("ident_in", "row1_in", "rows_in", "consts_in", "gains_in", "p_in"))
        ones_ready, gains_turned, gcol_ready, angles_ready, tables_ready = (
            sem(n) for n in ("ones_ready", "gains_turned", "gcol_ready", "angles_ready", "tables_ready"))
        ss_ready, var_ready, dev_ready, inv_ready = (sem(n) for n in ("ss_ready", "var_ready", "dev_ready", "inv_ready"))
        diag_ready, row_turned, row_ready = (sem(n) for n in ("diag_ready", "row_turned", "row_ready"))
        turned, tr_hi, tr_lo = sem("turned"), sem("tr_hi"), sem("tr_lo")
        gi_ready, sig_ready, gs_ready, am_ready, ah_ready, a_ready = (
            sem(n) for n in ("gi_ready", "sig_ready", "gs_ready", "am_ready", "ah_ready", "a_ready"))
        res_ready = sem("res_ready")
        lat_tok, lat_ss, lat_var, lat_dev, lat_ready = (
            sem(n) for n in ("lat_tok", "lat_ss", "lat_var", "lat_dev", "lat_ready"))
        uq_tok, ukv_tok, uq_tok_1, ukv_tok_1 = (sem(n) for n in ("uq_tok", "ukv_tok", "uq_tok_1", "ukv_tok_1"))
        mla_sq, mla_var, mla_dev, mla_inv, mla_scaled, q_rotated, mla_ready, mla_turned, rT_ready, nT_even, nT_odd = (
            sem(n) for n in ("mla_sq", "mla_var", "mla_dev", "mla_inv", "mla_scaled", "q_rotated", "mla_ready",
                             "mla_turned", "rT_ready", "nT_even", "nT_odd"))
        dil_tok, dil_sq, dil_ss, dil_var, dil_dev, dil_ready, dil_turned, dil_T, dil_v = (
            sem(n) for n in ("dil_tok", "dil_sq", "dil_ss", "dil_var", "dil_dev", "dil_ready", "dil_turned",
                             "dil_T", "dil_v"))
        score_done, masked, exp_done, prob_ready, prob_turned, pT_ready, pv_done, o_hi, o_lo = (
            sem(n) for n in ("score_done", "masked", "exp_done", "prob_ready", "prob_turned", "pT_ready",
                             "pv_done", "o_hi", "o_lo"))
        gate_out, mgi_ready, msig_ready, mprod_ready, m_sum, mh_ready, m_ready = (
            sem(n) for n in ("gate_out", "mgi_ready", "msig_ready", "mprod_ready", "m_sum", "mh_ready", "m_ready"))
        p_turned, p_hi, p_lo, psig_ready, psig_used, last_done, last_used, out_ready, out_done = (
            sem(n) for n in ("p_turned", "p_hi", "p_lo", "psig_ready", "psig_used", "last_done", "last_used",
                             "out_ready", "out_done"))
        dve_step = sem("dve_step")

        ssq = small[:, 0:4]
        var, dev, inv, nwt = (small[:, 4 + 2 * j:6 + 2 * j] for j in range(4))
        css, cvar, cdev, cinv, cnwt = (small[:, 12 + 4 * j:16 + 4 * j] for j in range(5))
        mss, mvar, mdev, minv, mnwt = (small[:, 32 + 32 * j:64 + 32 * j] for j in range(5))
        dss, dvar, ddev, dinv, dnwt = (small[:, 32 + 32 * j:48 + 32 * j] for j in range(5))
        s_max, s_bias, s_sum, s_inv = (small[:, 192 + 16 * j:208 + 16 * j] for j in range(4))
        kss_m = small[:, 10:12]

        items = [(h, t) for h in range(H) for t in range(T)]

        PAIRS = [r * KD // 2 + (NG // 2 if r >= 2 else 0) for r in range(4)]
        C_PAIRS = PAIRS[1] + KD // 2

        block = ctx.enter_context(nc.Block())

        @block.sync
        def _(sp):
            def wide(n, j, w, k, c0, width=UNIT):
                sp.wait_ge(lo_ready, n - (SLOTS - 1))
                sp.dma_start(raw[:, j % SLOTS, 0:width], w[0, k * P:(k + 1) * P, ds(c0, width)])\
                  .then_inc(raw_in[j % SLOTS], 16)

            def square(n, j, w, k, c0, waits=1):
                if waits and not (isinstance(n, int) and n < SLOTS):
                    sp.wait_ge(lo_ready, n + waits - SLOTS)
                sp.dma_start(raw[:, j % SLOTS, :].rearrange("p (k c) -> p k c", k=2),
                             w[0, k * P:(k + 2) * P, ds(c0, BANK)].rearrange("(k p) c -> p k c", p=P))\
                  .then_inc(raw_in[j % SLOTS], 16)

            def load_x(quarter):
                c0, c1 = quarter * BANK, (quarter + 1) * BANK
                sp.dma_start(res[:, :, c0:c1], x[0, :, c0:c1].rearrange("(t p) c -> p t c", p=P))\
                  .then_inc(x_in[quarter], 16)

            def load_gains():
                r0 = 0
                for g in (g_mix, g_ffn2, g_ple, g_cq, g_ckv, g_q_mla[:, 0:NOPE], g_k_mla[:, 0:NOPE]):
                    n = g.shape[1] // P
                    sp.dma_start(grow_rest[r0:r0 + n, :], g[0].rearrange("(k p) -> k p", p=P)).then_inc(rows_in, 16)
                    r0 += n

            def load_tables():
                sp.dma_start(freq[:, :], inverse_frequencies[0].partition_broadcast(P)).then_inc(consts_in, 16)
                with nc.allow_non_contiguous_dma(reason="256 positions"):
                    sp.dma_start(pos_i[:, :], positions[0].rearrange("(t p) -> p t", p=P)).then_inc(consts_in, 16)
                for dst, src in ((gq_mla, g_q_mla[0]), (gk_mla, g_k_mla[0])):
                    sp.dma_start(dst[:, :], src.partition_broadcast(P)).then_inc(gains_in, 16)
                for dst, src in ((gq_dil, g_q_dil[0]), (gk_dil, g_k_dil[0])):
                    sp.dma_start(dst[:, :, :], src.partition_broadcast(P)).then_inc(gains_in, 16)
                sp.dma_start(m_mla[:, :], mla_masks).then_inc(gains_in, 16)
                sp.dma_start(m_dil[:, :, :], dil_masks.rearrange("p (g c) -> p g c", g=GROUPS)).then_inc(gains_in, 16)

            def gate_up(u0, w_gate, w_up, i):
                for j in range(KD // 2):
                    if i is None and j in (2, 3):
                        load_x(j)
                    if i is None and j == 4:
                        load_gains()
                    square(u0 + (i or 0) * FFN_BODY + j if i is None else u0 + i * FFN_BODY + j, j, w_gate, 2 * j,
                           0 if i is None else i * BANK)
                for j in range(KD // 2):
                    n = KD // 2 + j
                    square(u0 + n if i is None else u0 + i * FFN_BODY + n, n, w_up, 2 * j, 0 if i is None else i * BANK)

            def projection(u0, c0):
                for k in range(KD):
                    wide(u0 + k, k, w_in, k, c0)

            Q_COLS, K_COLS, V_COLS = (LAT + a * UNIT for a in range(3))
            sp.dma_start(ident[:, :], identity).then_inc(ident_in, 16)
            sp.dma_start(grow_1[:, :], g_ffn1[0].rearrange("(k p) -> k p", p=P)).then_inc(row1_in, 16)
            load_x(0)
            load_x(1)
            gate_up(U_GU1, w1_gate, w1_up, None)
            load_tables()
            with sp.Fori(1, FFN_TURNS) as i:
                gate_up(U_GU1, w1_gate, w1_up, i)
            with sp.Fori(0, 2) as i:
                for k in range(KF):
                    wide(U_DOWN1 + i * KF + k, k, w1_down, k, i * UNIT)
            for k in range(KD):
                wide(U_LAT + k, k, w_in, k, 0, LAT)
            projection(U_V0, V_COLS)
            for h in range(2):
                for k in range(LQ // P):
                    wide(U_UQ + h * (LQ // P) + k, k, w_uq, k, h * HQ, HQ)
            for h in range(2):
                for k in range(LKV // P):
                    wide(U_UKV + h * (LKV // P) + k, h * (LKV // P) + k, w_ukv, k, h * HK, HK)
            projection(U_V1, V_COLS + 3 * UNIT)
            projection(U_QK, Q_COLS)
            with sp.Fori(0, GROUPS - 1) as g:
                projection(U_QK + KD + g * (2 * KD), K_COLS + g * (3 * UNIT))
                projection(U_QK + 2 * KD + g * (2 * KD), Q_COLS + 3 * UNIT + g * (3 * UNIT))
            projection(U_QK + (2 * GROUPS - 1) * KD, K_COLS + (GROUPS - 1) * 3 * UNIT)
            projection(U_V2, V_COLS + (GROUPS - 1) * 3 * UNIT)
            j = 0
            for w, c0, K in ((w_in, OFF_GATE, KD), (w_in, OFF_GATE + D, KD), (w_br_mla, 0, H), (w_br_dil, 0, H)):
                for k in range(0, K, 2):
                    square(U_MERGE + j, j, w, k, c0)
                    j += 1
            with sp.Fori(1, MERGE_TURNS) as i:
                j = 0
                for w, c0, K in ((w_in, OFF_GATE, KD), (w_br_mla, 0, H), (w_in, OFF_GATE + D, KD), (w_br_dil, 0, H)):
                    for k in range(0, K, 2):
                        waits = 2 if j == KD // 2 - 1 else 0 if j == KD // 2 else 1
                        square(U_MERGE + i * MERGE_BODY + j, j, w, k, c0 + i * BANK, waits)
                        j += 1
            with sp.Fori(0, 2) as i:
                for k in range(KD):
                    wide(U_WO + i * KD + k, k, w_o, k, i * UNIT)
            with sp.Fori(0, FFN_TURNS) as i:
                gate_up(U_GU2, w2_gate, w2_up, i)
            with sp.Fori(0, 2) as i:
                for k in range(KF):
                    wide(U_DOWN2 + i * KF + k, k, w2_down, k, i * UNIT)
            j = 0
            for h in range(2):
                for k in range(KD):
                    wide(U_PLE + j, j, w_ple_gate, k, h * UNIT)
                    j += 1
                for k in range(PLE // P):
                    wide(U_PLE + j, j, w_ple_proj, k, h * UNIT)
                    j += 1
            for t in range(T):
                sp.wait_ge(res_ready, PRIMED + 12 + t + 1)
                sp.dma_start(out[0, t * P:(t + 1) * P, 0:UNIT], res[:, t, 0:UNIT]).then_inc(out_done, 16)
            for n in range(T * UNIT // BANK):
                t, c0 = n // (UNIT // BANK), UNIT + n % (UNIT // BANK) * BANK
                sp.wait_ge(out_ready, n + 1)
                sp.dma_start(out[0, t * P:(t + 1) * P, c0:c0 + BANK], res[:, t, c0:c0 + BANK]).then_inc(out_done, 16)
            sp.wait_ge(out_done, 6 * 16)

        @block.gpsimd
        def _(pool):
            for s in (gs_ready, am_ready, a_ready, res_ready, dil_turned, dil_T, dil_ready, gi_ready):
                pool.sem_inc(s, PRIMED)
            pool.memset(ones[:, :], 1.0).then_inc(ones_ready, 1)

        @block.tensor
        def _(pe):
            def wide_tile(j, t, k, hi, lo, b0, width, K):
                s = j % SLOTS
                cols = [(c, min(width, c + BANK)) for c in range(0, width, BANK)]
                xh, xl = hi[:, k, t * P:(t + 1) * P], lo[:, k, t * P:(t + 1) * P]
                for a, w, first, last in ((xh, wh, k == 0, False), (xh, wl, False, False), (xl, wh, False, k == K - 1)):
                    for m, (c, e) in enumerate(cols):
                        mm = pe.matmul(ps[:, b0 + 2 * t + m, 0:e - c], a, w[:, s, c:e], start=first, stop=last)
                return mm

            def wide_unit(n, j, k, hi, lo, b0, width, K):
                pe.wait_ge(lo_ready, n + 1)
                for t in range(T):
                    mm = wide_tile(j, t, k, hi, lo, b0, width, K)
                mm.then_inc(unit_done, 1)

            def square_unit(n, j, k, hi, lo, b0, K):
                pe.wait_ge(lo_ready, n + 1)
                s = j % SLOTS
                for kk in range(2):
                    for c in range(4):
                        w0 = kk * BANK + c * P
                        o, end = ps[:, b0 + c // 2, (c % 2) * S:(c % 2 + 1) * S], k + kk == K - 1
                        pe.matmul(o, wh[:, s, w0:w0 + P], hi[:, k + kk, :], start=(k + kk == 0 and c % 2 == 0),
                                  stop=False, skip_group_check=True)
                        pe.matmul(o, wh[:, s, w0:w0 + P], lo[:, k + kk, :], start=False, stop=False,
                                  skip_group_check=True)
                        mm = pe.matmul(o, wl[:, s, w0:w0 + P], hi[:, k + kk, :], start=False, stop=end,
                                       skip_group_check=True)
                mm.then_inc(unit_done, 1)

            def turn(src, pairs, b0):
                for n, p in enumerate(pairs):
                    for s in range(2):
                        for t in range(T):
                            mm = pe.transpose(ps[:, b0 + n, s * S + t * P:s * S + (t + 1) * P],
                                              src[:, t, (2 * p + s) * P:(2 * p + s + 1) * P], ident[:, :])
                    mm.then_inc(turned, 1)

            LEFT, RIGHT = range(KD // 4), range(KD // 4, KD // 2)

            def entry(r, j):
                if j == 0 and r:
                    pe.wait_ge(tr_lo, 2 * PAIRS[r] + KD // 2)
                if j == 2:
                    if r == 0:
                        pe.wait_ge(x_in[2], 16)
                        pe.wait_ge(x_in[3], 16)
                        pe.wait_ge(tr_lo, KD // 2)
                    else:
                        pe.wait_ge(res_ready, PRIMED + 4 * r)
                    turn(res, RIGHT, 4)
                if j == 6:
                    pe.wait_ge(diag_ready, r + 1)
                    pe.wait_ge(tr_lo, 2 * PAIRS[r] + KD // 2 + 2)
                    pe.wait_ge(ones_ready, 1)
                    pe.matmul(ps[:, 4, 0:S], ones[:, :], diag[:, :, :].rearrange("p t c -> p (t c)"),
                              start=True, stop=True).then_inc(row_turned, 1)

            def gate_up(u0, f):
                r = 2 * f
                for j in range(KD // 2):
                    entry(r, j)
                    if f == 0 and j == 4:
                        pe.wait_ge(rows_in, 16 * 7)
                        n = 3 * KD + NG + 2
                        pe.transpose(ps[:, 3, 0:n], grow_rest[:, :], ident[0:n, 0:n]).then_inc(gains_turned, 1)
                    pe.wait_ge(tr_lo, 2 * PAIRS[r] + 2 * j + 2)
                    square_unit(u0 + j, j, 2 * j, hTh, hTl, 0, KD)
                pe.wait_ge(row_ready, r + 1)
                for j in range(KD // 2):
                    square_unit(u0 + KD // 2 + j, j, 2 * j, hTh, hTl, 4, KD)
                with pe.Fori(1, FFN_TURNS) as i:
                    pe.wait_ge(gi_ready, PRIMED + f * FFN_TURNS + i)
                    for j in range(KD // 2):
                        square_unit(u0 + i * FFN_BODY + j, j, 2 * j, hTh, hTl, 0, KD)
                    pe.wait_ge(am_ready, PRIMED + f * FFN_TURNS + i)
                    for j in range(KD // 2):
                        square_unit(u0 + i * FFN_BODY + KD // 2 + j, j, 2 * j, hTh, hTl, 4, KD)

            def down(u0, hi, lo, K, r, ready, before, after):
                pe.wait_ge(ready, PRIMED + before)
                for half in range(2):
                    for k in range(K):
                        if half == 0 and k == K - 4:
                            pe.wait_ge(ready, PRIMED + after)
                        if half == 1 and k == 6:
                            pe.wait_ge(res_ready, PRIMED + 4 * (r - 1) + 2)
                            turn(res, LEFT, 0)
                        wide_unit(u0 + half * K + k, k, k, hi, lo, 4 * half, UNIT, K)

            def score(first, u, scores, bank):
                h, t = items[u]
                if u:
                    pe.wait_ge(masked, first + u)
                for c, keys, parts in scores(h, t):
                    for m, (q, k) in enumerate(parts):
                        mm = pe.matmul(flat[:, bank * BANK + c:bank * BANK + c + keys], q, k,
                                       start=(m == 0), stop=(m == len(parts) - 1))
                mm.then_inc(score_done, 1)

            def attention(first, scores, values, n_keys, prob, pT, score_bank, turned_bank, out_bank, between):

                def output(u):
                    h, t = items[u]
                    n = n_keys * (t + 1)
                    pe.wait_ge(pT_ready, first + u + 1)
                    if u >= 2:
                        pe.wait_ge(o_lo, first + u - 1)
                    for m in range(n):
                        mm = pe.matmul(ps[:, out_bank + u % 2, 0:P], values(h, t, m), pT[:, m * P:(m + 1) * P],
                                       start=(m == 0), stop=(m == n - 1))
                    mm.then_inc(pv_done, 1)

                for u, (h, t) in enumerate(items):
                    if u + 1 < len(items):
                        score(first, u + 1, scores, score_bank)
                    pe.wait_ge(prob_ready, first + u + 1)
                    if u:
                        pe.wait_ge(pT_ready, first + u)
                    for m in range(n_keys * (t + 1)):
                        mm = pe.transpose(flat[:, turned_bank * BANK + m * P:turned_bank * BANK + (m + 1) * P],
                                          prob[:, u % 2, m * P:(m + 1) * P], ident[:, :])
                    mm.then_inc(prob_turned, 1)
                    if u:
                        output(u - 1)
                    between(u)
                output(len(items) - 1)

            pe.wait_ge(ident_in, 16)
            pe.wait_ge(row1_in, 16)
            pe.transpose(ps[:, 2, 0:KD], grow_1[:, :], ident[0:KD, 0:KD]).then_inc(gains_turned, 1)
            for quarter in range(2):
                pe.wait_ge(x_in[quarter], 16)
                turn(res, LEFT[2 * quarter:2 * quarter + 2], 4 + 2 * quarter)

            gate_up(U_GU1, 0)
            down(U_DOWN1, aTh, aTl, KF, 1, a_ready, FFN_TURNS - 1, FFN_TURNS)

            for k in range(KD):
                entry(1, k)
                if k % 2 == 0:
                    pe.wait_ge(tr_lo, 2 * PAIRS[1] + k + 2)
                wide_unit(U_LAT + k, k, k, hTh, hTl, 0, LAT, KD)
            for k in range(KD):
                if k == 0:
                    pe.wait_ge(tr_lo, 2 * PAIRS[1] + KD)
                    pe.wait_ge(row_ready, 2)
                if k == 6:
                    pe.wait_ge(lat_ready, 1)
                    turn(c_tok, range(NG // 2), 0)
                wide_unit(U_V0 + k, k, k, hTh, hTl, 4, UNIT, KD)
            pe.wait_ge(tr_lo, 2 * C_PAIRS + NG)
            for h in range(2):
                if h:
                    pe.wait_ge(dil_v, 2)
                for k in range(LQ // P):
                    wide_unit(U_UQ + h * (LQ // P) + k, k, k, cTh, cTl, 4 * h, HQ, LQ // P)
            ch, cl = cTh[:, LQ // P:NG, :], cTl[:, LQ // P:NG, :]
            for h in range(2):
                pe.wait_ge(uq_tok, h + 1)
                pe.wait_ge(uq_tok_1, h + 1)
                for k in range(LKV // P):
                    wide_unit(U_UKV + h * (LKV // P) + k, h * (LKV // P) + k, k, ch, cl, 4 * h, HK, LKV // P)
            def turn_heads(heads):
                for h in heads:
                    b, c0 = 4 + h % 4, h * (NOPE + HD)
                    for t in range(T):
                        pe.transpose(ps[:, b, t * P:(t + 1) * P], q_tok[:, t, h * QK:h * QK + NOPE], ident[:, :])
                    for t in range(T):
                        mm = pe.transpose(ps[:, b, S + t * P:S + (t + 1) * P], kv_tok[:, t, c0:c0 + NOPE], ident[:, :])
                    mm.then_inc(mla_turned, 1)

            def mla_scores(h, t):
                q0, r0 = t * P, (h % 2) * ROPE
                keys = (t + 1) * P
                yield 0, keys, [(nT[:, h, 0, q0:q0 + P], nT[:, h, 1, 0:keys]),
                                (rT[r0:r0 + ROPE, 0, h // 2, q0:q0 + P], rT[r0:r0 + ROPE, 1, h // 2, 0:keys])]

            pe.wait_ge(ukv_tok, 1)
            pe.wait_ge(ukv_tok_1, 1)
            for k in range(KD):
                if k == 10:
                    pe.wait_ge(ukv_tok, 2)
                    pe.wait_ge(ukv_tok_1, 2)
                    pe.wait_ge(mla_ready, 2)
                    for a in range(2):
                        for h2 in range(H // 2):
                            for t in range(T):
                                c0 = (h2 % 2) * S + t * P
                                mm = pe.transpose(ps[:, 4 + 2 * a + h2 // 2, c0:c0 + P],
                                                  rh[:, t, a, 2 * h2:2 * h2 + 2, :].rearrange("p h c -> p (h c)"),
                                                  ident[:, :])
                        mm.then_inc(mla_turned, 1)
                if k == 12:
                    pe.wait_ge(rT_ready, 2)
                    pe.wait_ge(mla_scaled, 4)
                    turn_heads(range(H // 2))
                if k == 14:
                    pe.wait_ge(nT_even, H // 4)
                    pe.wait_ge(nT_odd, H // 4)
                    turn_heads(range(H // 2, H))
                if k == 15:
                    pe.wait_ge(nT_even, H // 2)
                    pe.wait_ge(nT_odd, H // 2)
                    score(0, 0, mla_scores, 4)
                wide_unit(U_V1 + k, k, k, hTh, hTl, 0, UNIT, KD)


            def mla_values(h, t, m):
                c0 = h * (NOPE + HD) + NOPE
                return kv_tok[:, m, c0:c0 + HD]

            def first_q(u):
                if u == 0:
                    pe.wait_ge(dil_v, 4)
                wide_unit(U_QK + u, u, u, hTh, hTl, 0, UNIT, KD)

            assert len(items) == KD
            attention(0, mla_scores, mla_values, 1, prob_m, pT_m, 4, 5, 6, first_q)

            def qk_pass(s, a, u0, at_last=None):
                for k in range(KD):
                    if k == KD - 1 and at_last:
                        at_last()
                    if k == 11:
                        pe.wait_ge(dil_ready, PRIMED + 2 * s)
                        for h in range(H):
                            for t in range(T):
                                c0 = (4 - 4 * a) * BANK + h * S + t * P
                                mm = pe.transpose(flat[:, c0:c0 + P], tok[:, t, h * HD:(h + 1) * HD], ident[:, :])
                        mm.then_inc(dil_turned, 1)
                    wide_unit(u0 + k, k, k, hTh, hTl, 4 * a, UNIT, KD)

            pe.wait_ge(o_lo, len(items))
            with pe.Fori(0, GROUPS - 1) as g:
                pe.wait_ge(dil_T, PRIMED + 4 * g)
                qk_pass(2 * g + 1, 1, U_QK + KD + g * (2 * KD))
                pe.wait_ge(dil_T, PRIMED + 4 * g + 2)
                qk_pass(2 * g + 2, 0, U_QK + 2 * KD + g * (2 * KD))
            last = 2 * GROUPS - 1
            pe.wait_ge(dil_T, PRIMED + 2 * last - 2)
            qk_pass(last, 1, U_QK + last * KD)
            def dil_scores(h, t):
                keys = (t + 1) * P
                for g in range(GROUPS):
                    q0, k0 = h * S + t * P, h * S
                    yield g * keys, keys, [(qT[:, g, q0:q0 + P], kT[:, g, k0:k0 + keys])]

            def dil_values(h, t, m):
                g, tk = m // (t + 1), m % (t + 1)
                return vd[:, g, tk * UNIT + h * HD:tk * UNIT + (h + 1) * HD]

            def first_scores():
                pe.wait_ge(dil_T, PRIMED + 4 * GROUPS)
                score(len(items), 0, dil_scores, 4)

            pe.wait_ge(dil_T, PRIMED + 2 * last)
            qk_pass(last + 1, 0, U_V2, first_scores)

            def first_gates(u):
                if u == 0:
                    pe.wait_ge(dil_v, 6)
                if u == KD // 2:
                    pe.wait_ge(gate_out, 1)
                square_unit(U_MERGE + u, u, 2 * (u % (KD // 2)), hTh, hTl, 2, KD)

            attention(len(items), dil_scores, dil_values, GROUPS, prob_d, pT_d, 4, 6, 0, first_gates)

            j = KD
            pe.wait_ge(masked, 2 * len(items))
            pe.wait_ge(pT_ready, 2 * len(items))
            for part, (hi, lo) in enumerate(((omh, oml), (odh, odl))):
                if part:
                    pe.wait_ge(o_lo, 2 * len(items))
                for k in range(0, H, 2):
                    square_unit(U_MERGE + j, j, k, hi, lo, 4 + 2 * part, H)
                    j += 1
            with pe.Fori(1, MERGE_TURNS) as i:
                j = 0
                for part, (hi, lo, K, b0) in enumerate(((hTh, hTl, KD, 2), (omh, oml, H, 4),
                                                        (hTh, hTl, KD, 0), (odh, odl, H, 6))):
                    if part == 0:
                        pe.wait_ge(mgi_ready, 2 * i)
                    if part == 1:
                        pe.wait_ge(mprod_ready, 2 * i - 1)
                    if part == 3:
                        pe.wait_ge(mprod_ready, 2 * i)
                    for k in range(0, K, 2):
                        square_unit(U_MERGE + i * MERGE_BODY + j, j, k, hi, lo, b0, K)
                        j += 1
            pe.wait_ge(mgi_ready, 2 * MERGE_TURNS)
            down(U_WO, mTh, mTl, KD, 2, m_ready, MERGE_TURNS - 1 - PRIMED, MERGE_TURNS - PRIMED)

            gate_up(U_GU2, 1)
            down(U_DOWN2, aTh, aTl, KF, 3, a_ready, 2 * FFN_TURNS - 1, 2 * FFN_TURNS)

            j = 0
            for h in range(2):
                if h:
                    pe.wait_ge(psig_ready, 2)
                for k in range(KD):
                    if h == 0:
                        entry(3, k)
                        if k % 2 == 0:
                            pe.wait_ge(tr_lo, 2 * PAIRS[3] + k + 2)
                        if k == 10:
                            pe.wait_ge(p_in, 16)
                            pe.wait_ge(tr_lo, 2 * PAIRS[3] + KD)
                            for t in range(T):
                                for c in range(PLE // P):
                                    mm = pe.transpose(ps[:, 5, c * S + t * P:c * S + (t + 1) * P],
                                                      p_tok[:, t, c * P:(c + 1) * P], ident[:, :])
                            mm.then_inc(p_turned, 1)
                    wide_unit(U_PLE + j, j, k, hTh, hTl, 0, UNIT, KD)
                    j += 1
                if h == 0:
                    pe.wait_ge(p_lo, 1)
                    pe.wait_ge(row_ready, 4)
                else:
                    pe.wait_ge(psig_used, 2)
                if h == 0:
                    for k in range(PLE // P):
                        wide_unit(U_PLE + j, j, k, pTh, pTl, 4, UNIT, PLE // P)
                        j += 1
            pe.wait_ge(lo_ready, UNITS)
            for t in range(T):
                for k in range(PLE // P):
                    mm = wide_tile(j + k, t, k, pTh, pTl, 4, UNIT, PLE // P)
                mm.then_inc(last_done, 1)

        @block.scalar
        def _(act):
            def split(n, j):
                first = isinstance(n, int) and n < SLOTS
                act.wait_ge(raw_in[j % SLOTS], ((n - j % SLOTS) * (16 // SLOTS) + 16) if not isinstance(n, int)
                            else 16 * (n // SLOTS + 1))
                if not first:
                    act.wait_ge(unit_done, n - (SLOTS - 1))
                act.activation(wh[:, j % SLOTS, :], raw[:, j % SLOTS, :], ACT.Copy).then_inc(hi_ready, 1)

            def ahead(n, j):
                split(n + SLOTS, j)

            def root(src, dst, ready, count, done):
                act.wait_ge(ready, count)
                act.activation(dst, src, ACT.Sqrt).then_inc(done, 1)

            def high(dst, g0, before, pairs, b0):
                for n, p in enumerate(pairs):
                    act.wait_ge(turned, before + p + 1)
                    for s in range(2):
                        k = 2 * p + s
                        act.activation(dst[:, k, :], ps[:, b0 + n, s * S:(s + 1) * S], ACT.Copy,
                                       scale=gcol[:, g0 + k:g0 + k + 1]).then_inc(tr_hi, 1)

            LEFT, RIGHT = range(KD // 4), range(KD // 4, KD // 2)

            def squares(r, half):
                for t in range(T):
                    if r == 0:
                        act.wait_ge(x_in[2 * half + 1], 16)
                        act.wait_ge(x_in[2 * half], 16)
                    else:
                        act.wait_ge(res_ready, PRIMED + 4 * (r - 1) + 2 * half + t + 1)
                    if 4 * r + 2 * half + t:
                        act.wait_ge(ss_ready, 4 * r + 2 * half + t)
                    c = 2 * half + t
                    act.activation(junk[:, :], res[:, t, half * UNIT:(half + 1) * UNIT], ACT.Square,
                                   accum_out=ssq[:, c:c + 1]).then_inc(ss_ready, 1)

            def entry(r, j):
                if j == 0:
                    squares(r, 1)
                if j == 1:
                    high(hTh, r * KD, PAIRS[r], RIGHT, 4)
                if j == 2:
                    root(var, dev, var_ready, r + 1, dev_ready)

            def gate_up(u0, f):
                def turn(i, j):
                    if j == KD // 2 - 1:
                        act.wait_ge(gi_ready, PRIMED + f * FFN_TURNS + i + 1)
                        act.activation(sg[:, :, :], gs[:, :, :], ACT.Sigmoid).then_inc(sig_ready, 1)
                    if j == FFN_BODY - 1:
                        act.wait_ge(am_ready, PRIMED + f * FFN_TURNS + i + 1)
                        act.activation(aTh[:, ds(i * 4, 4), :], gs[:, :, :], ACT.Copy).then_inc(ah_ready, 1)

                for j in range(FFN_BODY):
                    ahead(u0 + j, j)
                    entry(2 * f, j)
                    if f == 0 and j == 4:
                        act.wait_ge(gains_turned, 2)
                        act.activation(gcol[:, KD:], ps[:, 3, 0:3 * KD + NG + 2], ACT.Copy).then_inc(gcol_ready, 1)
                    turn(0, j)
                with act.Fori(1, FFN_TURNS) as i:
                    for j in range(FFN_BODY):
                        ahead(u0 + i * FFN_BODY + j, j)
                        turn(i, j)

            def down(u0, K, r, meanwhile=None):
                for half in range(2):
                    for k in range(K):
                        ahead(u0 + half * K + k, k)
                        if half == 0 and meanwhile:
                            meanwhile(k)
                        if half == 1 and k == 5:
                            squares(r, 0)
                        if half == 1 and k in (6, 8, 10, 12):
                            high(hTh, r * KD, PAIRS[r], LEFT[k // 2 - 3:k // 2 - 2], k // 2 - 3)

            def v_tile(g, b0):
                act.wait_ge(unit_done, (U_V0, U_V1, U_V2)[g] + KD)
                act.activation(vd[:, g, 0:UNIT], banks(b0, UNIT), ACT.Copy, scale=inv[:, 0:1]).then_inc(dil_v, 1)

            def square_heads(t, src, step, width):
                a = 0 if src is q_tok else 1
                if 2 * a + t:
                    act.wait_ge(mla_sq, 2 * a + t)
                if a == 0:
                    act.wait_ge(uq_tok, 2)
                    act.wait_ge(uq_tok_1, 2)
                elif t:
                    act.wait_ge(ukv_tok_1, 2)
                for h in range(H):
                    c = (a * T + t) * H + h
                    last = act.activation(sq[:, h * width:(h + 1) * width], src[:, t, h * step:h * step + width],
                                          ACT.Square, accum_out=mss[:, c:c + 1])
                last.then_inc(mla_sq, 1)

            def exp(first, u, prob, n_keys, scale):
                h, t = items[u]
                n = n_keys * (t + 1) * P
                act.wait_ge(masked, first + u + 1)
                act.activation(prob[:, u % 2, 0:n], prob[:, u % 2, 0:n], ACT.Exp, bias=s_bias[:, u:u + 1],
                               scale=scale, accum_out=s_sum[:, u:u + 1]).then_inc(exp_done, 1)

            def attention(first, prob, pT, oh, n_keys, scale, turned_bank, out_bank, between):
                def out_high(u):
                    h, t = items[u]
                    act.wait_ge(pv_done, first + u + 1)
                    act.activation(oh[:, h, t * P:(t + 1) * P], ps[:, out_bank + u % 2, 0:P], ACT.Copy)\
                       .then_inc(o_hi, 1)

                for u, (h, t) in enumerate(items):
                    if u:
                        between(u - 1)
                    n = n_keys * (t + 1) * P
                    act.wait_ge(prob_turned, first + u + 1)
                    if u:
                        act.wait_ge(pv_done, first + u)
                    act.activation(pT[:, 0:n], banks(turned_bank, n), ACT.Copy).then_inc(pT_ready, 1)
                    if u + 1 < len(items):
                        exp(first, u + 1, prob, n_keys, scale)
                    if u:
                        out_high(u - 1)
                out_high(len(items) - 1)
                between(len(items) - 1)

            act.wait_ge(gains_turned, 1)
            act.activation(gcol[:, 0:KD], ps[:, 2, 0:KD], ACT.Copy).then_inc(gcol_ready, 1)
            act.wait_ge(gcol_ready, 1)
            for n in range(SLOTS):
                high(hTh, 0, PAIRS[0], LEFT[n:n + 1], 4 + n)
                split(n, n)
            squares(0, 0)
            gate_up(U_GU1, 0)
            def tables(k):
                if k in (2, 4, 6, 8):
                    n = k // 2 - 1
                    act.wait_ge(angles_ready, n + 1)
                    act.activation((sin, cos)[n % 2][:, n // 2, :], turns[:, :], ACT.Sin).then_inc(tables_ready, 1)

            down(U_DOWN1, KF, 1, tables)

            for k in range(KD):
                ahead(U_LAT + k, k)
                entry(1, k)
            act.wait_ge(inv_ready, 2)
            for t in range(T):
                act.activation(c_tok[:, t, :], banks(2 * t, LAT), ACT.Copy, scale=inv[:, t:t + 1]).then_inc(lat_tok, 1)
            act.wait_ge(lat_tok, T)
            for t in range(T):
                for a, (c0, c1) in enumerate(((0, LQ), (LQ, LQ + LKV), (LQ + LKV, LAT))):
                    total = css[:, 2 * t + a:2 * t + a + 1] if a < 2 else kss_m[:, t:t + 1]
                    src = flat[:, 2 * t * BANK + c0:2 * t * BANK + c1]
                    act.activation(src, c_tok[:, t, c0:c1], ACT.Square, accum_out=total).then_inc(lat_ss, 1)
            for k in range(KD):
                if k == KD - 1:
                    v_tile(0, 4)
                ahead(U_V0 + k, k)
                if k == 1:
                    root(cvar, cdev, lat_var, 2, lat_dev)
                if k == 6:
                    high(cTh, 4 * KD, C_PAIRS, range(NG // 2), 0)
            for h in range(2):
                for k in range(LQ // P):
                    ahead(U_UQ + h * (LQ // P) + k, k)
                act.activation(q_tok[:, 0, h * HQ:(h + 1) * HQ], banks(4 * h, HQ), ACT.Copy).then_inc(uq_tok, 1)
            for h in range(2):
                for k in range(LKV // P):
                    ahead(U_UKV + h * (LKV // P) + k, h * (LKV // P) + k)
                    if k == 0:
                        square_heads(h, q_tok, QK, QK)
                act.activation(kv_tok[:, 0, h * HK:(h + 1) * HK], banks(4 * h, HK), ACT.Copy).then_inc(ukv_tok, 1)
            for k in range(KD):
                if k == KD - 1:
                    v_tile(1, 0)
                ahead(U_V1 + k, k)
                if k < 2:
                    if k == 0:
                        act.wait_ge(ukv_tok, 2)
                    square_heads(k, kv_tok, NOPE + HD, NOPE)
                if k == 2:
                    root(mvar, mdev, mla_var, 1, mla_dev)
                if k in (3, 4, 5, 6):
                    if k == 3:
                        act.wait_ge(mla_inv, 1)
                    t, a = (k - 3) // 2, (k - 3) % 2
                    for h in range(H):
                        c = (a * T + t) * H + h
                        src, step = ((q_tok, QK), (kv_tok, NOPE + HD))[a]
                        v = src[:, t, h * step:h * step + NOPE]
                        last = act.activation(v, v, ACT.Copy, scale=minv[:, c:c + 1])
                    last.then_inc(mla_scaled, 1)
                if k in (11, 13):
                    for h in range((k - 11) * 2, (k - 11) * 2 + 4, 2):
                        act.wait_ge(mla_turned, 2 + h + 1)
                        for a in range(2):
                            ins = act.activation(nT[:, h, a, :], ps[:, 4 + h % 4, a * S:(a + 1) * S], ACT.Copy,
                                                 scale=gcol[:, 4 * KD + NG + a:4 * KD + NG + a + 1])
                        ins.then_inc(nT_even, 1)
                if k == KD - 2:
                    exp(0, 0, prob_m, 1, SCALE_MLA)
            attention(0, prob_m, pT_m, omh, 1, SCALE_MLA, 5, 6, lambda u: ahead(U_QK + u, u))

            def evict(s, a):
                act.wait_ge(dil_turned, PRIMED + s)
                for t in range(T):
                    act.activation(tok[:, t, :], banks(4 * a + 2 * t, UNIT), ACT.Copy, scale=inv[:, t:t + 1])\
                       .then_inc(dil_tok, 1)
                act.wait_ge(dil_tok, 2 * s + 2)
                for t in range(T):
                    act.activation(banks(4 * a + 2 * t, UNIT), tok[:, t, :], ACT.Square).then_inc(dil_sq, 1)

            def follow(s, a, g, k):
                if k == 2:
                    root(dvar, ddev, dil_var, s + 1, dil_dev)
                if k == 11:
                    act.wait_ge(dil_turned, PRIMED + s + 1)
                    for e in range(2):
                        act.activation((qT, kT)[a][:, ds(g, 1), e * UNIT:(e + 1) * UNIT].rearrange("p a c -> p (a c)"),
                                       banks(4 * a + 2 * e, UNIT), ACT.Copy).then_inc(dil_T, 1)

            evict(0, 0)
            with act.Fori(0, GROUPS - 1) as g:
                for k in range(KD):
                    ahead(U_QK + KD + g * (2 * KD) + k, k)
                    follow(2 * g, 0, g, k)
                evict(2 * g + 1, 1)
                for k in range(KD):
                    ahead(U_QK + 2 * KD + g * (2 * KD) + k, k)
                    follow(2 * g + 1, 1, g, k)
                evict(2 * g + 2, 0)
            last = 2 * GROUPS - 1
            for k in range(KD):
                ahead(U_QK + last * KD + k, k)
                follow(last - 1, 0, GROUPS - 1, k)
            evict(last, 1)
            for k in range(KD):
                if k == KD - 1:
                    v_tile(GROUPS - 1, 0)
                ahead(U_V2 + k, k)
                follow(last, 1, GROUPS - 1, k)
                if k == KD - 2:
                    exp(len(items), 0, prob_d, GROUPS, SCALE_DIL)

            def first_gates(u):
                ahead(U_MERGE + u, u)
                if u == KD // 2 - 1:
                    act.wait_ge(unit_done, U_MERGE + KD // 2)
                    act.activation(sg_first[:, :, :], quad(2), ACT.Copy).then_inc(gate_out, 1)

            attention(len(items), prob_d, pT_d, odh, GROUPS, SCALE_DIL, 6, 0, first_gates)

            def gate(n, dst):
                act.wait_ge(mgi_ready, n)
                act.activation(dst[:, :, :], dst[:, :, :], ACT.Sigmoid).then_inc(msig_ready, 1)

            def merged(i):
                act.wait_ge(m_sum, i + 1)
                act.activation(mTh[:, ds(i * 4, 4), :], gs[:, :, :], ACT.Copy).then_inc(mh_ready, 1)

            gate(1, sg_first)
            for j in range(KD, MERGE_BODY):
                ahead(U_MERGE + j, j)
                if j == KD:
                    gate(2, sg)
            merged(0)
            with act.Fori(1, MERGE_TURNS) as i:
                for j in range(MERGE_BODY):
                    ahead(U_MERGE + i * MERGE_BODY + j, j)
                    for a in range(2):
                        if j == a * (MERGE_BODY // 2) + KD // 2 - 1:
                            gate(2 * i + a + 1, sg)
                    if j == MERGE_BODY - 1:
                        merged(i)
            down(U_WO, KD, 2)
            gate_up(U_GU2, 1)
            down(U_DOWN2, KF, 3)

            act.wait_ge(unit_done, U_PLE)
            act.dma_start(p_tok[:, :, :], p[0, 0].rearrange("(t p) c -> p t c", p=P)).then_inc(p_in, 16)
            j = 0
            for h in range(2):
                for k in range(KD + PLE // P):
                    if U_PLE + j + SLOTS < UNITS:
                        ahead(U_PLE + j, j)
                    if h == 0:
                        entry(3, k)
                    if h == 0 and k == 10:
                        act.wait_ge(p_turned, 1)
                        act.activation(pTh[:, :, :], ps[:, 5, :].rearrange("p (k s) -> p k s", s=S), ACT.Copy).then_inc(p_hi, 1)
                    if k == KD - 1:
                        act.wait_ge(unit_done, U_PLE + j + 1)
                        if h == 0:
                            act.wait_ge(inv_ready, 4)
                        for t in range(T):
                            if h:
                                act.wait_ge(res_ready, PRIMED + 12 + t + 1)
                            act.activation(sgp[:, t, :], banks(2 * t, UNIT), ACT.Sigmoid, scale=inv[:, t:t + 1])\
                               .then_inc(psig_ready, 1)
                    j += 1

        @block.vector
        def _(dve):
            chain = Chain(dve, dve_step)

            def split(n, j):
                dve.wait_ge(hi_ready, n + 1)
                dve.tensor_tensor(wl[:, j % SLOTS, :], raw[:, j % SLOTS, :], wh[:, j % SLOTS, :].bitcast(F32),
                                  ALU.subtract).then_inc(lo_ready, 1)

            def ahead(n, j):
                split(n + SLOTS, j)

            def rsqrt(v, s, y, tmp, ready, count):
                dve.wait_ge(ready, count)
                chain(dve.reciprocal(y, s))
                chain(dve.scalar_tensor_tensor(out=tmp, in0=y, scalar=-0.5, in1=y, op0=ALU.mult, op1=ALU.mult))
                chain(dve.tensor_tensor(tmp, tmp, v, ALU.mult))
                return dve.scalar_tensor_tensor(out=y, in0=tmp, scalar=1.5, in1=y, op0=ALU.add, op1=ALU.mult)

            def rest(dst, hi, g0, before, pairs, b0):
                for n, p in enumerate(pairs):
                    dve.wait_ge(tr_hi, 2 * (before + p) + 2)
                    for s in range(2):
                        k = 2 * p + s
                        dve.scalar_tensor_tensor(out=dst[:, k, :], in0=ps[:, b0 + n, s * S:(s + 1) * S],
                                                 scalar=gcol[:, g0 + k:g0 + k + 1], in1=hi[:, k, :].bitcast(F32),
                                                 op0=ALU.mult, op1=ALU.subtract).then_inc(tr_lo, 1)

            LEFT, RIGHT = range(KD // 4), range(KD // 4, KD // 2)

            def entry(r, j):
                if j == 1:
                    rest(hTl, hTh, r * KD, PAIRS[r], RIGHT, 4)
                if j == 2:
                    dve.wait_ge(ss_ready, 4 * r + 4)
                    chain(dve.tensor_tensor(var, ssq[:, 0:2], ssq[:, 2:4], ALU.add))
                    dve.tensor_scalar(var, var, 1.0 / D, EPS, ALU.mult, ALU.add).then_inc(var_ready, 1)
                    rsqrt(var, dev, inv, nwt, dev_ready, r + 1).then_inc(inv_ready, 1)
                    dve.wait_ge(inv_ready, r + 1)
                    for t in range(T):
                        ins = dve.tensor_scalar(diag[:, t, :], ident[:, :], inv[:, t:t + 1], None, ALU.mult)
                    ins.then_inc(diag_ready, 1)
                if j == 6:
                    dve.wait_ge(row_turned, r + 1)
                    dve.tensor_copy(inv_row[:, :], ps[:, 4, 0:S]).then_inc(row_ready, 1)
                    dve.wait_ge(row_ready, r + 1)

            rms4 = inv_row[:, :].unsqueeze(1).to_broadcast([P, 4, S])

            def gate_up(u0, f):
                def turn(i, j, n):
                    if j == KD // 2 - 1:
                        dve.wait_ge(unit_done, n + 1)
                        dve.wait_ge(a_ready, PRIMED + f * FFN_TURNS + i)
                        dve.tensor_tensor(gs[:, :, :], quad(0), rms4, ALU.mult).then_inc(gi_ready, 1)
                    if j == KD // 2:
                        dve.wait_ge(sig_ready, f * FFN_TURNS + i + 1)
                        chain(dve.tensor_tensor(gs[:, :, :], gs[:, :, :], sg[:, :, :], ALU.mult))
                        dve.tensor_tensor(gs[:, :, :], gs[:, :, :], rms4, ALU.mult).then_inc(gs_ready, 1)
                    if j == FFN_BODY - 1:
                        dve.wait_ge(unit_done, n + 1)
                        dve.wait_ge(gs_ready, PRIMED + f * FFN_TURNS + i + 1)
                        dve.tensor_tensor(gs[:, :, :], quad(4), gs[:, :, :], ALU.mult).then_inc(am_ready, 1)
                        dve.wait_ge(ah_ready, f * FFN_TURNS + i + 1)
                        dve.tensor_tensor(aTl[:, ds(i * 4, 4), :], gs[:, :, :],
                                          aTh[:, ds(i * 4, 4), :].bitcast(F32), ALU.subtract).then_inc(a_ready, 1)

                for j in range(FFN_BODY):
                    ahead(u0 + j, j)
                    entry(2 * f, j)
                    turn(0, j, u0 + j)
                with dve.Fori(1, FFN_TURNS) as i:
                    chain.enter(i - 1, 1)
                    for j in range(FFN_BODY):
                        ahead(u0 + i * FFN_BODY + j, j)
                        turn(i, j, u0 + i * FFN_BODY + j)
                    chain.leave(FFN_TURNS - 1)

            def down(u0, K, r, factor, meanwhile=None):
                for half in range(2):
                    for k in range(K):
                        if k == K - 1:
                            dve.wait_ge(unit_done, u0 + half * K + K)
                            for t in range(T):
                                part = res[:, t, half * UNIT:(half + 1) * UNIT]
                                dve.scalar_tensor_tensor(out=part, in0=banks(4 * half + 2 * t, UNIT), scalar=factor,
                                                         in1=part, op0=ALU.mult, op1=ALU.add).then_inc(res_ready, 1)
                        ahead(u0 + half * K + k, k)
                        if half == 0 and meanwhile:
                            meanwhile(k)
                        if half == 1 and k in (6, 8, 10, 12):
                            rest(hTl, hTh, r * KD, PAIRS[r], LEFT[k // 2 - 3:k // 2 - 2], k // 2 - 3)

            def rotate(x1, x2, c, s, a, b):
                dve.tensor_tensor(a, x2, s, ALU.mult)
                chain(dve.tensor_tensor(b, x1, s, ALU.mult))
                dve.tensor_tensor(x1, x1, c, ALU.mult)
                chain(dve.tensor_tensor(x2, x2, c, ALU.mult))
                dve.tensor_tensor(x1, x1, a, ALU.subtract)
                return dve.tensor_tensor(x2, x2, b, ALU.add)

            def v_tile(g, b0):
                dve.wait_ge(unit_done, (U_V0, U_V1, U_V2)[g] + KD)
                dve.tensor_scalar(vd[:, g, UNIT:2 * UNIT], banks(b0 + 2, UNIT), inv[:, 1:2], None, ALU.mult)\
                   .then_inc(dil_v, 1)

            def mask(first, u, prob, masks, n_keys, scale, bank):
                h, t = items[u]
                n = n_keys * (t + 1) * P
                dve.wait_ge(score_done, first + u + 1)
                if u >= 2:
                    dve.wait_ge(prob_turned, first + u - 1)
                a = prob[:, u % 2, 0:n].rearrange("p (g c) -> p g c", g=n_keys)
                s = banks(bank, n).rearrange("p (g c) -> p g c", g=n_keys)
                chain(dve.tensor_tensor_reduce(a, s, masks(t), 1.0, -3.0e38, ALU.add, ALU.max, s_max[:, u:u + 1]))
                dve.tensor_scalar(s_bias[:, u:u + 1], s_max[:, u:u + 1], -scale, None, ALU.mult).then_inc(masked, 1)

            def norm(first, u, prob, n_keys):
                h, t = items[u]
                n = n_keys * (t + 1) * P
                dve.wait_ge(exp_done, first + u + 1)
                chain(dve.reciprocal(s_inv[:, u:u + 1], s_sum[:, u:u + 1]))
                dve.tensor_scalar(prob[:, u % 2, 0:n], prob[:, u % 2, 0:n], s_inv[:, u:u + 1], None, ALU.mult)\
                   .then_inc(prob_ready, 1)

            def attention(first, prob, masks, ol, oh, n_keys, scale, score_bank, out_bank, between):
                def out_rest(u):
                    h, t = items[u]
                    dve.wait_ge(o_hi, first + u + 1)
                    dve.tensor_tensor(ol[:, h, t * P:(t + 1) * P], ps[:, out_bank + u % 2, 0:P],
                                      oh[:, h, t * P:(t + 1) * P].bitcast(F32), ALU.subtract).then_inc(o_lo, 1)

                for u in range(len(items)):
                    if u + 1 < len(items):
                        mask(first, u + 1, prob, masks, n_keys, scale, score_bank)
                    if u:
                        between(u - 1)
                    if u + 1 < len(items):
                        norm(first, u + 1, prob, n_keys)
                    if u >= 2:
                        out_rest(u - 2)
                out_rest(len(items) - 2)
                out_rest(len(items) - 1)
                between(len(items) - 1)

            for n in range(SLOTS):
                rest(hTl, hTh, 0, PAIRS[0], LEFT[n:n + 1], 4 + n)
                split(n, n)
            gate_up(U_GU1, 0)

            def angles(k):
                if k == 0:
                    dve.wait_ge(consts_in, 16 * 2)
                    chain(dve.tensor_copy(pos_f[:, :], pos_i[:, :]))
                if k in (1, 3, 5, 7):
                    n = k // 2
                    t, quarter = n // 2, (n % 2) * 0.25
                    if n:
                        dve.wait_ge(angles_ready, n)
                    chain(dve.tensor_scalar(angle[:, :], freq[:, :], pos_f[:, t:t + 1], None, ALU.mult))
                    if n:
                        dve.wait_ge(tables_ready, n)
                    chain(dve.tensor_scalar(turns[:, :], angle[:, :], 0.15915494309189535, quarter, ALU.mult, ALU.add))
                    chain(dve.tensor_scalar(turns[:, :], turns[:, :], ROUND, -ROUND, ALU.add, ALU.add))
                    for part in (TWO_PI_1, TWO_PI_2, TWO_PI_3):
                        chain(dve.scalar_tensor_tensor(out=angle[:, :], in0=turns[:, :], scalar=-part,
                                                       in1=angle[:, :], op0=ALU.mult, op1=ALU.add))
                    chain(dve.tensor_scalar(angle[:, :], angle[:, :], quarter * 6.283185307179586, PI_DOWN,
                                            ALU.add, ALU.min))
                    dve.tensor_scalar(turns[:, :], angle[:, :], -PI_DOWN, None, ALU.max).then_inc(angles_ready, 1)

            down(U_DOWN1, KF, 1, 0.5, angles)

            half = ROPE // 2
            for k in range(KD):
                ahead(U_LAT + k, k)
                entry(1, k)
            for k in range(KD):
                if k == KD - 1:
                    v_tile(0, 4)
                ahead(U_V0 + k, k)
                if k == 8:
                    dve.wait_ge(gains_in, 16 * 6)
                    g_rot = gk_mla[:, NOPE:QK].unsqueeze(1).to_broadcast([P, T, ROPE])
                    chain(dve.tensor_tensor(k_rot[:, :, :], c_tok[:, :, LQ + LKV:LAT], g_rot, ALU.mult))
                    chain(rotate(k_rot[:, :, 0:half], k_rot[:, :, half:ROPE], cos[:, :, 0:half], sin[:, :, 0:half],
                                 tmpA[:, 0:T, :], tmpB[:, 0:T, :]))
                if k == 1:
                    dve.wait_ge(lat_ss, 6)
                    cs, cv = (a.rearrange("p (t a) -> p t a", a=2) for a in (css, cvar))
                    dve.tensor_scalar(cv[:, :, 0], cs[:, :, 0], 1.0 / LQ, EPS, ALU.mult, ALU.add).then_inc(lat_var, 1)
                    dve.tensor_scalar(cv[:, :, 1], cs[:, :, 1], 1.0 / LKV, EPS, ALU.mult, ALU.add).then_inc(lat_var, 1)
                    dve.wait_ge(lat_var, 2)
                    chain(rsqrt(cvar, cdev, cinv, cnwt, lat_dev, 1))
                if k == 2:
                    for t in range(T):
                        for a, (c0, c1) in enumerate(((0, LQ), (LQ, LQ + LKV))):
                            ins = dve.tensor_scalar(c_tok[:, t, c0:c1], c_tok[:, t, c0:c1],
                                                    cinv[:, 2 * t + a:2 * t + a + 1], None, ALU.mult)
                    ins.then_inc(lat_ready, 1)
                if k == 6:
                    rest(cTl, cTh, 4 * KD, C_PAIRS, range(NG // 2), 0)
            for n in range(2 * (LQ // P)):
                ahead(U_UQ + n, n)
                if (n + 1) % (LQ // P) == 0:
                    h = n // (LQ // P)
                    dve.tensor_copy(q_tok[:, 1, h * HQ:(h + 1) * HQ], banks(4 * h + 2, HQ)).then_inc(uq_tok_1, 1)
            for n in range(2 * (LKV // P)):
                ahead(U_UKV + n, n)
                if (n + 1) % (LKV // P) == 0:
                    h = n // (LKV // P)
                    dve.tensor_copy(kv_tok[:, 1, h * HK:(h + 1) * HK], banks(4 * h + 2, HK)).then_inc(ukv_tok_1, 1)

            def mla_mask(t):
                return m_mla[:, (1 - t) * P:2 * P].unsqueeze(1)

            ms = mss.rearrange("p (a t h) -> p a t h", a=2, t=T)
            mi = minv.rearrange("p (a t h) -> p a t h", a=2, t=T)

            def gain(g, a, e):
                return g[:, a:e].unsqueeze(1).to_broadcast([P, H, e - a])

            for k in range(KD):
                if k == KD - 1:
                    v_tile(1, 0)
                ahead(U_V1 + k, k)
                if k < T:
                    qr = rh[:, k, 0, :, :]
                    q_rot = q_tok[:, k, :].rearrange("p (h c) -> p h c", h=H)[:, :, NOPE:QK]
                    c, s = (b[:, k, 0:half].unsqueeze(1).to_broadcast([P, H, half]) for b in (cos, sin))
                    if k == 0:
                        dve.wait_ge(uq_tok, 2)
                        dve.wait_ge(uq_tok_1, 2)
                    chain(dve.tensor_tensor(qr, q_rot, gain(gq_mla, NOPE, QK), ALU.mult))
                    rotate(qr[:, :, 0:half], qr[:, :, half:ROPE], c, s, tmpA[:, :, :], tmpB[:, :, :])\
                        .then_inc(q_rotated, 1)
                    dve.wait_ge(q_rotated, k + 1)
                if k == 2:
                    dve.wait_ge(mla_sq, 4)
                    for t in range(T):
                        ins = dve.tensor_scalar(ms[:, 1, t, :], ms[:, 1, t, :], kss_m[:, t:t + 1], None, ALU.add)
                    chain(ins)
                    dve.tensor_scalar(mvar, mss, 1.0 / QK, EPS, ALU.mult, ALU.add).then_inc(mla_var, 1)
                    dve.wait_ge(mla_var, 1)
                    rsqrt(mvar, mdev, minv, mnwt, mla_dev, 1).then_inc(mla_inv, 1)
                    dve.wait_ge(mla_inv, 1)
                if k in (4, 5):
                    t = k - 4
                    iq, ik = (mi[:, a, t, :].unsqueeze(2).to_broadcast([P, H, ROPE]) for a in range(2))
                    dve.tensor_tensor(rh[:, t, 0, :, :], rh[:, t, 0, :, :], iq, ALU.mult)
                    dve.tensor_tensor(rh[:, t, 1, :, :], k_rot[:, t, :].unsqueeze(1).to_broadcast([P, H, ROPE]), ik,
                                      ALU.mult).then_inc(mla_ready, 1)
                if k == 9:
                    for a in range(2):
                        dve.wait_ge(mla_turned, a + 1)
                        dve.tensor_copy(rT[:, a, :, :].rearrange("p h s -> p (h s)"), banks(4 + 2 * a, UNIT))\
                           .then_inc(rT_ready, 1)
                if k in (11, 13):
                    for h in range((k - 11) * 2 + 1, (k - 11) * 2 + 5, 2):
                        dve.wait_ge(mla_turned, 2 + h + 1)
                        for a in range(2):
                            ins = dve.tensor_scalar(nT[:, h, a, :], ps[:, 4 + h % 4, a * S:(a + 1) * S],
                                                    gcol[:, 4 * KD + NG + a:4 * KD + NG + a + 1], None, ALU.mult)
                        ins.then_inc(nT_odd, 1)
                if k == KD - 2:
                    mask(0, 0, prob_m, mla_mask, 1, SCALE_MLA, 4)
                    norm(0, 0, prob_m, 1)
            attention(0, prob_m, mla_mask, oml, omh, 1, SCALE_MLA, 4, 6, lambda u: ahead(U_QK + u, u))

            di = dinv.rearrange("p (t h) -> p t h", t=T)

            def follow(s, a, g, k):
                if k == 0:
                    for t in range(T):
                        dve.wait_ge(dil_sq, 2 * s + t + 1)
                        dve.tensor_reduce(dss[:, t * H:(t + 1) * H], banks(4 * a + 2 * t, UNIT)
                                          .rearrange("p (h c) -> p h c", h=H), AX_X, ALU.add).then_inc(dil_ss, 1)
                if k == 2:
                    dve.wait_ge(dil_ss, 2 * s + 2)
                    dve.tensor_scalar(dvar, dss, 1.0 / HD, EPS, ALU.mult, ALU.add).then_inc(dil_var, 1)
                    dve.wait_ge(dil_var, s + 1)
                    chain(rsqrt(dvar, ddev, dinv, dnwt, dil_dev, s + 1))
                for t in range(T):
                    if k == 3 + 2 * t:
                        gains = (gq_dil, gk_dil)[a][:, ds(g, 1), :].rearrange("p a c -> p (a c)")
                        for h in range(H):
                            v = tok[:, t, h * HD:(h + 1) * HD]
                            ins = dve.scalar_tensor_tensor(out=v, in0=v, scalar=di[:, t, h:h + 1], in1=gains,
                                                           op0=ALU.mult, op1=ALU.mult)
                        chain(ins)
                    if k == 4 + 2 * t:
                        v = tok[:, t, :].rearrange("p (h c) -> p h c", h=H)
                        hf = ROT // 2
                        c, sn = (b[:, t, NF - hf:NF].unsqueeze(1).to_broadcast([P, H, hf]) for b in (cos, sin))
                        dve.wait_ge(dil_ready, PRIMED + 2 * s + t)
                        rotate(v[:, :, 0:hf], v[:, :, hf:ROT], c, sn, ropeA[:, :, :], ropeB[:, :, :])\
                            .then_inc(dil_ready, 1)

            def dil_mask(t):
                return m_dil[:, :, (1 - t) * P:2 * P]

            FOLLOW_STEPS = 4 + T * 3
            with dve.Fori(0, GROUPS - 1) as g:
                chain.enter(g, 2 * FOLLOW_STEPS)
                for k in range(KD):
                    ahead(U_QK + KD + g * (2 * KD) + k, k)
                    follow(2 * g, 0, g, k)
                for k in range(KD):
                    ahead(U_QK + 2 * KD + g * (2 * KD) + k, k)
                    follow(2 * g + 1, 1, g, k)
                chain.leave(GROUPS - 1)
            last = 2 * GROUPS - 1
            for k in range(KD):
                ahead(U_QK + last * KD + k, k)
                follow(last - 1, 0, GROUPS - 1, k)
            for k in range(KD):
                if k == KD - 1:
                    v_tile(GROUPS - 1, 0)
                ahead(U_V2 + k, k)
                follow(last, 1, GROUPS - 1, k)
                if k == KD - 2:
                    mask(len(items), 0, prob_d, dil_mask, GROUPS, SCALE_DIL, 4)
                    norm(len(items), 0, prob_d, GROUPS)

            def gate(n, b0, dst, units):
                dve.wait_ge(unit_done, units)
                dve.tensor_tensor(dst[:, :, :], quad(b0), rms4, ALU.mult).then_inc(mgi_ready, 1)

            attention(len(items), prob_d, dil_mask, odl, odh, GROUPS, SCALE_DIL, 4, 0,
                      lambda u: ahead(U_MERGE + u, u))
            dve.wait_ge(gate_out, 1)
            dve.tensor_tensor(sg_first[:, :, :], sg_first[:, :, :], rms4, ALU.mult).then_inc(mgi_ready, 1)
            dve.wait_ge(prob_turned, 2 * len(items))
            dve.wait_ge(prob_ready, 2 * len(items))
            gate(2, 2, sg, U_MERGE + KD)

            def product(n, b0, src, dst, units):
                dve.wait_ge(msig_ready, n)
                dve.wait_ge(unit_done, units)
                dve.tensor_tensor(dst[:, :, :], quad(b0), src[:, :, :], ALU.mult).then_inc(mprod_ready, 1)

            def merged(i):
                dve.wait_ge(mprod_ready, 2 * i + 2)
                dve.tensor_tensor(gs[:, :, :], gs[:, :, :], am[:, :, :], ALU.add).then_inc(m_sum, 1)
                dve.wait_ge(mh_ready, i + 1)
                dve.tensor_tensor(mTl[:, ds(i * 4, 4), :], gs[:, :, :],
                                  mTh[:, ds(i * 4, 4), :].bitcast(F32), ALU.subtract).then_inc(m_ready, 1)

            for j in range(KD, MERGE_BODY):
                ahead(U_MERGE + j, j)
                if j == KD + H // 2 - 1:
                    dve.wait_ge(pv_done, 2 * len(items))
                    product(1, 4, sg_first, gs, U_MERGE + j + 1)
                if j == MERGE_BODY - 1:
                    product(2, 6, sg, am, U_MERGE + j + 1)
            merged(0)
            with dve.Fori(1, MERGE_TURNS) as i:
                for j in range(MERGE_BODY):
                    ahead(U_MERGE + i * MERGE_BODY + j, j)
                    for a in range(2):
                        if j == a * (MERGE_BODY // 2) + KD // 2 - 1:
                            dve.wait_ge(mprod_ready, 2 * i + a)
                            gate(2 * i + a + 1, (2, 0)[a], sg, U_MERGE + i * MERGE_BODY + j + 1)
                        if j == (a + 1) * (MERGE_BODY // 2) - 1:
                            if a == 0:
                                dve.wait_ge(m_ready, i)
                            product(2 * i + a + 1, (4, 6)[a], sg, (gs, am)[a], U_MERGE + i * MERGE_BODY + j + 1)
                merged(i)
            down(U_WO, KD, 2, 1.0)
            gate_up(U_GU2, 1)
            down(U_DOWN2, KF, 3, 0.5)

            j = 0
            for h in range(2):
                for k in range(KD + PLE // P):
                    if U_PLE + j + SLOTS < UNITS:
                        ahead(U_PLE + j, j)
                    if h == 0:
                        entry(3, k)
                    if h == 0 and k == 10:
                        dve.wait_ge(p_hi, 1)
                        dve.tensor_tensor(pTl[:, :, :], ps[:, 5, :].rearrange("p (k s) -> p k s", s=S),
                                          pTh[:, :, :].bitcast(F32), ALU.subtract).then_inc(p_lo, 1)
                    j += 1
                if h == 0:
                    dve.wait_ge(unit_done, U_PLE + j)
                    for t in range(T):
                        dve.wait_ge(psig_ready, t + 1)
                        part, dst = sgp[:, t, :], res[:, t, 0:UNIT]
                        dve.tensor_tensor(part, part, banks(4 + 2 * t, UNIT), ALU.mult).then_inc(psig_used, 1)
                        dve.wait_ge(psig_used, t + 1)
                        dve.tensor_tensor(dst, dst, part, ALU.add).then_inc(res_ready, 1)
            for t in range(T):
                dve.wait_ge(last_done, t + 1)
                dve.wait_ge(psig_ready, T + t + 1)
                for m in range(UNIT // BANK):
                    part = sgp[:, t, m * BANK:(m + 1) * BANK]
                    dst = res[:, t, UNIT + m * BANK:UNIT + (m + 1) * BANK]
                    dve.tensor_tensor(part, part, ps[:, 4 + 2 * t + m, :], ALU.mult).then_inc(last_used, 1)
                    dve.wait_ge(last_used, t * (UNIT // BANK) + m + 1)
                    dve.tensor_tensor(dst, dst, part, ALU.add).then_inc(out_ready, 1)


_INS = ['x', 'p', 'positions', 'g_ffn1', 'w1_gate', 'w1_up', 'w1_down', 'g_mix', 'w_in', 'g_cq', 'w_uq',
        'g_ckv', 'w_ukv', 'g_q_mla', 'g_k_mla', 'g_q_dil', 'g_k_dil', 'w_br_mla', 'w_br_dil', 'w_o', 'g_ffn2',
        'w2_gate', 'w2_up', 'w2_down', 'g_ple', 'w_ple_gate', 'w_ple_proj']


def constants(np, bf16):
    P, NEG, THETA = 128, -1e30, 500000.0
    q, k = np.arange(P)[:, None], np.arange(P)[None, :]
    causal = k <= q
    mla = np.concatenate([np.ones((P, P), bool), causal], axis=1)
    groups = ((128, 1), (512, 4), (2048, 16))

    def seen(qi, ki, win, dil):
        gap = qi - ki
        return (gap >= 0) & (gap % dil == 0) & (gap <= win)

    dil = np.concatenate([seen(q + P, np.arange(2 * P)[None, :], w, d) for w, d in groups], axis=1)
    freq = [THETA ** (-np.arange(rd // 2, dtype=np.float64) * 2.0 / rd) for rd in (64, 32)]
    return {
        "identity": np.eye(P, dtype=np.float32),
        "mla_masks": np.where(mla, 0.0, NEG).astype(bf16),
        "dil_masks": np.where(dil, 0.0, NEG).astype(bf16),
        "inverse_frequencies": np.concatenate(freq).astype(np.float32)[None, :],
    }


def kernel(**inputs):
    import ml_dtypes
    import numpy as np
    import concourse.bacc as bacc
    from concourse.bass_utils import run_bass_kernel_spmd

    nc = bacc.Bacc("TRN2", target_bir_lowering=False, num_devices=1)
    arrays = {name: np.ascontiguousarray(inputs[name]) for name in _INS}
    arrays.update(constants(np, ml_dtypes.bfloat16))
    aps = {name: nc.dram_tensor(f"in_{name}", a.shape, mybir.dt.from_np(a.dtype), kind="ExternalInput").ap()
           for name, a in arrays.items()}
    out = nc.dram_tensor("out_x", arrays["x"].shape, F32, kind="ExternalOutput").ap()
    hybrid_layer(nc, out, **aps)
    r = run_bass_kernel_spmd(nc, [{f"in_{name}": a for name, a in arrays.items()}], core_ids=[0])
    return r.results[0]["out_x"]
```
